# Optimizing a Trainium2 kernel written in Bass

```python
import jax, jax.numpy as jnp
from jax import lax
import numpy as np
import math

D_MODEL = 1024
BATCH = 1
SEQ = 1024
DEPTH = 1

GRID_W = 64
HEAD_DIM = 64
D_MIX = D_MODEL
A_HEADS = 8
A_KV_HEADS = 2
B_HEADS = 8
A_WIDTH = A_HEADS * HEAD_DIM
A_KV_WIDTH = A_KV_HEADS * HEAD_DIM
B_WIDTH = B_HEADS * HEAD_DIM
SPLITS = (A_WIDTH, A_KV_WIDTH, A_KV_WIDTH, A_WIDTH, B_WIDTH, B_WIDTH, B_WIDTH, B_WIDTH)
D_IN = sum(SPLITS)
Q_BLOCK = 128
AXIS_DIM = HEAD_DIM // 2
ROPE_PAIRS = AXIS_DIM // 2
ROPE_THETA = 10000.0
NA_KH = 8
NA_KW = 16
NA_COL_BLOCK = 16
NA_BAND = NA_COL_BLOCK + NA_KW
EPS = 1e-6


def _rmsnorm(x, gain):
    x32 = x.astype(jnp.float32)
    y = x32 * lax.rsqrt(jnp.mean(x32 * x32, axis=-1, keepdims=True) + EPS)
    return (y * gain.astype(jnp.float32)).astype(x.dtype)

def _axial_rope_tables(seq, dtype):
    t = jnp.arange(seq, dtype=jnp.int32)
    row = (t // GRID_W).astype(jnp.float32)
    col = (t % GRID_W).astype(jnp.float32)
    inv = ROPE_THETA ** (-jnp.arange(ROPE_PAIRS, dtype=jnp.float32) * (2.0 / AXIS_DIM))
    ang_r = row[:, None] * inv[None, :]
    ang_c = col[:, None] * inv[None, :]
    ang = jnp.concatenate([ang_r, ang_r, ang_c, ang_c], axis=-1)
    return jnp.cos(ang)[:, None, :].astype(dtype), jnp.sin(ang)[:, None, :].astype(dtype)

def _rotate_half_axial(x):
    shp = x.shape
    xr = x.reshape(shp[:-1] + (2, 2, ROPE_PAIRS))
    x1 = xr[..., 0, :]
    x2 = xr[..., 1, :]
    return jnp.stack([-x2, x1], axis=-2).reshape(shp)

def _gqa_blocked(q, k, v):
    b, s, h, d = q.shape
    hk = k.shape[2]
    g = h // hk
    nb = s // Q_BLOCK
    qb = q.reshape(b, nb, Q_BLOCK, hk, g, d).transpose(1, 0, 2, 3, 4, 5)
    scale = d ** -0.5

    def block(qi):
        sc = jnp.einsum('bqkgd,bskd->bkgqs', qi, k).astype(jnp.float32) * scale
        p = jax.nn.softmax(sc, axis=-1).astype(v.dtype)
        return jnp.einsum('bkgqs,bskd->bqkgd', p, v)

    o = lax.map(block, qb)
    return o.transpose(1, 0, 2, 3, 4, 5).reshape(b, s, h * d)

def _neighbourhood_attn(q, k, v, rpb):
    b, s, h, d = q.shape
    rows = s // GRID_W
    kh = min(NA_KH, rows)
    n_cb = GRID_W // NA_COL_BLOCK
    qg = q.reshape(b, rows, GRID_W, h, d)
    kg = k.reshape(b, rows, GRID_W, h, d)
    vg = v.reshape(b, rows, GRID_W, h, d)
    c = np.arange(GRID_W)
    col_start = np.clip(c - NA_KW // 2, 0, GRID_W - NA_KW)
    band_start = np.clip(np.arange(n_cb) * NA_COL_BLOCK - NA_KW // 2, 0, GRID_W - NA_BAND)
    band_cols = band_start[:, None] + np.arange(NA_BAND)[None, :]
    qc = c.reshape(n_cb, NA_COL_BLOCK)
    qcs = col_start.reshape(n_cb, NA_COL_BLOCK)
    kc = band_cols[:, None, :]
    col_valid = (kc >= qcs[..., None]) & (kc < qcs[..., None] + NA_KW)
    col_idx = np.clip(kc - qc[..., None] + (NA_KW - 1), 0, 2 * NA_KW - 2)
    rpb_col = rpb[:, :, col_idx]
    mask = jnp.asarray(col_valid[:, :, None, :])
    scale = d ** -0.5

    def row_block(args):
        r, q_row = args
        r0 = jnp.clip(r - kh // 2, 0, rows - kh)
        k_rows = lax.dynamic_slice_in_dim(kg, r0, kh, axis=1)
        v_rows = lax.dynamic_slice_in_dim(vg, r0, kh, axis=1)
        k_band = jnp.take(k_rows, band_cols, axis=2)
        v_band = jnp.take(v_rows, band_cols, axis=2)
        qb = q_row.reshape(b, n_cb, NA_COL_BLOCK, h, d)
        sc = jnp.einsum('bjqhd,bkjchd->bhjqkc', qb, k_band).astype(jnp.float32) * scale
        row_idx = r0 + jnp.arange(kh) - r + (NA_KH - 1)
        bias = rpb_col[:, row_idx].transpose(0, 2, 3, 1, 4)
        sc = jnp.where(mask, sc + bias.astype(jnp.float32), -jnp.inf)
        p = jax.nn.softmax(sc, axis=(-2, -1)).astype(v.dtype)
        o = jnp.einsum('bhjqkc,bkjchd->bjqhd', p, v_band)
        return o.reshape(b, GRID_W, h * d)

    o = lax.map(row_block, (jnp.arange(rows), qg.transpose(1, 0, 2, 3, 4)))
    return o.transpose(1, 0, 2, 3).reshape(b, s, h * d)

def first_inputs(seed: int = 0) -> dict:
    key = jax.random.key(seed)
    ks = jax.random.split(key, 9)
    x = jax.random.normal(ks[0], (BATCH, SEQ, D_MODEL), jnp.float32)
    norm_gain = 1.0 + 0.02 * jax.random.normal(ks[1], (DEPTH, D_MODEL), jnp.float32)
    w_in = jax.random.normal(ks[2], (DEPTH, D_MODEL, D_IN), jnp.float32) * D_MODEL ** -0.5
    q_norm_a = 1.0 + 0.02 * jax.random.normal(ks[3], (DEPTH, HEAD_DIM), jnp.float32)
    k_norm_a = 1.0 + 0.02 * jax.random.normal(ks[4], (DEPTH, HEAD_DIM), jnp.float32)
    na_rpb = 0.02 * jax.random.normal(ks[5], (DEPTH, B_HEADS, 2 * NA_KH - 1, 2 * NA_KW - 1), jnp.float32)
    w_out = jax.random.normal(ks[6], (DEPTH, D_MIX, D_MODEL), jnp.float32) * D_MIX ** -0.5
    final_norm_gain = 1.0 + 0.02 * jax.random.normal(ks[7], (D_MODEL,), jnp.float32)
    return {"x": x, "norm_gain": norm_gain, "w_in": w_in, "q_norm_a": q_norm_a,
            "k_norm_a": k_norm_a, "na_rpb": na_rpb, "w_out": w_out,
            "final_norm_gain": final_norm_gain}

def first_block(x, norm_gain, w_in, q_norm_a, k_norm_a, na_rpb, w_out, final_norm_gain):
    b, s, _ = x.shape
    cos, sin = _axial_rope_tables(s, x.dtype)
    split_at = [int(v) for v in np.cumsum(SPLITS)[:-1]]
    for l in range(DEPTH):
        h = _rmsnorm(x, norm_gain[l])
        proj = h @ w_in[l]
        q_a, k_a, v_a, g_a, q_b, k_b, v_b, g_b = jnp.split(proj, split_at, axis=-1)
        q_a = _rmsnorm(q_a.reshape(b, s, A_HEADS, HEAD_DIM), q_norm_a[l])
        k_a = _rmsnorm(k_a.reshape(b, s, A_KV_HEADS, HEAD_DIM), k_norm_a[l])
        q_a = q_a * cos + _rotate_half_axial(q_a) * sin
        k_a = k_a * cos + _rotate_half_axial(k_a) * sin
        v_a = v_a.reshape(b, s, A_KV_HEADS, HEAD_DIM)
        o_a = _gqa_blocked(q_a, k_a, v_a) * jax.nn.silu(g_a)
        o_b = _neighbourhood_attn(q_b.reshape(b, s, B_HEADS, HEAD_DIM),
                                  k_b.reshape(b, s, B_HEADS, HEAD_DIM),
                                  v_b.reshape(b, s, B_HEADS, HEAD_DIM), na_rpb[l])
        o_b = o_b * jax.nn.silu(g_b)
        mixed = jnp.concatenate([o_a, o_b], axis=-1)
        x = x + mixed @ w_out[l]
    return _rmsnorm(x, final_norm_gain)


A_HEAD_DIM = 64
A_WIDTH_2 = A_HEADS * A_HEAD_DIM
DECAY_LORA = 64
ICLR_LORA = 64
DECAY_SCALE = 0.6065306597
GN_EPS = 64e-5
QK_NOPE_DIM = 64
QK_ROPE_DIM = 32
V_HEAD_DIM = 64
Q_LORA_RANK = 256
KV_LORA_RANK = 128
B_WIDTH_2 = B_HEADS * V_HEAD_DIM
NORM_EPS = 1e-6
N_BRANCHES = 2
SHIFT_COLS = 3 * A_WIDTH_2 + DECAY_LORA + ICLR_LORA
IN_COLS = SHIFT_COLS + A_WIDTH_2 + Q_LORA_RANK + KV_LORA_RANK + QK_ROPE_DIM + B_WIDTH_2 + N_BRANCHES * D_MODEL


def rmsnorm(x, g, eps=NORM_EPS):
    xf = x.astype(jnp.float32)
    y = xf * lax.rsqrt(jnp.mean(xf * xf, axis=-1, keepdims=True) + eps)
    return (y * g.astype(jnp.float32)).astype(x.dtype)

def split_cols(t, sizes):
    idx = np.cumsum(sizes)[:-1].tolist()
    return jnp.split(t, idx, axis=-1)

def token_shift(feat, mu):
    prev = jnp.pad(feat, ((0, 0), (1, 0), (0, 0)))[:, :-1, :]
    return feat + mu * (prev - feat)

def rwkv7_branch(feat, z, mu_shift, w0, w_decay_up, a0, w_iclr_up, k_k, k_a, r_k, gn_gain, gn_bias, w_out_a):
    bsz, seq, _ = feat.shape
    dt = feat.dtype
    f = token_shift(feat, mu_shift)
    r, k, v, wd, ad = split_cols(f, [A_WIDTH_2, A_WIDTH_2, A_WIDTH_2, DECAY_LORA, ICLR_LORA])
    w_logit = (w0 + jnp.tanh(wd) @ w_decay_up).astype(jnp.float32)
    w = jnp.exp(-DECAY_SCALE * jax.nn.sigmoid(w_logit))
    a = jax.nn.sigmoid((a0 + ad @ w_iclr_up).astype(jnp.float32))
    hs = lambda t: t.reshape(bsz, seq, A_HEADS, A_HEAD_DIM).astype(jnp.float32)
    r, k, v, w, a = hs(r), hs(k), hs(v), hs(w), hs(a)
    kk = k * k_k.reshape(A_HEADS, A_HEAD_DIM)
    kk = kk / jnp.maximum(jnp.linalg.norm(kk, axis=-1, keepdims=True), 1e-12)
    k = k * (1.0 + (a - 1.0) * k_a.reshape(A_HEADS, A_HEAD_DIM))

    def step(S, inp):
        r_t, w_t, k_t, v_t, kk_t, a_t = inp
        sa = jnp.einsum('bhvk,bhk->bhv', S, -kk_t)
        S = S * w_t[:, :, None, :] + sa[..., None] * (kk_t * a_t)[:, :, None, :] + v_t[..., None] * k_t[:, :, None, :]
        return S, jnp.einsum('bhvk,bhk->bhv', S, r_t)

    tm = lambda t: jnp.moveaxis(t, 1, 0)
    S0 = jnp.zeros((bsz, A_HEADS, A_HEAD_DIM, A_HEAD_DIM), jnp.float32)
    _, y = lax.scan(step, S0, (tm(r), tm(w), tm(k), tm(v), tm(kk), tm(a)))
    y = jnp.moveaxis(y, 0, 1)
    mean = jnp.mean(y, axis=-1, keepdims=True)
    var = jnp.mean(jnp.square(y - mean), axis=-1, keepdims=True)
    y = (y - mean) * lax.rsqrt(var + GN_EPS)
    y = y * gn_gain.reshape(A_HEADS, A_HEAD_DIM) + gn_bias.reshape(A_HEADS, A_HEAD_DIM)
    y = y + jnp.sum(r * k * r_k, axis=-1, keepdims=True) * v
    y = y.reshape(bsz, seq, A_WIDTH_2).astype(dt) * jax.nn.silu(z)
    return y @ w_out_a

def rope(t, cos, sin):
    t1, t2 = jnp.split(t, 2, axis=-1)
    return jnp.concatenate([t1 * cos - t2 * sin, t2 * cos + t1 * sin], axis=-1)

def mla_branch(c_q, c_kv, k_pe, z, positions, g_q, w_uq, g_kv, w_ukv, w_out_b):
    bsz, seq, _ = c_q.shape
    dt = c_q.dtype
    q = (rmsnorm(c_q, g_q) @ w_uq).reshape(bsz, seq, B_HEADS, QK_NOPE_DIM + QK_ROPE_DIM)
    q_nope, q_pe = q[..., :QK_NOPE_DIM], q[..., QK_NOPE_DIM:]
    kv = (rmsnorm(c_kv, g_kv) @ w_ukv).reshape(bsz, seq, B_HEADS, QK_NOPE_DIM + V_HEAD_DIM)
    k_nope, v = kv[..., :QK_NOPE_DIM], kv[..., QK_NOPE_DIM:]
    inv_freq = ROPE_THETA ** (-jnp.arange(0, QK_ROPE_DIM, 2, dtype=jnp.float32) / QK_ROPE_DIM)
    ang = positions.astype(jnp.float32)[..., None] * inv_freq
    cos, sin = jnp.cos(ang).astype(dt), jnp.sin(ang).astype(dt)
    q_pe = rope(q_pe, cos[:, :, None, :], sin[:, :, None, :])
    k_pe = rope(k_pe, cos, sin)
    scale = 1.0 / math.sqrt(QK_NOPE_DIM + QK_ROPE_DIM)
    nb = seq // Q_BLOCK
    blk = lambda t: jnp.moveaxis(t.reshape(bsz, nb, Q_BLOCK, *t.shape[2:]), 1, 0)
    key_idx = jnp.arange(seq)

    def attend(args):
        qn, qp, b = args
        s = jnp.einsum('bqhd,bkhd->bhqk', qn, k_nope) + jnp.einsum('bqhr,bkr->bhqk', qp, k_pe)
        s = s.astype(jnp.float32) * scale
        q_idx = b * Q_BLOCK + jnp.arange(Q_BLOCK)
        s = jnp.where(key_idx[None, :] <= q_idx[:, None], s, jnp.finfo(jnp.float32).min)
        p = jax.nn.softmax(s, axis=-1).astype(dt)
        return jnp.einsum('bhqk,bkhd->bqhd', p, v)

    o = lax.map(attend, (blk(q_nope), blk(q_pe), jnp.arange(nb)))
    o = jnp.moveaxis(o, 0, 1).reshape(bsz, seq, B_WIDTH_2)
    return (o * jax.nn.silu(z)) @ w_out_b

def second_inputs(seed: int = 0) -> dict:
    key = jax.random.key(seed)
    ks = jax.random.split(key, 24)
    n = lambda i, shape, s=1.0: s * jax.random.normal(ks[i], shape, jnp.float32)
    x = n(0, (BATCH, SEQ, D_MODEL))
    positions = (jnp.arange(SEQ, dtype=jnp.int32)[None, :]
                 + jax.random.randint(ks[1], (BATCH, 1), 0, 1024, dtype=jnp.int32))
    return {
        'x': x,
        'positions': positions,
        'g_pre': 1.0 + n(2, (D_MODEL,), 0.05),
        'w_in': n(3, (D_MODEL, IN_COLS), D_MODEL ** -0.5),
        'b_gate': n(4, (N_BRANCHES * D_MODEL,), 0.01),
        'mu_shift': jax.random.uniform(ks[5], (SHIFT_COLS,), jnp.float32),
        'w0': n(6, (A_WIDTH_2,), 0.5),
        'w_decay_up': n(7, (DECAY_LORA, A_WIDTH_2), 0.1),
        'a0': n(8, (A_WIDTH_2,), 0.5),
        'w_iclr_up': n(9, (ICLR_LORA, A_WIDTH_2), 0.5 * ICLR_LORA ** -0.5),
        'k_k': 0.85 + n(10, (A_WIDTH_2,), 0.05),
        'k_a': 1.0 + n(11, (A_WIDTH_2,), 0.05),
        'r_k': n(12, (A_HEADS, A_HEAD_DIM), 0.1),
        'gn_gain': 1.0 + n(13, (A_WIDTH_2,), 0.05),
        'gn_bias': n(14, (A_WIDTH_2,), 0.01),
        'w_out_a': n(15, (A_WIDTH_2, D_MODEL), A_WIDTH_2 ** -0.5),
        'g_q': 1.0 + n(16, (Q_LORA_RANK,), 0.05),
        'w_uq': n(17, (Q_LORA_RANK, B_HEADS * (QK_NOPE_DIM + QK_ROPE_DIM)), Q_LORA_RANK ** -0.5),
        'g_kv': 1.0 + n(18, (KV_LORA_RANK,), 0.05),
        'w_ukv': n(19, (KV_LORA_RANK, B_HEADS * (QK_NOPE_DIM + V_HEAD_DIM)), KV_LORA_RANK ** -0.5),
        'w_out_b': n(20, (B_WIDTH_2, D_MODEL), B_WIDTH_2 ** -0.5),
        'w_o': n(21, (D_MODEL, D_MODEL), D_MODEL ** -0.5),
        'g_post': 1.0 + n(22, (D_MODEL,), 0.05),
    }

def second_block(x, positions, g_pre, w_in, b_gate, mu_shift, w0, w_decay_up, a0, w_iclr_up, k_k, k_a, r_k,
              gn_gain, gn_bias, w_out_a, g_q, w_uq, g_kv, w_ukv, w_out_b, w_o, g_post):
    h = x
    for _ in range(DEPTH):
        u = rmsnorm(h, g_pre)
        proj = u @ w_in
        feat_a, z_a, c_q, c_kv, k_pe, z_b, gate_logits = split_cols(
            proj, [SHIFT_COLS, A_WIDTH_2, Q_LORA_RANK, KV_LORA_RANK, QK_ROPE_DIM, B_WIDTH_2, N_BRANCHES * D_MODEL])
        y_a = rwkv7_branch(feat_a, z_a, mu_shift, w0, w_decay_up, a0, w_iclr_up, k_k, k_a, r_k,
                           gn_gain, gn_bias, w_out_a)
        y_b = mla_branch(c_q, c_kv, k_pe, z_b, positions, g_q, w_uq, g_kv, w_ukv, w_out_b)
        gates = jax.nn.sigmoid(gate_logits + b_gate)
        g_a, g_b = gates[..., :D_MODEL], gates[..., D_MODEL:]
        merged = g_a * y_a + g_b * y_b
        h = h + rmsnorm(merged @ w_o, g_post)
    return h


def setup_inputs(seed=0):
    out = dict(first_inputs(seed))
    for name, value in second_inputs(seed + 1).items():
        if name != "x":
            out[name + "_2"] = value
    return out


def reference(
    x, norm_gain, w_in, q_norm_a, k_norm_a, na_rpb, w_out, final_norm_gain, positions_2,
    g_pre_2, w_in_2, b_gate_2, mu_shift_2, w0_2, w_decay_up_2, a0_2, w_iclr_up_2, k_k_2, k_a_2,
    r_k_2, gn_gain_2, gn_bias_2, w_out_a_2, g_q_2, w_uq_2, g_kv_2, w_ukv_2, w_out_b_2, w_o_2,
    g_post_2,
):
    x = first_block(
        x, norm_gain, w_in, q_norm_a, k_norm_a, na_rpb, w_out, final_norm_gain,
    )
    return second_block(
        x, positions_2, g_pre_2, w_in_2, b_gate_2, mu_shift_2, w0_2, w_decay_up_2, a0_2,
        w_iclr_up_2, k_k_2, k_a_2, r_k_2, gn_gain_2, gn_bias_2, w_out_a_2, g_q_2, w_uq_2,
        g_kv_2, w_ukv_2, w_out_b_2, w_o_2, g_post_2,
    )


_drawn_inputs = setup_inputs


def setup_inputs(seed=0):
    import zlib

    import numpy as np

    out = dict(_drawn_inputs(seed))
    spreads = {}
    factors = {'norm_gain': 8.0,
     'q_norm_a': 8.0,
     'k_norm_a': 8.0,
     'na_rpb': 8.0,
     'b_gate_2': 8.0,
     'k_k_2': 49.144,
     'gn_bias_2': 58.593,
     'g_q_2': 8.0,
     'g_kv_2': 7.947,
     'w0_2': 3.376,
     'w_decay_up_2': 6.012,
     'w_iclr_up_2': 2.888,
     'k_a_2': 8.0,
     'gn_gain_2': 8.0}
    for name, (base, spread) in spreads.items():
        noise = np.random.default_rng([zlib.crc32(name.encode()), seed]).standard_normal(out[name].shape)
        drawn = base * np.exp(spread * noise) if base else spread * noise
        out[name] = __import__('jax').numpy.asarray(drawn.astype(out[name].dtype))
    for name, factor in factors.items():
        out[name] = (out[name] * factor).astype(out[name].dtype)
    return out
```

```python
from contextlib import ExitStack

import numpy as np

import concourse.bass as bass
from concourse import mybir

F = mybir.dt.float32
R = mybir.dt.float32r
I32 = mybir.dt.int32
ALU = mybir.AluOpType
ACT = mybir.ActivationFunctionType
X = mybir.AxisListType.X

KB = 1024
T = 1024
D = 1024
NT = 8
NEG = -1.0e30
DECAY = 0.6065306597

C_ID, C_CAUS, C_BLK, C_BLKM, C_COL = 0, 128, 256, 384, 512
C_MD, C_MS, C_MI, C_MDT, C_MOT, C_I64, C_INV, C_ONE2 = 576, 640, 704, 768, 832, 896, 960, 976
C_END = 978
C_COS, C_SIN, C_RST = 978, 978 + 512, 978 + 1024
C_ALL = 978 + 2048

VROWS = [("pos", 8), ("norm_gain", 8), ("g_pre", 8), ("mu", 13), ("w0", 4), ("a0", 4), ("k_k", 4), ("k_a", 4),
         ("r_k", 4), ("gn_gain", 4), ("gn_bias", 4), ("g_q", 2), ("g_kv", 1), ("b_gate", 16)]
VOFF = {}
_o = 0
for _n, _c in VROWS:
    VOFF[_n] = _o
    _o += _c
VTOT = _o


def constants():
    c = np.zeros((128, C_ALL), np.float64)
    p = np.arange(128)
    c[:, C_ID:C_ID + 128] = np.eye(128)
    c[:, C_CAUS:C_CAUS + 128] = np.where(p[None, :] <= p[:, None], 0.0, NEG)
    same = (p[:, None] // 64) == (p[None, :] // 64)
    c[:, C_BLK:C_BLK + 128] = same
    c[:, C_BLKM:C_BLKM + 128] = same / 64.0
    j = np.arange(64)
    col = p % 64
    start = np.clip(col - 8, 0, 48)
    c[:, C_COL:C_COL + 64] = np.where((j[None] >= start[:, None]) & (j[None] < start[:, None] + 16), 0.0, NEG)
    s = (p % 64)[:, None]
    t = j[None]
    blk = (s // 16) == (t // 16)
    c[:, C_MD:C_MD + 64] = (s < t) & blk
    c[:, C_MS:C_MS + 64] = s < t
    c[:, C_MI:C_MI + 64] = s <= t
    c[:, C_MDT:C_MDT + 64] = (t < s) & blk
    c[:, C_MOT:C_MOT + 64] = (t < s) & ~blk
    c[:, C_I64:C_I64 + 64] = s == t
    c[:, C_INV:C_INV + 16] = (np.float32(10000.0) ** (-np.arange(0, 32, 2, dtype=np.float32) / np.float32(32)))[None]
    c[:64, C_ONE2] = 1.0
    c[64:, C_ONE2 + 1] = 1.0
    inv = np.float32(10000.0) ** (-np.arange(16, dtype=np.float32) * np.float32(2.0 / 32))
    tok = np.arange(T)
    ar = (tok // 64).astype(np.float32)[:, None] * inv[None]
    ac = (tok % 64).astype(np.float32)[:, None] * inv[None]
    ang = np.concatenate([ar, ar, ac, ac], 1).astype(np.float64)
    sign = np.where((np.arange(64) // 16) % 2 == 0, -1.0, 1.0)
    c[:, C_COS:C_COS + 512] = np.cos(ang).reshape(8, 128, 64).transpose(1, 0, 2).reshape(128, 512)
    c[:, C_SIN:C_SIN + 512] = (np.sin(ang) * sign).reshape(8, 128, 64).transpose(1, 0, 2).reshape(128, 512)
    c[:, C_RST:C_RST + 1024] = (np.arange(T) % 64 != 0)[None]
    return c.astype(np.float32)


class Queue:

    def __init__(self, sem, serial=False):
        self.sem, self.n, self.seen, self.items = sem, 0, {}, []
        self.serial = serial

    def wait(self, *tokens):
        for tok in tokens:
            if tok is None:
                continue
            if isinstance(tok, list):
                self.wait(*tok)
                continue
            sem, value = tok
            if value and self.seen.get(id(sem), 0) < value:
                self.seen[id(sem)] = value
                self.items.append(lambda e, s=sem, v=value: e.wait_ge(s, v))

    def do(self, make, *tokens):
        self.wait(*tokens)
        if self.serial:
            self.wait((self.sem, self.n))
        self.n += 1
        self.items.append(lambda e: make(e).then_inc(self.sem, 1))
        return (self.sem, self.n)

    def quiet(self, make, *tokens):
        self.wait(*tokens)
        self.items.append(make)

    def dma(self, out, in_, land, *tokens):
        self.wait(*tokens)
        land.n += 16
        self.items.append(lambda e: e.dma_start(out, in_).then_inc(land.sem, 16))
        return (land.sem, land.n)

    def last(self):
        return (self.sem, self.n)

    def emit(self, engine):
        for item in self.items:
            item(engine)


class Land:

    def __init__(self, sem):
        self.sem, self.n = sem, 0


class Place:

    def __init__(self, ap):
        self.ap, self.free = ap, []


def bc(ap, dim, n):
    shape = list(ap.shape)
    shape.insert(dim, n)
    return ap.unsqueeze(dim).to_broadcast(shape)


def build(nc, a, out):
    ctx = ExitStack()
    with ctx:
        def sem(name):
            return ctx.enter_context(nc.semaphore(name))

        BASE = nc.sbuf_base + (-nc.sbuf_base) % 32
        count = [0]

        def sb(shape, dt, offset):
            count[0] += 1
            return nc.alloc_sbuf_tensor_at(f"t{count[0]}", shape, dt, offset=BASE + offset)

        PE, ACTQ, DVE, SP = (Queue(sem(n)) for n in ("s_pe", "s_act", "s_dve", "s_sp"))
        POOL = Queue(sem("s_pool"), serial=True)
        lands = {}

        def land(name):
            if name not in lands:
                lands[name] = Land(sem("d_" + name))
            return lands[name]

        ps_all = ctx.enter_context(nc.psum_tensor("ps", [128, 4096], F))
        banks = [Place(ps_all[:, 512 * i:512 * (i + 1)]) for i in range(8)]

        RA = 0
        RW = 64 * KB
        RC = 104 * KB
        RS = 108 * KB
        W0 = 114 * KB
        AH = sb([128, 8, T], R, RA)
        AL = sb([128, 8, T], R, RA + 32 * KB)
        WST = sb([128, 2048], F, RW)
        WHI = [sb([128, 2048], R, RW + (8 + 8 * i) * KB) for i in range(2)]
        WLO = [sb([128, 2048], R, RW + (24 + 8 * i) * KB) for i in range(2)]
        CST = sb([128, C_END], F, RC)
        VT = sb([128, 128], F, RS)
        VTR = sb([128, 128], F, RS + 512)
        STAT = sb([128, 512], F, RS + 1024)
        POSI = sb([8, 128], I32, RS + 3072)
        HALF = sb([128, 128], F, RS + 3584)
        NMX = sb([128, 16], F, RS + 4096)
        RSM = sb([128, 16], F, RS + 4160)
        RIN = sb([128, 16], F, RS + 4224)
        S2 = sb([128, 2, 64], F, RS + 4288)
        PCT = sb([128, 16], F, RS + 4800)

        def cst(col, n):
            return CST[:, col:col + n]

        ident = cst(C_ID, 128)

        def vec(name, k=0, p0=0, p1=128):
            return VT[p0:p1, VOFF[name] + k:VOFF[name] + k + 1]

        def dram(name, shape):
            return nc.dram_tensor(name, shape, F, kind="Internal").ap()

        rpb_d = dram("rpb_pad", [120, 128])
        bias_d = dram("rpb_rows", [120, 64, 64])
        x2_d = dram("x2_spill", [T, D])
        feat_d = dram("feat_spill", [13, 128, T])
        zg_d = dram("zgate_spill", [20, 128, T])

        t_cst = POOL.dma(CST[:, :], a["consts"][:, 0:C_END], land("cst"))
        t_vrow = []
        srcs = {"norm_gain": a["norm_gain"].rearrange("a (r c) -> (a r) c", c=128)}
        for name, key in [("g_pre", "g_pre_2"), ("mu", "mu_shift_2"), ("w0", "w0_2"), ("a0", "a0_2"), ("k_k", "k_k_2"),
                          ("k_a", "k_a_2"), ("gn_gain", "gn_gain_2"), ("gn_bias", "gn_bias_2"), ("g_q", "g_q_2"),
                          ("g_kv", "g_kv_2"), ("b_gate", "b_gate_2")]:
            srcs[name] = a[key].rearrange("(r c) -> r c", c=128)
        srcs["r_k"] = a["r_k_2"].rearrange("(r h) d -> r (h d)", h=2)
        t_zero = POOL.do(lambda e: e.memset(VTR[:, :], 0.0))
        for n, (name, rows) in enumerate(VROWS[1:]):
            o = VOFF[name]
            t_vrow.append(POOL.dma(VTR[o:o + rows, :], srcs[name], land(f"v{n}"), t_zero))
        t_posi = POOL.dma(POSI[:, :], a["positions_2"].rearrange("a (r c) -> (a r) c", c=128), land("posi"))
        t_half = POOL.do(lambda e: e.memset(HALF[:, :], -0.5))
        t_pos = DVE.do(lambda e: e.tensor_copy(VTR[0:8, :], POSI[:, :]), t_posi, t_zero)
        t_vt = PE.do(lambda e: e.transpose(banks[7].ap[:, 0:128], VTR[:, :], ident), t_cst, t_vrow, t_pos)
        t_vec = DVE.do(lambda e: e.tensor_copy(VT[:, :], banks[7].ap[:, 0:128]), t_vt)
        banks[7].free = [t_vec]

        wplan = []

        def want(src, kt, cols):
            wplan.append((src, kt, cols))

        w1 = a["w_in"].rearrange("a k n -> (a k) n")
        w2 = a["w_in_2"]
        wo1 = a["w_out"].rearrange("a k n -> (a k) n")
        O1 = dict(qkv=0, ga=768, qb=1280, kb=1792, vb=2304, gb=2816)
        for c in range(0, 768, 256):
            want(w1[:, c:c + 256], 8, 256)
        for c in range(768, 1280, 256):
            want(w1[:, c:c + 256], 8, 256)
        for h in range(2):
            for s in ("qb", "kb", "vb", "gb"):
                c = O1[s] + 256 * h
                want(w1[:, c:c + 256], 8, 256)
        for c in range(0, 1024, 256):
            want(wo1[:, c:c + 256], 8, 256)
        want(w2[:, 2176:2432], 8, 256)
        want(w2[:, 2432:2592], 8, 160)
        for c in (2592, 2848):
            want(w2[:, c:c + 256], 8, 256)
        for c in range(0, 1664, 256):
            want(w2[:, c:min(c + 256, 1664)], 8, min(256, 1664 - c))
        for c in (1664, 1920):
            want(w2[:, c:c + 256], 8, 256)
        for c in range(3104, 5152, 256):
            want(w2[:, c:c + 256], 8, 256)
        want(a["w_uq_2"], 2, 768)
        want(a["w_ukv_2"], 1, 1024)
        for c in range(0, 1024, 256):
            want(a["w_out_a_2"][:, c:c + 256], 4, 256)
            want(a["w_out_b_2"][:, c:c + 256], 4, 256)
        for c in range(0, 1024, 256):
            want(a["w_o_2"][:, c:c + 256], 8, 256)

        wst = Place(WST)
        wsl = [Place(None), Place(None)]
        wready = []
        wnext = [0]
        hold = [False]

        def wload():
            n = len(wready)
            if n >= len(wplan):
                return
            src, kt, cols = wplan[n]
            sl = wsl[n % 2]
            size = kt * cols
            st = WST[:, 0:size].rearrange("p (k c) -> p k c", k=kt)
            if src is a["w_ukv_2"]:
                by_head = src.rearrange("p (h s c) -> p s h c", s=2, c=64)
                for s in range(2):
                    t_d = SP.dma(WST[:, 512 * s:512 * s + 512].rearrange("p (h c) -> p h c", c=64), by_head[:, s], land("w"), wst.free)
            else:
                t_d = SP.dma(st, src.rearrange("(k p) c -> p k c", p=128), land("w"), wst.free)
            hi, lo = WHI[n % 2][:, 0:size], WLO[n % 2][:, 0:size]
            t_h = ACTQ.do(lambda e: e.activation(hi, WST[:, 0:size], ACT.Copy), t_d, sl.free)
            t_l = POOL.do(lambda e: e.tensor_tensor(lo, WST[:, 0:size], hi.bitcast(F), ALU.subtract), t_h, sl.free)
            wst.free = [t_h, t_l]
            wready.append((hi.rearrange("p (k c) -> p k c", k=kt), lo.rearrange("p (k c) -> p k c", k=kt), [t_h, t_l], sl))

        class Block:

            def __enter__(self):
                n = wnext[0]
                wnext[0] += 1
                while len(wready) < n + (1 if hold[0] else 2) and len(wready) < len(wplan):
                    wload()
                self.hi, self.lo, self.tok, self.slot = wready[n]
                return self

            def __exit__(self, *exc):
                self.slot.free = [PE.last()]

        rot = [0]

        def bank(choice):
            rot[0] += 1
            return banks[choice[rot[0] % len(choice)]]

        def mm(out_ap, lhs, rhs, start, stop):
            return lambda e: e.matmul(out_ap, lhs, rhs, start=start, stop=stop)

        def product(dst, lefts, rights, *tokens):
            PE.wait(*tokens)
            n = len(lefts)
            for k in range(n):
                (lh, ll), (rh, rl) = lefts[k], rights[k]
                PE.quiet(mm(dst, lh, rh, k == 0, False))
                PE.quiet(mm(dst, lh, rl, False, False))
                last = mm(dst, ll, rh, False, k == n - 1)
                if k < n - 1:
                    PE.quiet(last)
            return PE.do(last)

        def gemm_nat(b, i, dst, act_h, act_l, kt, c0, c1, *tokens):
            sl = slice(128 * i, 128 * i + 128)
            return product(dst, [(act_h[:, k, sl], act_l[:, k, sl]) for k in range(kt)],
                           [(b.hi[:, k, c0:c1], b.lo[:, k, c0:c1]) for k in range(kt)], b.tok, *tokens)

        def gemm_tr(b, c0, c1, half, dst, act_h, act_l, kt, *tokens):
            sl = slice(512 * half, 512 * half + 512)
            return product(dst, [(b.hi[:, k, c0:c1], b.lo[:, k, c0:c1]) for k in range(kt)],
                           [(act_h[:, k, sl], act_l[:, k, sl]) for k in range(kt)], b.tok, *tokens)

        def everyone():
            return [PE.last(), ACTQ.last(), DVE.last(), POOL.last()]

        def enter_phase():
            toks = everyone()
            for q in (ACTQ, DVE, POOL, SP):
                q.wait(toks)

        def act(o, i, f, *tokens, **kw):
            return ACTQ.do(lambda e: e.activation(o, i, f, **kw), *tokens)

        def tt(q, o, x, y, op, *tokens):
            return q.do(lambda e: e.tensor_tensor(o, x, y, op), *tokens)

        def ts(q, o, x, s1, s2, op0, op1, *tokens):
            return q.do(lambda e: e.tensor_scalar(o, x, s1, s2, op0, op1) if s2 is not None
                        else e.tensor_scalar(o, x, s1, None, op0), *tokens)

        def stt(o, x, s, y, op0, op1, *tokens):
            return DVE.do(lambda e: e.scalar_tensor_tensor(out=o, in0=x, scalar=s, in1=y, op0=op0, op1=op1), *tokens)

        def cp(q, o, i, *tokens):
            return q.do(lambda e: e.tensor_copy(o, i), *tokens)

        def rpow(o, i, n, *tokens):
            return POOL.do(lambda e: e.tensor_tensor(o, i, HALF[:, 0:n], ALU.pow), t_half, *tokens)

        def split_group(ps, k, g, gain, t_ps):
            sl = slice(512 * g, 512 * g + 512)
            if gain is None:
                t_h = act(AH[:, k, sl], ps.ap, ACT.Copy, t_ps)
                t_l = tt(DVE, AL[:, k, sl], ps.ap, AH[:, k, sl].bitcast(F), ALU.subtract, t_h)
            else:
                t_h = act(AH[:, k, sl], ps.ap, ACT.Identity, t_ps, t_vec, scale=gain)
                t_l = stt(AL[:, k, sl], ps.ap, gain, AH[:, k, sl].bitcast(F), ALU.mult, ALU.subtract, t_h)
            ps.free = [t_h, t_l]
            return t_l

        def norm_transpose(src, t_src, dst, junk, gain_name):
            t_n = []
            for i in range(NT):
                t_s = act(junk, src(i), ACT.Square, t_src[i], ACTQ.last(), accum_out=STAT[:, i:i + 1])
                t_m = ts(DVE, STAT[:, 8 + i:9 + i], STAT[:, i:i + 1], 1.0 / D, 1e-6, ALU.mult, ALU.add, t_s)
                t_r = rpow(STAT[:, 16 + i:17 + i], STAT[:, 8 + i:9 + i], 1, t_m)
                t_n.append(ts(DVE, dst(i), src(i), STAT[:, 16 + i:17 + i], None, ALU.mult, None, t_r))
            t_l = None
            for g in range(2):
                for k in range(8):
                    ps = bank(range(8))
                    PE.wait(ps.free, t_n[4 * g:4 * g + 4], t_cst)
                    for i in range(4):
                        last = (lambda o, s: lambda e: e.transpose(o, s, ident))(
                            ps.ap[:, 128 * i:128 * i + 128], dst(4 * g + i)[:, 128 * k:128 * k + 128])
                        if i < 3:
                            PE.quiet(last)
                    t_ps = PE.do(last)
                    t_l = split_group(ps, k, g, vec(gain_name, k), t_ps)
            return t_l

        XS = sb([128, 8, D], F, W0)
        JUNK = sb([128, D], F, W0 + 32 * KB)
        xv = a["x"].rearrange("a (i p) c -> i p (a c)", p=128)
        t_x = [SP.dma(XS[:, i, :], xv[i], land(f"x{i}")) for i in range(NT)]
        wload()
        t_act = norm_transpose(lambda i: XS[:, i, :], t_x, lambda i: XS[:, i, :], JUNK[:, :], "norm_gain")

        MIXA = sb([128, 8, 512], F, W0)
        QKV = sb([128, 8, 768], F, W0 + 16 * KB)
        QT = sb([128, 4, T], R, W0 + 40 * KB)
        KT = sb([128, 2, T], R, W0 + 56 * KB)
        PB = [sb([128, T], F, W0 + (64 + 4 * i) * KB) for i in range(2)]
        PT = [sb([128, T], F, W0 + (72 + 4 * i) * KB) for i in range(2)]
        COS = sb([128, 8, 64], F, W0 + 64 * KB)
        SIN = sb([128, 8, 64], F, W0 + 66 * KB)
        GT = sb([128, 640], F, W0 + 68 * KB)
        TMP = sb([128, 640], F, W0 + 71 * KB)
        TMP2 = sb([128, 640], F, W0 + 74 * KB)
        QS = sb([128, 4, 2, 64], F, W0 + 80 * KB)
        KS = sb([128, 4, 64], F, W0 + 82 * KB)
        enter_phase()
        t_cos = SP.dma(COS[:, :, :], a["consts"][:, C_COS:C_COS + 512].rearrange("p (i c) -> p i c", c=64), land("cos"))
        t_sin = SP.dma(SIN[:, :, :], a["consts"][:, C_SIN:C_SIN + 512].rearrange("p (i c) -> p i c", c=64), land("sin"))
        t_g1 = SP.dma(GT[:, 0:64], a["q_norm_a"][0].partition_broadcast(128), land("gq"))
        t_g2 = SP.dma(GT[:, 512:576], a["k_norm_a"][0].partition_broadcast(128), land("gk"))
        t_g = ts(DVE, GT[:, 0:64], GT[:, 0:64], 0.125, None, ALU.mult, None, t_g1)
        t_ga = cp(DVE, GT[:, 64:512].rearrange("p (h c) -> p h c", c=64), bc(GT[:, 0:64], 1, 7), t_g)
        t_gb = cp(DVE, GT[:, 576:640], GT[:, 512:576], t_g2)

        t_qkv = [[] for _ in range(NT)]
        for n in range(3):
            with Block() as b:
                for i in range(NT):
                    ps = bank(range(8))
                    t = gemm_nat(b, i, ps.ap[:, 0:256], AH, AL, 8, 0, 256, ps.free, t_act)
                    t = act(QKV[:, i, 256 * n:256 * n + 256], ps.ap[:, 0:256], ACT.Copy, t)
                    ps.free = [t]
                    t_qkv[i].append(t)
        t_rope = []
        for i in range(NT):
            qk = QKV[:, i, 0:640]
            q3 = qk.rearrange("p (h c) -> p h c", c=64)
            tm = TMP[:, :]
            t = tt(DVE, tm, qk, qk, ALU.mult, t_qkv[i], t_rope[-1:])
            t = DVE.do(lambda e, i=i: e.tensor_reduce(STAT[:, 32 + 10 * i:42 + 10 * i],
                                                      TMP[:, :].rearrange("p (h c) -> p h c", c=64), X, ALU.add), t)
            t = ts(DVE, STAT[:, 112 + 10 * i:122 + 10 * i], STAT[:, 32 + 10 * i:42 + 10 * i], 1.0 / 64, 1e-6,
                   ALU.mult, ALU.add, t)
            t = rpow(STAT[:, 192 + 10 * i:202 + 10 * i], STAT[:, 112 + 10 * i:122 + 10 * i], 10, t)
            t = tt(DVE, q3, q3, bc(STAT[:, 192 + 10 * i:202 + 10 * i], 2, 64), ALU.mult, t)
            t = tt(DVE, qk, qk, GT[:, :], ALU.mult, t, t_ga, t_gb)
            t1 = tt(POOL, tm.rearrange("p (h c) -> p h c", c=64), q3, bc(COS[:, i, :], 1, 10), ALU.mult, t, t_cos)
            q5 = qk.rearrange("p (h x f c) -> p h x f c", x=2, f=2, c=16)
            s5 = bc(SIN[:, i, :], 1, 10).rearrange("p h (x f c) -> p h x f c", x=2, f=2)
            o5 = TMP2[:, :].rearrange("p (h x f c) -> p h x f c", x=2, f=2, c=16)
            ta = tt(DVE, o5[:, :, :, 0, :], q5[:, :, :, 1, :], s5[:, :, :, 0, :], ALU.mult, t, t_sin)
            tb = tt(DVE, o5[:, :, :, 1, :], q5[:, :, :, 0, :], s5[:, :, :, 1, :], ALU.mult, t, t_sin)
            t_rope.append(tt(DVE, qk, tm, TMP2[:, :], ALU.add, t1, ta, tb))

        t_gA = [[] for _ in range(NT)]
        for n in range(2):
            with Block() as b:
                for i in range(NT):
                    ps = bank(range(8))
                    t = gemm_nat(b, i, ps.ap[:, 0:256], AH, AL, 8, 0, 256, ps.free, t_act)
                    t = act(MIXA[:, i, 256 * n:256 * n + 256], ps.ap[:, 0:256], ACT.Silu, t)
                    ps.free = [t]
                    t_gA[i].append(t)

        pslot = [Place(None), Place(None)]
        seq = [0]

        def attention(items, pbuf, tbuf):
            spair = [(banks[0], banks[1]), (banks[2], banks[3])]
            tpair = (banks[4], banks[5])
            opair = [banks[6], banks[7]]
            st = []
            single = tbuf[0] is tbuf[1]
            tslot = [Place(None)] * 2 if single else [Place(None), Place(None)]

            def scores(n):
                it = items[n]
                z = seq[0] + n
                s0, s1 = spair[z % 2]
                ps = ps_all[:, 1024 * (z % 2):1024 * (z % 2) + 1024]
                t_s = it["scores"](ps, s0.free + s1.free)
                c = slice(z % 16, z % 16 + 1)
                pl = pslot[z % 2]
                src, t_m, t_free = it["stat"](ps, pbuf[z % 2], NMX[:, c], t_s, pl.free)
                w = sum(it["nk"])
                p = pbuf[z % 2][:, 0:w]
                t_e = act(p, src, ACT.Exp, t_m, pl.free, bias=NMX[:, c], scale=1.0, accum_out=RSM[:, c])
                s0.free = s1.free = [t_free if t_free is not None else t_e]
                t_r = DVE.do(lambda e: e.reciprocal(RIN[:, c], RSM[:, c]), t_e)
                st.append(dict(z=z, c=c, p=p, t_e=t_e, t_r=t_r))

            def turn(n):
                it, s = items[n], st[n]
                z = s["z"]
                PE.wait(s["t_e"], tpair[0].free, tpair[1].free)
                pt = tbuf[z % 2]
                off = 0
                toks = []
                for half in range(2):
                    ks = list(range(4 * half, min(4 * half + 4, len(it["nk"]))))
                    if not ks:
                        continue
                    b = tpair[half]
                    for k in ks:
                        w = it["nk"][k]
                        last = (lambda o, i: lambda e: e.transpose(o, i, ident))(
                            b.ap[0:w, 128 * (k % 4):128 * (k % 4) + 128], s["p"][:, 128 * k:128 * k + w])
                        if k != ks[-1]:
                            PE.quiet(last)
                    toks.append((half, ks, PE.do(last)))
                pslot[z % 2].free = [PE.last()]
                outs = []
                for half, ks, t in toks:
                    b = tpair[half]
                    full = [k for k in ks if it["nk"][k] == 128]
                    parts = []
                    if full:
                        o0 = 128 * (full[0] % 4)
                        parts.append((slice(0, 128), 128 * full[0], 128 * len(full), o0))
                    if len(full) < len(ks):
                        parts.append((slice(0, it["nk"][ks[-1]]), 128 * ks[-1], 128, 128 * (ks[-1] % 4)))
                    for pr, d0, n_, o0 in parts:
                        if half == 0:
                            t2 = cp(DVE, pt[pr, d0:d0 + n_], b.ap[pr, o0:o0 + n_], t, tslot[z % 2].free)
                        else:
                            t2 = act(pt[pr, d0:d0 + n_], b.ap[pr, o0:o0 + n_], ACT.Copy, t, tslot[z % 2].free)
                        outs.append(t2)
                    b.free = [outs[-1]] if len(parts) == 1 else outs[-2:]
                s["t_pt"] = outs

            def values(n):
                it, s = items[n], st[n]
                z = s["z"]
                ob = opair[z % 2]
                PE.wait(ob.free, s["t_pt"], it["t_v"])
                pt = tbuf[z % 2]
                nk = it["nk"]
                for k, w in enumerate(nk):
                    last = mm(ob.ap[:, 0:64], pt[0:w, 128 * k:128 * k + 128], it["v"](k)[0:w], k == 0, k == len(nk) - 1)
                    if k < len(nk) - 1:
                        PE.quiet(last)
                t_o = PE.do(last)
                tslot[z % 2].free = [t_o]
                t_f = stt(it["out"], ob.ap[:, 0:64], RIN[:, s["c"]], it["out"], ALU.mult, ALU.mult, t_o, s["t_r"], it["t_g"])
                ob.free = [t_f]
                it["done"] = t_f

            N = len(items)
            for n in range(N + 2):
                if n < N:
                    scores(n)
                if single and n >= 2:
                    values(n - 2)
                if 1 <= n <= N:
                    turn(n - 1)
                if not single and n >= 2:
                    values(n - 2)
            seq[0] += N
            for p in banks:
                p.free = p.free + [PE.last(), ACTQ.last(), DVE.last()]

        def max_stat(ps, p, nmx, t_s, free, w):
            t_m = DVE.do(lambda e: e.tensor_reduce(nmx, ps[:, 0:w], X, ALU.max, negate=True), t_s)
            return ps[:, 0:w], t_m, None

        for kv in range(2):
            t_qt, t_kt = [], []
            t_lastq = t_lastk = None
            enter_phase()
            for i in range(NT):
                q3 = QKV[:, i, 256 * kv:256 * kv + 256].rearrange("p (h c) -> p h c", c=64)
                k1 = QKV[:, i, 512 + 64 * kv:576 + 64 * kv]
                t1 = act(QS[:, :, 0, :].bitcast(R), q3, ACT.Copy, t_rope[i], t_lastq)
                t2 = tt(DVE, QS[:, :, 1, :], q3, QS[:, :, 0, :], ALU.subtract, t1)
                t3 = act(KS[:, 0:2, :].bitcast(R), bc(k1, 1, 2), ACT.Copy, t_rope[i], t_lastk)
                t4 = tt(DVE, KS[:, 2:4, :], bc(k1, 1, 2), KS[:, 0:2, :], ALU.subtract, t3)
                ps = bank(range(8))
                PE.wait(ps.free, t2)
                for h in range(4):
                    f = (lambda o, s: lambda e: e.transpose(o, s, ident))(ps.ap[:, 128 * h:128 * h + 128], QS[:, h, :, :])
                    if h < 3:
                        PE.quiet(f)
                t_p = t_lastq = PE.do(f)
                t = act(QT[:, :, 128 * i:128 * i + 128], ps.ap.rearrange("p (h c) -> p h c", c=128), ACT.Copy, t_p)
                ps.free = [t]
                t_qt.append(t)
                ps = bank(range(8))
                PE.wait(ps.free, t4)
                for h in range(2):
                    f = (lambda o, s: lambda e: e.transpose(o, s, ident))(ps.ap[:, 128 * h:128 * h + 128], KS[:, 2 * h:2 * h + 2, :])
                    if h < 1:
                        PE.quiet(f)
                t_p = t_lastk = PE.do(f)
                t = cp(DVE, KT[:, :, 128 * i:128 * i + 128], ps.ap[:, 0:256].rearrange("p (h c) -> p h c", c=128), t_p)
                ps.free = [t]
                t_kt.append(t)
            items = []
            for h in range(4):
                for i in range(NT):
                    def scores(ps, free, h=h, i=i, t_kt=t_kt, t_qt=t_qt):
                        PE.wait(free, t_qt[i], t_kt)
                        for half in range(2):
                            for n in range(2):
                                f = mm(ps[:, 512 * half:512 * half + 512], QT[:, h, 128 * i:128 * i + 128],
                                       KT[:, n, 512 * half:512 * half + 512], n == 0, n == 1)
                                if half + n < 2:
                                    PE.quiet(f)
                        return PE.do(f)

                    items.append(dict(
                        nk=[128] * 8, scores=scores,
                        stat=lambda ps, p, nmx, t_s, free: max_stat(ps, p, nmx, t_s, free, 1024),
                        v=lambda k, kv=kv: QKV[:, k, 640 + 64 * kv:704 + 64 * kv], t_v=[t_qkv[k][2] for k in range(8)],
                        out=MIXA[:, i, 64 * (4 * kv + h):64 * (4 * kv + h) + 64], t_g=t_gA[i]))
            attention(items, PB, PT)

        MIXB = sb([128, 8, 512], F, W0 + 16 * KB)
        QH = sb([128, 2, T], R, W0 + 32 * KB)
        QL = sb([128, 2, T], R, W0 + 40 * KB)
        KH = sb([128, 2, T], R, W0 + 48 * KB)
        KL = sb([128, 2, T], R, W0 + 56 * KB)
        VB = sb([128, 8, 256], F, W0 + 64 * KB)
        BI = sb([128, 4, 14, 64], F, W0 + 72 * KB)
        SBN = [sb([128, 576], F, W0 + 86 * KB + 2304 * i) for i in range(2)]
        PTN = [sb([128, 640], F, W0 + 86 * KB + 4608)] * 2
        ZERO = sb([120, 128], F, W0 + 72 * KB)

        enter_phase()
        t = POOL.do(lambda e: e.memset(ZERO[:, :], 0.0))
        t = SP.dma(rpb_d, ZERO[:, :], land("rpb"), t)
        t_pad = SP.dma(rpb_d[:, 48:79], a["na_rpb"].rearrange("a h r c -> (a h r) c"), land("rpb"), t)
        t_pad = SP.dma(bias_d, bass.AP(rpb_d.tensor, 63, [[128, 120], [-1, 64], [1, 64]]), land("rpb"), t_pad)
        for hh in range(2):
            enter_phase()
            t_b = []
            for half in range(2):
                for h in range(4):
                    first = (4 * hh + h) * 15 + (1 if half == 0 else 0)
                    src = bias_d[first:first + 14].rearrange("r c k -> c r k")
                    t_b.append(SP.dma(BI[64 * half:64 * half + 64, h, :, :], src, land(f"bi{half}{h}"), t_pad))
            t_bi = []
            for h in range(4):
                t_bi.append(tt(POOL, BI[:, h, :, :], BI[:, h, :, :], bc(cst(C_COL, 64), 1, 14), ALU.add, t_b[h], t_b[4 + h], t_cst))
            t_q, t_k = [], []
            for (hi, lo, toks, sc) in ((QH, QL, t_q, 0.125), (KH, KL, t_k, 1.0)):
                with Block() as b:
                    for c in range(2):
                        for half in range(2):
                            ps = bank(range(8))
                            t = gemm_tr(b, 128 * c, 128 * c + 128, half, ps.ap, AH, AL, 8, ps.free, t_act)
                            sl = slice(512 * half, 512 * half + 512)
                            t_h = act(hi[:, c, sl], ps.ap, ACT.Copy, t, scale=sc)
                            t_l = stt(lo[:, c, sl], ps.ap, sc, hi[:, c, sl].bitcast(F), ALU.mult, ALU.subtract, t_h)
                            ps.free = [t_h, t_l]
                            toks += [t_h, t_l]
            t_v, t_g = [], []
            with Block() as b:
                for i in range(NT):
                    ps = bank(range(8))
                    t = gemm_nat(b, i, ps.ap[:, 0:256], AH, AL, 8, 0, 256, ps.free, t_act)
                    t = act(VB[:, i, :], ps.ap[:, 0:256], ACT.Copy, t)
                    ps.free = [t]
                    t_v.append(t)
            with Block() as b:
                for i in range(NT):
                    ps = bank(range(8))
                    t = gemm_nat(b, i, ps.ap[:, 0:256], AH, AL, 8, 0, 256, ps.free, t_act)
                    t = act(MIXB[:, i, 256 * hh:256 * hh + 256], ps.ap[:, 0:256], ACT.Silu, t)
                    ps.free = [t]
                    t_g.append(t)
            for inner in range(2):
                items = []
                t_mask = []
                if inner:
                    t_all = DVE.last()
                    t_mask = [POOL.do(lambda e: e.memset(BI[64:128, :, 2, :], NEG), t_all),
                              POOL.do(lambda e: e.memset(BI[0:64, :, 10, :], NEG), t_all)]
                for h in range(4):
                    for i in ((2, 3, 4, 5) if inner else (0, 1, 6, 7)):
                        w = 576 if inner else 512
                        row0 = 2 * i - 4 if inner else (0 if i < 2 else 8)
                        k0 = 64 * row0
                        j0 = row0 - 2 * i + 6

                        def scores(ps, free, h=h, i=i, w=w, k0=k0, t_q=t_q, t_k=t_k):
                            PE.wait(free, t_q, t_k)
                            pr = slice(64 * (h % 2), 64 * (h % 2) + 64)
                            qs = slice(128 * i, 128 * i + 128)
                            c = h // 2
                            for s in range(0, w, 512):
                                n = min(512, w - s)
                                ks = slice(k0 + s, k0 + s + n)
                                o = ps[:, s:s + n]
                                PE.quiet(mm(o, QH[pr, c, qs], KH[pr, c, ks], True, False))
                                PE.quiet(mm(o, QL[pr, c, qs], KH[pr, c, ks], False, False))
                                f = mm(o, QH[pr, c, qs], KL[pr, c, ks], False, True)
                                if s + 512 < w:
                                    PE.quiet(f)
                            return PE.do(f)

                        def stat(ps, p, nmx, t_s, free, h=h, w=w, j0=j0, t_bi=t_bi, t_mask=t_mask):
                            bias = BI[:, h, j0:j0 + w // 64, :].rearrange("p r c -> p (r c)")
                            t_a = tt(DVE, p[:, 0:w], ps[:, 0:w], bias, ALU.add, t_s, free, t_bi[h], t_mask)
                            t_m = DVE.do(lambda e: e.tensor_reduce(nmx, p[:, 0:w], X, ALU.max, negate=True), t_a)
                            return p[:, 0:w], t_m, t_a

                        nk = [128] * 4 + ([64] if inner else [])
                        items.append(dict(
                            nk=nk, scores=scores, stat=stat,
                            v=lambda k, h=h, k0=k0: VB[:, k0 // 128 + k, 64 * h:64 * h + 64], t_v=t_v,
                            out=MIXB[:, i, 64 * (4 * hh + h):64 * (4 * hh + h) + 64], t_g=t_g[i]))
                attention(items, SBN, PTN)

        XR = sb([128, 8, D], F, W0 + 32 * KB)
        FG = sb([128, D], F, W0 + 64 * KB)
        JK2 = sb([128, D], F, W0 + 68 * KB)
        XN = sb([128, 8, D], F, W0)
        enter_phase()
        t_xr = [SP.dma(XR[:, i, :], xv[i], land(f"x{i}")) for i in range(NT)]
        t_fg = SP.dma(FG[:, :], a["final_norm_gain"].partition_broadcast(128), land("fg"))
        t_act = None
        for i in range(NT):
            for g in range(2):
                ps = bank(range(8))
                PE.wait(ps.free)
                src = MIXA if g == 0 else MIXB
                for k in range(4):
                    f = (lambda o, s: lambda e: e.transpose(o, s, ident))(
                        ps.ap[:, 128 * k:128 * k + 128], src[:, i, 128 * k:128 * k + 128])
                    if k < 3:
                        PE.quiet(f, DVE.last())
                t_p = PE.do(f)
                sl = slice(128 * i, 128 * i + 128)
                pv = ps.ap.rearrange("p (k c) -> p k c", c=128)
                t_h = act(AH[:, 4 * g:4 * g + 4, sl], pv, ACT.Copy, t_p)
                t_l = tt(DVE, AL[:, 4 * g:4 * g + 4, sl], pv, AH[:, 4 * g:4 * g + 4, sl].bitcast(F), ALU.subtract, t_h)
                ps.free = [t_h, t_l]
                t_act = t_l
        t_x1 = [[] for _ in range(NT)]
        for n in range(4):
            with Block() as b:
                for i in range(NT):
                    ps = bank(range(8))
                    t = gemm_nat(b, i, ps.ap[:, 0:256], AH, AL, 8, 0, 256, ps.free, t_act)
                    xs = XR[:, i, 256 * n:256 * n + 256]
                    t = tt(DVE, xs, xs, ps.ap[:, 0:256], ALU.add, t, t_xr[i])
                    ps.free = [t]
                    t_x1[i].append(t)
        t_x2, t_sp = [], []
        for i in range(NT):
            t = act(JK2[:, :], XR[:, i, :], ACT.Square, t_x1[i], ACTQ.last(), accum_out=STAT[:, 24 + i:25 + i])
            t = ts(DVE, STAT[:, 32 + i:33 + i], STAT[:, 24 + i:25 + i], 1.0 / D, 1e-6, ALU.mult, ALU.add, t)
            t = rpow(STAT[:, 40 + i:41 + i], STAT[:, 32 + i:33 + i], 1, t)
            t = stt(XR[:, i, :], XR[:, i, :], STAT[:, 40 + i:41 + i], FG[:, :], ALU.mult, ALU.mult, t, t_fg)
            t_x2.append(t)
            t_sp.append(SP.dma(x2_d[128 * i:128 * i + 128, :], XR[:, i, :], land(f"x{i}"), t))

        t_act = norm_transpose(lambda i: XR[:, i, :], t_x2, lambda i: XN[:, i, :], JK2[:, :], "g_pre")
        ZB = sb([128, 8, 512], F, W0)
        CN = sb([128, 8, 416], F, W0 + 16 * KB)
        RT = sb([128, 2, 8, 2, 16], F, W0 + 29 * KB)
        CTH = sb([128, 3, T], R, W0 + 31 * KB)
        CTL = sb([128, 3, T], R, W0 + 43 * KB)
        STG = [sb([128, T], F, W0 + (55 + 4 * i) * KB) for i in range(3)]
        VN = sb([128, 8, 512], F, W0 + 55 * KB)
        QN = [sb([128, 768], F, W0 + (71 + 3 * i) * KB) for i in range(2)]
        PM = [sb([128, T], F, W0 + (77 + 4 * i) * KB) for i in range(2)]
        PTM = [sb([128, T], F, W0 + (85 + 4 * i) * KB) for i in range(2)]
        TAB = [sb([128, 8, 16], F, W0 + 77 * KB + 512 * i) for i in range(5)]
        JK3 = sb([128, 256], F, W0 + 85 * KB)
        QTM = sb([96, 8, T], F, RA)
        KTM = sb([96, 8, T], F, RA + 32 * KB)
        enter_phase()
        for q in (ACTQ, DVE, POOL):
            q.wait(t_sp)

        t_c = [[] for _ in range(NT)]
        for n, w in ((0, 256), (1, 160)):
            with Block() as b:
                for i in range(NT):
                    ps = bank(range(8))
                    t = gemm_nat(b, i, ps.ap[:, 0:w], AH, AL, 8, 0, w, ps.free, t_act)
                    t = act(CN[:, i, 256 * n:256 * n + w], ps.ap[:, 0:w], ACT.Copy, t)
                    ps.free = [t]
                    t_c[i].append(t)
        t_zb = [[] for _ in range(NT)]
        for n in range(2):
            with Block() as b:
                for i in range(NT):
                    ps = bank(range(8))
                    t = gemm_nat(b, i, ps.ap[:, 0:256], AH, AL, 8, 0, 256, ps.free, t_act)
                    t = act(ZB[:, i, 256 * n:256 * n + 256], ps.ap[:, 0:256], ACT.Silu, t)
                    ps.free = [t]
                    t_zb[i].append(t)

        t_st = []
        for i in range(NT):
            t_st.append(act(JK3[:, :], CN[:, i, 0:256], ACT.Square, t_c[i], ACTQ.last(), accum_out=STAT[:, 64 + 2 * i:65 + 2 * i]))
            t_st.append(act(JK3[:, 0:128], CN[:, i, 256:384], ACT.Square, ACTQ.last(), accum_out=STAT[:, 65 + 2 * i:66 + 2 * i]))
        s_in = STAT[:, 64:80].rearrange("p (i s) -> p s i", s=2)
        s_ms = STAT[:, 80:96].rearrange("p (i s) -> p s i", s=2)
        t_m = [ts(DVE, s_ms[:, s, :], s_in[:, s, :], 1.0 / n, 1e-6, ALU.mult, ALU.add, t_st) for s, n in ((0, 256), (1, 128))]
        t_r = rpow(STAT[:, 96:112], STAT[:, 80:96], 16, t_m)
        t_cn = []
        for i in range(NT):
            t1 = ts(DVE, CN[:, i, 0:256], CN[:, i, 0:256], STAT[:, 96 + 2 * i:97 + 2 * i], None, ALU.mult, None, t_r)
            t2 = ts(DVE, CN[:, i, 256:384], CN[:, i, 256:384], STAT[:, 97 + 2 * i:98 + 2 * i], None, ALU.mult, None, t_r)
            t_cn.append([t1, t2])

        ang, sinT, cosT, yy, nn = (TAB[i][:, :, :] for i in range(5))
        MAGIC = 12582912.0
        two_pi = 2.0 * np.pi
        c1 = 6.28125
        c2 = float((np.float32(two_pi - c1).view(np.uint32) & np.uint32(0xFFFFF000)).view(np.float32))
        c3 = float(two_pi - c1 - c2)
        t_a = tt(DVE, ang, bc(VT[:, 0:8], 2, 16), bc(cst(C_INV, 16), 1, 8), ALU.mult, t_vec)
        t_tab = []
        for dst, turn_, add in ((sinT, 0.0, 0.0), (cosT, 0.25, float(np.pi / 2))):
            t = ts(DVE, yy, ang, 1.0 / two_pi, turn_, ALU.mult, ALU.add, t_a, t_tab)
            t = ts(DVE, nn, yy, MAGIC, None, ALU.add, None, t)
            t = ts(DVE, yy, nn, -MAGIC, None, ALU.add, None, t)
            f2 = lambda ap: ap.rearrange("p i c -> p (i c)")
            t = stt(f2(dst), f2(yy), -c1, f2(ang), ALU.mult, ALU.add, t)
            t = stt(f2(dst), f2(yy), -c2, f2(dst), ALU.mult, ALU.add, t)
            t = stt(f2(dst), f2(yy), -c3, f2(dst), ALU.mult, ALU.add, t)
            t = ts(DVE, dst, dst, add, None, ALU.add, None, t)
            t = ts(DVE, dst, dst, 3.1415925, -3.1415925, ALU.min, ALU.max, t)
            t_tab = [act(dst, dst, ACT.Sin, t)] + t_tab
        kp = CN[:, :, 384:416].rearrange("p i (f c) -> p i f c", f=2)
        RA_, RB_ = RT[:, 0], RT[:, 1]

        def rotate(x4, cos, sin, *tokens):
            t1 = tt(DVE, RA_, x4, bc(cos, 2, 2), ALU.mult, DVE.last(), *tokens)
            t2 = tt(DVE, RB_[:, :, 0, :], x4[:, :, 1, :], sin, ALU.mult, DVE.last(), *tokens)
            t3 = tt(DVE, RB_[:, :, 1, :], x4[:, :, 0, :], sin, ALU.mult, DVE.last(), *tokens)
            t4 = tt(DVE, x4[:, :, 0, :], RA_[:, :, 0, :], RB_[:, :, 0, :], ALU.subtract, t1, t2, t3)
            return tt(DVE, x4[:, :, 1, :], RA_[:, :, 1, :], RB_[:, :, 1, :], ALU.add, t4)

        t_kp = rotate(kp, cosT, sinT, t_tab, *[t_c[i][1] for i in range(NT)])

        stage = [Place(STG[i]) for i in range(3)]
        n_st = [0]
        t_feat, t_zg = [None] * 13, [None] * 20

        def spill(ntiles, dst, toks, func, bias):
            j = 0
            while j < ntiles:
                w = min(2, ntiles - j)
                with Block() as b:
                    for c in range(w):
                        z = n_st[0] % 3
                        n_st[0] += 1
                        st_ = stage[z]
                        t_o = []
                        for half in range(2):
                            ps = bank(range(8))
                            t = gemm_tr(b, 128 * c, 128 * c + 128, half, ps.ap, AH, AL, 8, ps.free, t_act)
                            kw = {} if bias is None else dict(bias=bias(j + c))
                            t = act(STG[z][:, 512 * half:512 * half + 512], ps.ap, func, t, st_.free, t_vec, **kw)
                            ps.free = [t]
                            t_o.append(t)
                        toks(j + c, SP.dma(dst(j + c), STG[z][:, :], land(f"stg{z}"), t_o))
                        st_.free = [(lands[f"stg{z}"].sem, lands[f"stg{z}"].n)]
                j += w

        spill(13, lambda j: feat_d[j], lambda j, t: t_feat.__setitem__(j, t), ACT.Copy, None)
        spill(4, lambda j: zg_d[j], lambda j, t: t_zg.__setitem__(j, t), ACT.Silu, None)
        spill(16, lambda j: zg_d[4 + j], lambda j, t: t_zg.__setitem__(4 + j, t), ACT.Sigmoid, lambda j: vec("b_gate", j))

        t_ct = [[], []]
        for k in range(3):
            gain = vec("g_q", k) if k < 2 else vec("g_kv")
            for g in range(2):
                ps = bank(range(8))
                PE.wait(ps.free, t_cn[4 * g:4 * g + 4])
                for i in range(4):
                    f = (lambda o, s: lambda e: e.transpose(o, s, ident))(
                        ps.ap[:, 128 * i:128 * i + 128], CN[:, 4 * g + i, 128 * k:128 * k + 128])
                    if i < 3:
                        PE.quiet(f)
                t = PE.do(f)
                sl = slice(512 * g, 512 * g + 512)
                t_h = act(CTH[:, k, sl], ps.ap, ACT.Identity, t, t_vec, scale=gain)
                t_l = stt(CTL[:, k, sl], ps.ap, gain, CTH[:, k, sl].bitcast(F), ALU.mult, ALU.subtract, t_h)
                ps.free = [t_h, t_l]
                t_ct[g] += [t_h, t_l]
        enter_phase()
        for q in (ACTQ, DVE, POOL):
            q.wait([stage[i].free for i in range(3)])
        t_q = [[] for _ in range(NT)]
        qfree = [[], []]
        with Block() as b:
            for i in range(NT):
                z = i % 2
                sl = slice(128 * i, 128 * i + 128)
                t_e = []
                for g in range(2):
                    ps = bank(range(8))
                    t = product(ps.ap[:, 0:384], [(CTH[:, k, sl], CTL[:, k, sl]) for k in range(2)],
                                [(b.hi[:, k, 384 * g:384 * g + 384], b.lo[:, k, 384 * g:384 * g + 384]) for k in range(2)],
                                b.tok, ps.free, t_ct[i // 4])
                    t = act(QN[z][:, 384 * g:384 * g + 384], ps.ap[:, 0:384], ACT.Copy, t, qfree[z], scale=96.0 ** -0.5)
                    ps.free = [t]
                    t_e.append(t)
                pe4 = QN[z][:, :].rearrange("p (h c) -> p h c", c=96)[:, :, 64:96].rearrange("p h (f c) -> p h f c", f=2)
                t_rot = rotate(pe4, bc(cosT[:, i, :], 1, 8), bc(sinT[:, i, :], 1, 8), t_tab, t_e)
                for g in range(2):
                    ps = bank(range(8))
                    PE.wait(ps.free, t_rot)
                    for h in range(4):
                        f = (lambda o, s: lambda e: e.transpose(o, s, ident))(
                            ps.ap[0:96, 128 * h:128 * h + 128], QN[z][:, 96 * (4 * g + h):96 * (4 * g + h) + 96])
                        if h < 3:
                            PE.quiet(f)
                    t = PE.do(f)
                    o = QTM[:, 4 * g:4 * g + 4, sl]
                    pv = ps.ap[0:96, :].rearrange("p (h c) -> p h c", c=128)
                    t = act(o, pv, ACT.Copy, t) if g else cp(DVE, o, pv, t)
                    ps.free = [t]
                    t_q[i].append(t)
                qfree[z] = [PE.last()]
        hold[0] = True
        t_k, t_v = [], []
        with Block() as b:
            kh_, kl_, vh_, vl_ = (x[:, 0, o:o + 512] for o in (0, 512) for x in (b.hi, b.lo))
            for i in range(NT):
                sl = slice(128 * i, 128 * i + 128)
                ps = bank(range(8))
                t = product(ps.ap, [(CTH[:, 2, sl], CTL[:, 2, sl])], [(vh_, vl_)],
                            b.tok, ps.free, t_ct[i // 4])
                t = act(VN[:, i, :], ps.ap, ACT.Copy, t)
                ps.free = [t]
                t_v.append(t)
            for j in range(4):
                for half in range(2):
                    sl = slice(512 * half, 512 * half + 512)
                    ps = bank(range(8))
                    t = product(ps.ap, [(kh_[:, 128 * j:128 * j + 128], kl_[:, 128 * j:128 * j + 128])],
                                [(CTH[:, 2, sl], CTL[:, 2, sl])], b.tok, ps.free, t_ct[half])
                    t1 = cp(DVE, KTM[0:64, 2 * j, sl], ps.ap[0:64, :], t)
                    t2 = act(KTM[0:64, 2 * j + 1, sl], ps.ap[64:128, :], ACT.Copy, t, t1)
                    ps.free = [t1, t2]
                    t_k += [t1, t2]
        for half in range(2):
            sl = slice(512 * half, 512 * half + 512)
            ps = bank(range(8))
            PE.wait(ps.free, t_kp)
            for i in range(4):
                f = (lambda o, s: lambda e: e.transpose(o, s, ident))(
                    ps.ap[0:32, 128 * i:128 * i + 128], CN[:, 4 * half + i, 384:416])
                if i < 3:
                    PE.quiet(f)
            t = PE.do(f)
            for h in range(0, 8, 2):
                t_k.append(cp(DVE, KTM[64:96, h, sl], ps.ap[0:32, :], t))
            t = [t, DVE.last()]
            for h in range(1, 8, 2):
                t_k.append(act(KTM[64:96, h, sl], ps.ap[0:32, :], ACT.Copy, t))
            ps.free = [DVE.last(), ACTQ.last()]

        enter_phase()
        items = []
        for h in range(8):
            for i in range(NT):
                w = 128 * (i + 1)

                def scores(ps, free, h=h, i=i, w=w):
                    PE.wait(free, t_q[i], t_k)
                    for s in range(0, w, 512):
                        n = min(512, w - s)
                        f = mm(ps[:, s:s + n], QTM[:, h, 128 * i:128 * i + 128], KTM[:, h, s:s + n], True, True)
                        if s + 512 < w:
                            PE.quiet(f)
                    return PE.do(f)

                def stat(ps, p, nmx, t_s, free, w=w):
                    d = ps[:, w - 128:w]
                    t_a = tt(DVE, d, d, cst(C_CAUS, 128), ALU.add, t_s)
                    return max_stat(ps, p, nmx, t_a, free, w)

                items.append(dict(nk=[128] * (i + 1), scores=scores, stat=stat,
                                  v=lambda k, h=h: VN[:, k, 64 * h:64 * h + 64], t_v=t_v,
                                  out=ZB[:, i, 64 * h:64 * h + 64], t_g=t_zb[i]))
        attention(items, PM, PTM)

        YAH = sb([128, 4, T], R, W0 + 16 * KB)
        YAL = sb([128, 4, T], R, W0 + 32 * KB)
        FR, FK, FV = (sb([128, T + 1], F, RA + 4352 * i) for i in range(3))
        SG, AI, CU, E1, E2, E3, KK, TM = (sb([128, T], F, RA + (13 + 4 * i) * KB) for i in range(8))
        CH = [[sb([128, 8, 64], F, RA + (13 + 14 * e + 2 * i) * KB) for i in range(7)] for e in range(2)]
        AR = sb([128, 2, 16, 64], F, RA + 45 * KB)
        BK = sb([128, 16, 2, 64], F, RA + 53 * KB)
        BON = sb([128, T], F, RA + 61 * KB)
        BHN, KHN, VNN = (sb([128, 8, 128], F, RA + (65 + 4 * i) * KB) for i in range(3))
        MTS, GS, QSS, YL, DG = (sb([128, 16, 64], F, RA + (77 + 4 * i) * KB) for i in range(5))
        YT = sb([128, T], F, RA + 97 * KB)
        ZAT = sb([128, T], F, W0 + 88 * KB)
        WA = sb([128, T], F, W0 + 48 * KB)
        LW = sb([128, 512], F, W0 + 52 * KB)
        RST = sb([128, T], F, W0 + 54 * KB)
        GM = [[sb([128, 8, 64], F, W0 + (58 + 6 * e + 2 * i) * KB) for i in range(3)] for e in range(2)]
        ZZ = [[sb([128, 8, 128], F, W0 + (70 + 8 * e + 4 * i) * KB) for i in range(2)] for e in range(2)]
        HX = sb([128, 16, 64], F, W0 + 74 * KB)
        KA1 = sb([128, 4], F, W0 + 86 * KB)
        CD = DECAY

        enter_phase()
        t_rst = SP.dma(RST[:, :], a["consts"][:, C_RST:C_RST + 1024], land("rst"))
        t_lw = [SP.dma(LW[0:64, :], a["w_decay_up_2"], land("lw0")), SP.dma(LW[64:128, :], a["w_iclr_up_2"], land("lw1"))]
        t_col = [POOL.do(lambda e, f=f: e.memset(f[:, 0:1], 0.0)) for f in (FR, FK, FV)]
        t_ka = ts(DVE, KA1[:, :], VT[:, VOFF["k_a"]:VOFF["k_a"] + 4], -1.0, 1.0, ALU.mult, ALU.add, t_vec)

        def shifted(buf, mu, t):
            x = buf[:, 1:T + 1]
            t = tt(DVE, TM[:, :], buf[:, 0:T], x, ALU.subtract, t, t_col, DVE.last())
            return stt(x, TM[:, :], mu, x, ALU.mult, ALU.add, t)

        def head_scale(sq, t_sq, c0, mul, add, floor):
            ps = bank(range(8))
            PE.wait(ps.free, t_sq)
            for m in range(8):
                f = mm(ps.ap[:, 2 * m:2 * m + 2], sq[:, 128 * m:128 * m + 128], cst(C_ONE2, 2), True, True)
                if m < 7:
                    PE.quiet(f)
            t = PE.do(f)
            s0, s1 = STAT[:, c0:c0 + 16], STAT[:, c0 + 16:c0 + 32]
            if floor is None:
                t = ts(DVE, s0, ps.ap[:, 0:16], mul, add, ALU.mult, ALU.add, t)
            else:
                t = ts(DVE, s0, ps.ap[:, 0:16], floor, None, ALU.max, None, t)
            ps.free = [t]
            t = rpow(s1, s0, 16, t)
            pair = (banks[6], banks[7])
            t = cp(POOL, HX[:, :, :], bc(s1, 2, 64), t, PE.last())
            PE.wait(t, pair[0].free, pair[1].free)
            for m in range(8):
                l = HX[:, 2 * m:2 * m + 2, :].rearrange("p h c -> p (h c)")
                f = mm(pair[m // 4].ap[:, 128 * (m % 4):128 * (m % 4) + 128], l, ident, True, True)
                if m < 7:
                    PE.quiet(f)
            return pair, PE.do(f)

        PS67 = ps_all[:, 3072:4096]
        low = range(6)
        ch3 = lambda t_: t_.rearrange("p (c t) -> p c t", t=64)
        t_fr = SP.dma(FR[:, 1:T + 1], feat_d[12], land("fr"), t_feat[12])
        t = shifted(FR, vec("mu", 12), t_fr)
        t_wa = [act(WA[0:64, :], FR[0:64, 1:T + 1], ACT.Tanh, t), cp(DVE, WA[64:128, :], FR[64:128, 1:T + 1], t)]

        for j in range(4):
            enter_phase()
            t_in = [SP.dma(b_[:, 1:T + 1], feat_d[4 * s + j], land(n_), t_feat[4 * s + j])
                    for s, (b_, n_) in enumerate(((FR, "fr"), (FK, "fk"), (FV, "fv")))]
            t_za = SP.dma(ZAT[:, :], zg_d[j], land("za"), t_zg[j])
            r_, k_, v_ = (b_[:, 1:T + 1] for b_ in (FR, FK, FV))
            t_s, t_ai = [], []
            for half in range(2):
                sl = slice(512 * half, 512 * half + 512)
                for p0, dst, bias, toks in ((0, SG, "w0", t_s), (64, AI, "a0", t_ai)):
                    ps = bank(low)
                    t = PE.do(mm(ps.ap, LW[p0:p0 + 64, 128 * j:128 * j + 128], WA[p0:p0 + 64, sl], True, True),
                              ps.free, t_lw, t_wa)
                    t = act(dst[:, sl], ps.ap, ACT.Sigmoid, t, t_vec, bias=vec(bias, j))
                    ps.free = [t]
                    toks.append(t)
            t_k1 = shifted(FK, vec("mu", 4 + j), t_in[1])
            t_kk = ts(DVE, KK[:, :], k_, vec("k_k", j), None, ALU.mult, None, t_k1)
            t_sq = act(E2[:, :], KK[:, :], ACT.Square, t_kk)
            pair, t_hs = head_scale(E2, t_sq, 256, None, None, 1e-24)
            t_cu = DVE.do(lambda e: e.tensor_tensor_scan(CU[:, :], RST[:, :], SG[:, :], 0.0, ALU.mult, ALU.add), t_s, t_rst)
            t_r1 = shifted(FR, vec("mu", j), t_in[0])
            t_v1 = shifted(FV, vec("mu", 8 + j), t_in[2])
            t_e1 = act(E1[:, :], CU[:, :], ACT.Exp, t_cu, scale=-CD)
            t_e3 = act(E3[:, :], CU[:, :], ACT.Exp, t_cu, scale=CD)
            t_kn = tt(DVE, KK[:, :], KK[:, :], PS67, ALU.mult, t_hs, t_sq)
            pair[0].free = pair[1].free = [t_kn]
            t_tm = tt(DVE, TM[:, :], CU[:, :], SG[:, :], ALU.subtract, t_cu, DVE.last())
            t_e2 = act(E2[:, :], TM[:, :], ACT.Exp, t_tm, PE.last(), scale=-CD)
            t_a0 = stt(AR[:, 0], ch3(KK[:, :]), -1.0, ch3(E2[:, :]), ALU.mult, ALU.mult, t_e2, t_kn)
            t_a1 = tt(POOL, AR[:, 1], ch3(r_), ch3(E1[:, :]), ALU.mult, t_e1, t_r1)
            t_pc = cp(DVE, PCT[:, :], ch3(E1[:, :])[:, :, 63], t_e1)
            t_dg = tt(POOL, DG[:, :, :], bc(cst(C_I64, 64), 1, 16), bc(PCT[:, :], 2, 64), ALU.mult, t_pc)
            t = ts(DVE, TM[:, :], AI[:, :], vec("k_a", j), KA1[:, j:j + 1], ALU.mult, ALU.add, t_ai, t_ka, t_e2)
            t_kf = tt(DVE, k_, k_, TM[:, :], ALU.mult, t, t_kk)
            t_b = tt(DVE, TM[:, :], KK[:, :], AI[:, :], ALU.mult, t_kf, t_kn)
            t_b0 = tt(DVE, BK[:, :, 0, :], ch3(TM[:, :]), ch3(E3[:, :]), ALU.mult, t_b, t_e3)
            t_b1 = tt(DVE, BK[:, :, 1, :], ch3(k_), ch3(E3[:, :]), ALU.mult, t_kf, t_e3)
            t_bh = tt(DVE, ch3(CU[:, :]), BK[:, :, 0, :], bc(PCT[:, :], 2, 64), ALU.mult, t_b0, t_pc, t_e1, t_e3, t_tm)
            t_kh = tt(DVE, ch3(SG[:, :]), BK[:, :, 1, :], bc(PCT[:, :], 2, 64), ALU.mult, t_b1, t_tm)
            t = stt(TM[:, :], r_, vec("r_k", j), k_, ALU.mult, ALU.mult, t_b0, t_r1, t_kf)
            t_p = []
            for half in range(2):
                sl = slice(512 * half, 512 * half + 512)
                ps = bank(low)
                t2 = PE.do(mm(ps.ap, cst(C_BLK, 128), TM[:, sl], True, True), t, ps.free)
                t_p.append(tt(DVE, BON[:, sl], v_[:, sl], ps.ap, ALU.mult, t2, t_v1))
                ps.free = [t_p[-1]]

            t_nat = dict(a=[], b=[], k=[], v=[])
            for name, src, t_src in (("a", None, t_a0), ("b", CU, t_bh), ("k", SG, t_kh), ("v", v_, t_v1)):
                for g in range(2):
                    ps = bank(low)
                    PE.wait(ps.free, t_src)
                    for m in range(4 * g, 4 * g + 4):
                        s = AR[:, 0, 2 * m:2 * m + 2, :].rearrange("p c t -> p (c t)") if name == "a" else src[:, 128 * m:128 * m + 128]
                        f = (lambda o, s_: lambda e: e.transpose(o, s_, ident))(ps.ap[:, 128 * (m % 4):128 * (m % 4) + 128], s)
                        if m % 4 < 3:
                            PE.quiet(f)
                    t = PE.do(f)
                    pv = ps.ap.rearrange("p (m c) -> p m c", c=128)
                    gs = slice(4 * g, 4 * g + 4)
                    if name == "a":
                        t1 = act(ZZ[0][0][:, gs, 0:64], pv[:, :, 0:64], ACT.Copy, t)
                        t2 = act(ZZ[1][0][:, gs, 0:64], pv[:, :, 64:128], ACT.Copy, t)
                        ps.free = [t2]
                        t_nat["a"] += [t1, t2]
                    else:
                        dst = {"b": BHN, "k": KHN, "v": VNN}[name]
                        t1 = act(dst[:, gs, :], pv, ACT.Copy, t)
                        ps.free = [t1]
                        t_nat[name].append(t1)
            t_ar, t_bk = [t_a0, t_a1], [t_b0, t_b1]
            DVE.wait(PE.last(), t_nat["b"], t_nat["k"], t_nat["v"])
            ACTQ.wait(PE.last(), t_p, t_dg, t_pc)

            def m3(col):
                return bc(cst(col, 64), 1, 8)

            t_g = [{}, {}]
            for e in range(2):
                pr = slice(64 * e, 64 * e + 64)
                ARB, AKT, RKT = GM[e]
                ND, NDT, NOT, B3, B4, B5, B6 = CH[e]
                tk = {x: [] for x in ("nd", "arb", "akt", "rkt")}
                for g in range(2):
                    gs = slice(4 * g, 4 * g + 4)
                    for s, d0, d1, n0, n1, k0 in ((0, ND, ARB, "nd", "arb", C_MD), (1, AKT, RKT, "akt", "rkt", C_MS)):
                        ps = bank(range(8))
                        PE.wait(ps.free, t_ar, t_bk)
                        for m in range(4 * g, 4 * g + 4):
                            for q in range(2):
                                c = 2 * m + q
                                f = mm(ps.ap[64 * q:64 * q + 64, 128 * (m % 4):128 * (m % 4) + 128], BK[pr, c, s, :],
                                       AR[pr, :, c, :], True, True)
                                if not (q and m % 4 == 3):
                                    PE.quiet(f)
                        t = PE.do(f)
                        pv = ps.ap.rearrange("p (m s c) -> p m s c", s=2, c=64)
                        t1 = tt(DVE, d0[:, gs, :], pv[:, :, 0, :], bc(cst(k0, 64), 1, 4), ALU.mult, t)
                        t2 = tt(DVE, d1[:, gs, :], pv[:, :, 1, :], bc(cst(C_MI, 64), 1, 4), ALU.mult, t)
                        ps.free = [t2]
                        tk[n0].append(t1)
                        tk[n1].append(t2)
                ps = bank(range(8))
                PE.wait(ps.free, t_ar, t_bk)
                for m in range(8):
                    for q in range(2):
                        c = 2 * m + q
                        f = mm(ps.ap[64 * q:64 * q + 64, 64 * m:64 * m + 64], AR[pr, 0, c, :], BK[pr, c, 0, :], True, True)
                        if not (q and m == 7):
                            PE.quiet(f)
                t = PE.do(f)
                pv = ps.ap.rearrange("p (m c) -> p m c", c=64)
                t1 = tt(DVE, NDT[:, :, :], pv, m3(C_MDT), ALU.mult, t)
                t2 = tt(DVE, NOT[:, :, :], pv, m3(C_MOT), ALU.mult, t)
                ps.free = [t2]
                tk["ndt"], tk["not"] = t1, t2
                tk["d1"] = tt(POOL, B5[:, :, :], ND[:, :, :], m3(C_I64), ALU.add, tk["nd"], t2)
                t_g[e] = tk

            def blocks(lhs, rhs, *tokens, n=64):
                per = 512 // n
                res = []
                PE.wait(*tokens)
                for g in range(8 // per):
                    ps = bank(range(8))
                    PE.wait(ps.free)
                    for m in range(per * g, per * g + per):
                        for q in range(2):
                            pq = slice(64 * q, 64 * q + 64)
                            f = mm(ps.ap[pq, n * (m - per * g):n * (m - per * g) + n], lhs(pq, m), rhs(pq, m), True, True)
                            if not (q and m == per * g + per - 1):
                                PE.quiet(f)
                    res.append((ps, PE.do(f)))
                return res

            def whole(buf):
                return lambda pq, m: buf[pq, m, :]

            def take(q, dst, r, add=None, *tokens):
                toks = []
                per = 8 // len(r)
                for g, (ps, t) in enumerate(r):
                    gs = slice(per * g, per * g + per)
                    pv = ps.ap.rearrange("p (m c) -> p m c", m=per)
                    if add is not None:
                        t2 = tt(DVE, dst[:, gs], pv, add[:, gs], ALU.add, t, *tokens)
                    elif q is ACTQ:
                        t2 = act(dst[:, gs], pv, ACT.Copy, t, *tokens)
                    else:
                        t2 = cp(DVE, dst[:, gs], pv, t, *tokens)
                    ps.free = [t2]
                    toks.append(t2)
                return toks

            steps = [{}, {}]
            for e in range(2):
                ND, NDT = CH[e][0], CH[e][1]
                s, tk = steps[e], t_g[e]
                s["r2"] = blocks(whole(NDT), whole(ND), tk["nd"], tk["ndt"])
                s["r2t"] = blocks(whole(ND), whole(NDT))
                s["x"] = blocks(whole(GM[e][1]), lambda pq, m, e=e: VNN[pq, m, 64 * e:64 * e + 64], tk["akt"], t_nat["v"])
            for e in range(2):
                s = steps[e]
                s["n2"] = take(ACTQ, CH[e][3], s["r2"])
                s["n2t"] = take(DVE, CH[e][4], s["r2t"])
                s["x"] = take(ACTQ, ZZ[e][0][:, :, 64:128], s["x"])
            for e in range(2):
                s = steps[e]
                s["rd2"] = blocks(whole(CH[e][4]), whole(CH[e][5]), s["n2t"], t_g[e]["d1"])
                s["r4"] = blocks(whole(CH[e][4]), whole(CH[e][3]), s["n2"])
                s["r4t"] = blocks(whole(CH[e][3]), whole(CH[e][4]))
            for e in range(2):
                s = steps[e]
                s["d2"] = take(DVE, CH[e][6], s["rd2"], CH[e][5])
                s["n4"] = take(ACTQ, CH[e][0], s["r4"], None, t_g[e]["d1"])
                s["n4t"] = take(ACTQ, CH[e][1], s["r4t"])
            for e in range(2):
                s = steps[e]
                s["rd3"] = blocks(whole(CH[e][1]), whole(CH[e][6]), s["n4t"], s["d2"])
                s["r8t"] = blocks(whole(CH[e][0]), whole(CH[e][1]), s["n4"])
            for e in range(2):
                s = steps[e]
                s["d3"] = take(DVE, CH[e][5], s["rd3"], CH[e][6])
                s["n8t"] = take(ACTQ, CH[e][3], s["r8t"])
            for e in range(2):
                s = steps[e]
                s["rd4"] = blocks(whole(CH[e][3]), whole(CH[e][5]), s["n8t"], s["d3"])
            for e in range(2):
                s = steps[e]
                s["d4"] = take(DVE, CH[e][6], s["rd4"], CH[e][5])
            for e in range(2):
                s = steps[e]
                s["rf"] = blocks(whole(CH[e][2]), whole(CH[e][6]), s["d4"], t_g[e]["not"])
                s["rz"] = blocks(whole(CH[e][6]), whole(ZZ[e][0]), s["x"], t_nat["a"], n=128)
            for e in range(2):
                s = steps[e]
                s["f"] = take(ACTQ, CH[e][4], s["rf"])
                s["z"] = take(ACTQ if e else DVE, ZZ[e][1], s["rz"])
            for it in range(3):
                for e in range(2):
                    s = steps[e]
                    s["rz"] = blocks(whole(CH[e][4]), whole(ZZ[e][1 if it == 0 else 0]), s["f"], s["z"], n=128)
                for e in range(2):
                    s = steps[e]
                    s["z"] = take(DVE, ZZ[e][0], s["rz"], ZZ[e][1])

            t_zz = steps[0]["z"] + steps[1]["z"]
            W_ = lambda e, pq, m: ZZ[e][0][pq, m, 0:64]
            U_ = lambda e, pq, m: ZZ[e][0][pq, m, 64:128]
            H_ = lambda buf: (lambda e, pq, m: buf[pq, m, 64 * e:64 * e + 64])
            G_ = lambda n: (lambda e, pq, m: GM[e][n][pq, m, :])
            plans = [("mt", [(W_, H_(BHN))]), ("q", [(W_, G_(0))]), ("g", [(H_(BHN), U_), (H_(KHN), H_(VNN))]),
                     ("y", [(U_, G_(0)), (H_(VNN), G_(2))])]
            t_out = {}
            for name, terms in plans:
                t_out[name] = []
                for q in range(2):
                    pq = slice(64 * q, 64 * q + 64)
                    ps = bank(range(8))
                    PE.wait(ps.free, t_zz, t_nat["b"], t_nat["k"], t_g[0]["arb"], t_g[1]["arb"], t_g[0]["rkt"], t_g[1]["rkt"])
                    for e in range(2):
                        for m in range(8):
                            for x, (l, r) in enumerate(terms):
                                f = mm(ps.ap[64 * e:64 * e + 64, 64 * m:64 * m + 64], l(e, pq, m), r(e, pq, m),
                                       x == 0, x == len(terms) - 1)
                                if not (e and m == 7 and x == len(terms) - 1):
                                    PE.quiet(f)
                    t = PE.do(f)
                    pv = ps.ap.rearrange("p (m c) -> p m c", c=64)
                    view = lambda b_: b_[:, :, :].rearrange("p (m q) c -> p m q c", q=2)[:, :, q, :]
                    if name == "mt":
                        t = tt(DVE, view(MTS), pv, view(DG), ALU.add, t, t_dg)
                    elif name == "q":
                        t = tt(DVE, view(QSS), pv, AR[:, 1].rearrange("p (m q) c -> p m q c", q=2)[:, :, q, :],
                               ALU.add, t, t_a1)
                    else:
                        t = act(view(GS if name == "g" else YL), pv, ACT.Copy, t)
                    ps.free = [t]
                    t_out[name].append(t)

            t_s = POOL.do(lambda e: e.memset(S2[:, 0, :], 0.0), DVE.last(), PE.last())
            t_y = []
            for c in range(16):
                if c % 8 == 0:
                    yb = banks[6 + c // 8]
                    PE.wait(yb.free)
                PE.wait(t_s, t_out["q"], t_out["mt"])
                cur, nxt = c % 2, (c + 1) % 2
                if c < 15:
                    sp = banks[4 + c % 2]
                    PE.wait(sp.free)
                    PE.quiet(mm(sp.ap[0:64, 0:64], MTS[0:64, c, :], S2[0:64, cur, :], True, True))
                    t_sp_ = PE.do(mm(sp.ap[64:128, 0:64], MTS[64:128, c, :], S2[64:128, cur, :], True, True))
                cc = 64 * (c % 8)
                PE.quiet(mm(yb.ap[0:64, cc:cc + 64], S2[0:64, cur, :], QSS[0:64, c, :], True, True))
                t_yc = PE.do(mm(yb.ap[64:128, cc:cc + 64], S2[64:128, cur, :], QSS[64:128, c, :], True, True))
                if c < 15:
                    t_s = tt(DVE, S2[:, nxt, :], sp.ap[:, 0:64], GS[:, c, :], ALU.add, t_sp_, t_out["g"],
                             t_y[-1:] if c % 8 == 0 else None, t_prev if c else None)
                    sp.free = [t_s]
                t_prev = t_yc
                if c % 8 == 7:
                    half = c // 8
                    t = tt(DVE, YT[:, 512 * half:512 * half + 512], yb.ap,
                           YL[:, 8 * half:8 * half + 8, :].rearrange("p c t -> p (c t)"), ALU.add, t_yc, t_out["y"])
                    yb.free = [t]
                    t_y.append(t)
            DVE.wait(t_y)
            t_yc = []
            for half in range(2):
                sl = slice(512 * half, 512 * half + 512)
                ps = bank(low)
                t = PE.do(mm(ps.ap, cst(C_BLKM, 128), YT[:, sl], True, True), t_y[half], ps.free)
                t = tt(DVE, YT[:, sl], YT[:, sl], ps.ap, ALU.subtract, t)
                ps.free = [t]
                t_yc.append(t)
            t_sq = act(E1[:, :], YT[:, :], ACT.Square, t_yc, PE.last())
            pair, t_hs = head_scale(E1, t_sq, 288, 1.0 / 64, 64e-5, None)
            t = tt(DVE, YT[:, :], YT[:, :], PS67, ALU.mult, t_hs, t_sq)
            pair[0].free = pair[1].free = [t]
            t = ts(DVE, YT[:, :], YT[:, :], vec("gn_gain", j), vec("gn_bias", j), ALU.mult, ALU.add, t)
            t = tt(DVE, YT[:, :], YT[:, :], BON[:, :], ALU.add, t, t_p)
            t = tt(DVE, YT[:, :], YT[:, :], ZAT[:, :], ALU.mult, t, t_za)
            t_h = act(YAH[:, j, :], YT[:, :], ACT.Copy, t)
            t_l = tt(DVE, YAL[:, j, :], YT[:, :], YAH[:, j, :].bitcast(F), ALU.subtract, t_h)

        YBH = sb([128, 4, T], R, W0 + 48 * KB)
        YBL = sb([128, 4, T], R, W0 + 64 * KB)
        GA = [sb([128, T], F, W0 + (80 + 4 * i) * KB) for i in range(2)]
        MG = sb([128, 2, T], F, W0)
        M2 = [sb([128, 512], F, W0 + (8 + 2 * i) * KB) for i in range(2)]
        OT = sb([128, 8, D], F, W0 + 16 * KB)
        X2 = sb([128, 8, D], F, W0 + 48 * KB)
        GP = sb([128, D], F, W0 + 88 * KB)
        JK4 = sb([128, D], F, W0 + 8 * KB)
        enter_phase()
        hold[0] = False
        for q in (SP,):
            q.wait(everyone())
        t_gp = SP.dma(GP[:, :], a["g_post_2"].partition_broadcast(128), land("gp"))
        t_yb = []
        for i in range(NT):
            ps = bank(range(8))
            PE.wait(ps.free)
            for k in range(4):
                f = (lambda o, s: lambda e: e.transpose(o, s, ident))(
                    ps.ap[:, 128 * k:128 * k + 128], ZB[:, i, 128 * k:128 * k + 128])
                if k < 3:
                    PE.quiet(f)
            t = PE.do(f)
            sl = slice(128 * i, 128 * i + 128)
            pv = ps.ap.rearrange("p (k c) -> p k c", c=128)
            t_h = act(YBH[:, :, sl], pv, ACT.Copy, t)
            t_l = tt(DVE, YBL[:, :, sl], pv, YBH[:, :, sl].bitcast(F), ALU.subtract, t_h)
            ps.free = [t_h, t_l]
            t_yb += [t_h, t_l]
        t_ya = [ACTQ.last(), DVE.last()]
        gfree = [[], []]
        n_g = 0
        mfree = [[], []]
        t_mer = []
        DVE.wait(PE.last())
        for n in range(4):
            t_m1 = {}
            for br, (H, L, t_in) in enumerate(((YAH, YAL, t_ya), (YBH, YBL, t_yb))):
                with Block() as b:
                    for c in range(2):
                        z = n_g % 2
                        n_g += 1
                        ct = 2 * n + c
                        t_gl = SP.dma(GA[z][:, :], zg_d[4 + 8 * br + ct], land(f"ga{z}"), gfree[z], t_zg[4 + 8 * br + ct])
                        for half in range(2):
                            sl = slice(512 * half, 512 * half + 512)
                            ps = bank(range(8))
                            t = gemm_tr(b, 128 * c, 128 * c + 128, half, ps.ap, H, L, 4, ps.free, t_in)
                            if br == 0:
                                t = tt(DVE, MG[:, c, sl], ps.ap, GA[z][:, sl], ALU.mult, t, t_gl, t_mer[-4:])
                                ps.free = [t]
                                t_m1[c, half] = t
                            else:
                                t1 = tt(DVE, M2[half][:, :], ps.ap, GA[z][:, sl], ALU.mult, t, t_gl, mfree[half])
                                ps.free = [t1]
                                t = tt(DVE, M2[half][:, :], M2[half][:, :], MG[:, c, sl], ALU.add, t1, t_m1[c, half])
                                t_h = act(AH[:, ct, sl], M2[half][:, :], ACT.Copy, t)
                                t_l = tt(DVE, AL[:, ct, sl], M2[half][:, :], AH[:, ct, sl].bitcast(F), ALU.subtract, t_h)
                                mfree[half] = [t_h, t_l]
                                t_mer += [t_h, t_l]
                        gfree[z] = [DVE.last()]
        for q in (SP, ACTQ, DVE):
            q.wait(everyone())
        t_x2 = [SP.dma(X2[:, i, :], x2_d[128 * i:128 * i + 128, :], land(f"x{i}"), t_sp[i]) for i in range(NT)]
        t_ot = [[] for _ in range(NT)]
        for n in range(4):
            with Block() as b:
                for i in range(NT):
                    ps = bank(range(8))
                    t = gemm_nat(b, i, ps.ap[:, 0:256], AH, AL, 8, 0, 256, ps.free, t_mer)
                    t = act(OT[:, i, 256 * n:256 * n + 256], ps.ap[:, 0:256], ACT.Copy, t)
                    ps.free = [t]
                    t_ot[i].append(t)
        t_out = []
        for i in range(NT):
            t = act(JK4[:, :], OT[:, i, :], ACT.Square, t_ot[i], ACTQ.last(), accum_out=STAT[:, 24 + i:25 + i])
            t = ts(DVE, STAT[:, 32 + i:33 + i], STAT[:, 24 + i:25 + i], 1.0 / D, 1e-6, ALU.mult, ALU.add, t)
            t = rpow(STAT[:, 40 + i:41 + i], STAT[:, 32 + i:33 + i], 1, t)
            t = stt(OT[:, i, :], OT[:, i, :], STAT[:, 40 + i:41 + i], GP[:, :], ALU.mult, ALU.mult, t, t_gp)
            t = tt(DVE, OT[:, i, :], OT[:, i, :], X2[:, i, :], ALU.add, t, t_x2[i])
            t_out.append(SP.dma(out[0, 128 * i:128 * i + 128, :], OT[:, i, :], land(f"o{i}"), t))
        SP.wait(t_out)

        block = ctx.enter_context(nc.Block())

        @block.sync
        def _(e):
            SP.emit(e)

        @block.gpsimd
        def _(e):
            POOL.emit(e)

        @block.vector
        def _(e):
            DVE.emit(e)

        @block.scalar
        def _(e):
            ACTQ.emit(e)

        @block.tensor
        def _(e):
            PE.emit(e)


_INS = ["x", "norm_gain", "w_in", "q_norm_a", "k_norm_a", "na_rpb", "w_out", "final_norm_gain", "positions_2", "g_pre_2",
        "w_in_2", "b_gate_2", "mu_shift_2", "w0_2", "w_decay_up_2", "a0_2", "w_iclr_up_2", "k_k_2", "k_a_2", "r_k_2",
        "gn_gain_2", "gn_bias_2", "w_out_a_2", "g_q_2", "w_uq_2", "g_kv_2", "w_ukv_2", "w_out_b_2", "w_o_2", "g_post_2"]


def kernel(**inputs):
    import numpy as _np
    import concourse.bacc as _bacc
    from concourse import mybir as _mybir
    from concourse.bass_utils import run_bass_kernel_spmd as _run

    nc = _bacc.Bacc("TRN2", target_bir_lowering=False, num_devices=1)
    arrays, args = {}, {}
    for name in _INS:
        arrays[f"in_{name}"] = _np.ascontiguousarray(inputs[name])
    arrays["in_consts"] = constants()
    for name, v in arrays.items():
        args[name[3:]] = nc.dram_tensor(name, v.shape, _mybir.dt.from_np(v.dtype), kind="ExternalInput").ap()
    out = nc.dram_tensor("out_0", (1, T, D), F, kind="ExternalOutput").ap()
    build(nc, args, out)
    r = _run(nc, [arrays], core_ids=[0])
    return r.results[0]["out_0"]
```

```python
from contextlib import ExitStack

import numpy as np

import concourse.bass as bass
from concourse import mybir

F = mybir.dt.float32
R = mybir.dt.float32r
I32 = mybir.dt.int32
ALU = mybir.AluOpType
ACT = mybir.ActivationFunctionType
X = mybir.AxisListType.X

KB = 1024
T = 1024
D = 1024
NT = 8
NEG = -1.0e30
DECAY = 0.6065306597

C_ID, C_CAUS, C_BLK, C_BLKM, C_COL = 0, 128, 256, 384, 512
C_MD, C_MS, C_MI, C_MDT, C_MOT, C_I64, C_INV, C_ONE2 = 576, 640, 704, 768, 832, 896, 960, 976
C_END = 978
C_COS, C_SIN, C_RST = 978, 978 + 512, 978 + 1024
C_ALL = 978 + 2048

VROWS = [("pos", 8), ("norm_gain", 8), ("g_pre", 8), ("mu", 13), ("w0", 4), ("a0", 4), ("k_k", 4), ("k_a", 4),
         ("r_k", 4), ("gn_gain", 4), ("gn_bias", 4), ("g_q", 2), ("g_kv", 1), ("b_gate", 16)]
VOFF = {}
_o = 0
for _n, _c in VROWS:
    VOFF[_n] = _o
    _o += _c
VTOT = _o


def constants():
    c = np.zeros((128, C_ALL), np.float64)
    p = np.arange(128)
    c[:, C_ID:C_ID + 128] = np.eye(128)
    c[:, C_CAUS:C_CAUS + 128] = np.where(p[None, :] <= p[:, None], 0.0, NEG)
    same = (p[:, None] // 64) == (p[None, :] // 64)
    c[:, C_BLK:C_BLK + 128] = same
    c[:, C_BLKM:C_BLKM + 128] = same / 64.0
    j = np.arange(64)
    col = p % 64
    start = np.clip(col - 8, 0, 48)
    c[:, C_COL:C_COL + 64] = np.where((j[None] >= start[:, None]) & (j[None] < start[:, None] + 16), 0.0, NEG)
    s = (p % 64)[:, None]
    t = j[None]
    blk = (s // 16) == (t // 16)
    c[:, C_MD:C_MD + 64] = (s < t) & blk
    c[:, C_MS:C_MS + 64] = s < t
    c[:, C_MI:C_MI + 64] = s <= t
    c[:, C_MDT:C_MDT + 64] = (t < s) & blk
    c[:, C_MOT:C_MOT + 64] = (t < s) & ~blk
    c[:, C_I64:C_I64 + 64] = s == t
    c[:, C_INV:C_INV + 16] = (np.float32(10000.0) ** (-np.arange(0, 32, 2, dtype=np.float32) / np.float32(32)))[None]
    c[:64, C_ONE2] = 1.0
    c[64:, C_ONE2 + 1] = 1.0
    inv = np.float32(10000.0) ** (-np.arange(16, dtype=np.float32) * np.float32(2.0 / 32))
    tok = np.arange(T)
    ar = (tok // 64).astype(np.float32)[:, None] * inv[None]
    ac = (tok % 64).astype(np.float32)[:, None] * inv[None]
    ang = np.concatenate([ar, ar, ac, ac], 1).astype(np.float64)
    sign = np.where((np.arange(64) // 16) % 2 == 0, -1.0, 1.0)
    c[:, C_COS:C_COS + 512] = np.cos(ang).reshape(8, 128, 64).transpose(1, 0, 2).reshape(128, 512)
    c[:, C_SIN:C_SIN + 512] = (np.sin(ang) * sign).reshape(8, 128, 64).transpose(1, 0, 2).reshape(128, 512)
    c[:, C_RST:C_RST + 1024] = (np.arange(T) % 64 != 0)[None]
    return c.astype(np.float32)


class Queue:

    def __init__(self, sem, serial=False):
        self.sem, self.n, self.seen, self.items = sem, 0, {}, []
        self.serial = serial

    def wait(self, *tokens):
        for tok in tokens:
            if tok is None:
                continue
            if isinstance(tok, list):
                self.wait(*tok)
                continue
            sem, value = tok
            if value and self.seen.get(id(sem), 0) < value:
                self.seen[id(sem)] = value
                self.items.append(lambda e, s=sem, v=value: e.wait_ge(s, v))

    def do(self, make, *tokens):
        self.wait(*tokens)
        if self.serial:
            self.wait((self.sem, self.n))
        self.n += 1
        self.items.append(lambda e: make(e).then_inc(self.sem, 1))
        return (self.sem, self.n)

    def quiet(self, make, *tokens):
        self.wait(*tokens)
        self.items.append(make)

    def dma(self, out, in_, land, *tokens):
        self.wait(*tokens)
        land.n += 16
        self.items.append(lambda e: e.dma_start(out, in_).then_inc(land.sem, 16))
        return (land.sem, land.n)

    def last(self):
        return (self.sem, self.n)

    def emit(self, engine):
        for item in self.items:
            item(engine)


class Land:

    def __init__(self, sem):
        self.sem, self.n = sem, 0


class Place:

    def __init__(self, ap):
        self.ap, self.free = ap, []


def bc(ap, dim, n):
    shape = list(ap.shape)
    shape.insert(dim, n)
    return ap.unsqueeze(dim).to_broadcast(shape)


def build(nc, a, out):
    ctx = ExitStack()
    with ctx:
        def sem(name):
            return ctx.enter_context(nc.semaphore(name))

        BASE = nc.sbuf_base + (-nc.sbuf_base) % 32
        count = [0]

        def sb(shape, dt, offset):
            count[0] += 1
            return nc.alloc_sbuf_tensor_at(f"t{count[0]}", shape, dt, offset=BASE + offset)

        PE, ACTQ, DVE, SP = (Queue(sem(n)) for n in ("s_pe", "s_act", "s_dve", "s_sp"))
        POOL = Queue(sem("s_pool"), serial=True)
        lands = {}

        def land(name):
            if name not in lands:
                lands[name] = Land(sem("d_" + name))
            return lands[name]

        ps_all = ctx.enter_context(nc.psum_tensor("ps", [128, 4096], F))
        banks = [Place(ps_all[:, 512 * i:512 * (i + 1)]) for i in range(8)]

        RA = 0
        RW = 64 * KB
        RC = 104 * KB
        RS = 108 * KB
        W0 = 114 * KB
        AH = sb([128, 8, T], R, RA)
        AL = sb([128, 8, T], R, RA + 32 * KB)
        WST = sb([128, 2048], F, RW)
        WHI = [sb([128, 2048], R, RW + (8 + 8 * i) * KB) for i in range(2)]
        WLO = [sb([128, 2048], R, RW + (24 + 8 * i) * KB) for i in range(2)]
        CST = sb([128, C_END], F, RC)
        VT = sb([128, 128], F, RS)
        VTR = sb([128, 128], F, RS + 512)
        STAT = sb([128, 512], F, RS + 1024)
        POSI = sb([8, 128], I32, RS + 3072)
        HALF = sb([128, 128], F, RS + 3584)
        NMX = sb([128, 16], F, RS + 4096)
        RSM = sb([128, 16], F, RS + 4160)
        RIN = sb([128, 16], F, RS + 4224)
        S2 = sb([128, 2, 64], F, RS + 4288)
        PCT = sb([128, 16], F, RS + 4800)

        def cst(col, n):
            return CST[:, col:col + n]

        ident = cst(C_ID, 128)

        def vec(name, k=0, p0=0, p1=128):
            return VT[p0:p1, VOFF[name] + k:VOFF[name] + k + 1]

        def dram(name, shape):
            return nc.dram_tensor(name, shape, F, kind="Internal").ap()

        rpb_d = dram("rpb_pad", [120, 128])
        bias_d = dram("rpb_rows", [120, 64, 64])
        x2_d = dram("x2_spill", [T, D])
        feat_d = dram("feat_spill", [13, 128, T])
        zg_d = dram("zgate_spill", [20, 128, T])
        cn_d = dram("compressed_spill", [T, 416])
        zb_d = dram("zb_spill", [T, 512])
        y_d = dram("recurrence_spill", [4, 128, T])

        t_cst = POOL.dma(CST[:, :], a["consts"][:, 0:C_END], land("cst"))
        t_vrow = []
        srcs = {"norm_gain": a["norm_gain"].rearrange("a (r c) -> (a r) c", c=128)}
        for name, key in [("g_pre", "g_pre_2"), ("mu", "mu_shift_2"), ("w0", "w0_2"), ("a0", "a0_2"), ("k_k", "k_k_2"),
                          ("k_a", "k_a_2"), ("gn_gain", "gn_gain_2"), ("gn_bias", "gn_bias_2"), ("g_q", "g_q_2"),
                          ("g_kv", "g_kv_2"), ("b_gate", "b_gate_2")]:
            srcs[name] = a[key].rearrange("(r c) -> r c", c=128)
        srcs["r_k"] = a["r_k_2"].rearrange("(r h) d -> r (h d)", h=2)
        t_zero = POOL.do(lambda e: e.memset(VTR[:, :], 0.0))
        for n, (name, rows) in enumerate(VROWS[1:]):
            o = VOFF[name]
            t_vrow.append(POOL.dma(VTR[o:o + rows, :], srcs[name], land(f"v{n}"), t_zero))
        t_posi = POOL.dma(POSI[:, :], a["positions_2"].rearrange("a (r c) -> (a r) c", c=128), land("posi"))
        t_half = POOL.do(lambda e: e.memset(HALF[:, :], -0.5))
        t_pos = DVE.do(lambda e: e.tensor_copy(VTR[0:8, :], POSI[:, :]), t_posi, t_zero)
        t_vt = PE.do(lambda e: e.transpose(banks[7].ap[:, 0:128], VTR[:, :], ident), t_cst, t_vrow, t_pos)
        t_vec = DVE.do(lambda e: e.tensor_copy(VT[:, :], banks[7].ap[:, 0:128]), t_vt)
        banks[7].free = [t_vec]

        wplan = []

        def want(src, kt, cols):
            wplan.append((src, kt, cols))

        w1 = a["w_in"].rearrange("a k n -> (a k) n")
        w2 = a["w_in_2"]
        wo1 = a["w_out"].rearrange("a k n -> (a k) n")
        O1 = dict(qkv=0, ga=768, qb=1280, kb=1792, vb=2304, gb=2816)
        for c in range(0, 768, 256):
            want(w1[:, c:c + 256], 8, 256)
        for c in range(768, 1280, 256):
            want(w1[:, c:c + 256], 8, 256)
        for h in range(2):
            for s in ("qb", "kb", "vb", "gb"):
                c = O1[s] + 256 * h
                want(w1[:, c:c + 256], 8, 256)
        for c in range(0, 1024, 256):
            want(wo1[:, c:c + 256], 8, 256)
        TILES = [("f", 12), ("f", 0), ("f", 4), ("f", 8), ("f", 1), ("f", 5), ("f", 9), ("z", 0), ("f", 2), ("f", 6),
                 ("f", 10), ("z", 1), ("f", 3), ("f", 7), ("f", 11), ("z", 2), ("z", 3)] + [("g", n) for n in range(16)]
        first_col = dict(f=0, z=1664, g=3104)
        PAIRS = [TILES[n:n + 2] for n in range(0, len(TILES), 2)]
        for pair in PAIRS:
            cols = [first_col[kind] + 128 * n for kind, n in pair]
            want([w2[:, c:c + 128] for c in cols], 8, 128 * len(pair))
        want(w2[:, 2176:2432], 8, 256)
        want(w2[:, 2432:2592], 8, 160)
        for c in (2592, 2848):
            want(w2[:, c:c + 256], 8, 256)
        want(a["w_uq_2"], 2, 768)
        want(a["w_ukv_2"], 1, 1024)
        for c in range(0, 1024, 256):
            want(a["w_out_a_2"][:, c:c + 256], 4, 256)
            want(a["w_out_b_2"][:, c:c + 256], 4, 256)
        for c in range(0, 1024, 256):
            want(a["w_o_2"][:, c:c + 256], 8, 256)

        wst = Place(WST)
        wsl = [Place(None), Place(None)]
        wready = []
        wcoming = []
        wnext = [0]

        def wfetch():
            n = len(wready) + len(wcoming)
            if n >= len(wplan) or wcoming:
                return
            src, kt, cols = wplan[n]
            st = WST[:, 0:kt * cols].rearrange("p (k c) -> p k c", k=kt)
            if src is a["w_ukv_2"]:
                by_head = src.rearrange("p (h s c) -> p s h c", s=2, c=64)
                parts = [(WST[:, 512 * s:512 * s + 512].rearrange("p (h c) -> p h c", c=64), by_head[:, s]) for s in range(2)]
            elif isinstance(src, list):
                parts = [(st[:, :, 128 * m:128 * m + 128], x.rearrange("(k p) c -> p k c", p=128)) for m, x in enumerate(src)]
            else:
                parts = [(st, src.rearrange("(k p) c -> p k c", p=128))]
            for o, x in parts:
                t = SP.dma(o, x, land("w"), wst.free)
            wcoming.append([t, 0, []])

        def wsplit(last):
            if not wcoming:
                return
            t_d, done, toks = wcoming[0]
            n = len(wready)
            src, kt, cols = wplan[n]
            sl = wsl[n % 2]
            size = kt * cols
            upto = size if last else min(size, done + 512)
            if done < upto:
                part = slice(done, upto)
                t_h = ACTQ.do(lambda e: e.activation(WHI[n % 2][:, part], WST[:, part], ACT.Copy), t_d, sl.free)
                t_l = POOL.do(lambda e: e.tensor_tensor(WLO[n % 2][:, part], WST[:, part], WHI[n % 2][:, part].bitcast(F),
                                                        ALU.subtract), t_h, sl.free)
                toks += [t_h, t_l]
                wcoming[0][1] = upto
            if upto == size:
                wcoming.pop()
                wst.free = toks[-2:]
                view = lambda x: x[n % 2][:, 0:size].rearrange("p (k c) -> p k c", k=kt)
                wready.append((view(WHI), view(WLO), toks[-2:], sl))

        ticks = [0, 0]

        def wtick(products):
            ticks[0] += products
            while wcoming and ticks[0] >= 20 + 9 * ticks[1]:
                ticks[1] += 1
                wsplit(False)

        class Block:

            def __enter__(self):
                n = wnext[0]
                wnext[0] += 1
                if len(wready) <= n:
                    wfetch()
                    wsplit(True)
                wfetch()
                ticks[:] = [0, 0]
                self.hi, self.lo, self.tok, self.slot = wready[n]
                return self

            def __exit__(self, *exc):
                if len(wready) == wnext[0]:
                    wsplit(True)
                self.slot.free = [PE.last()]

        rot = [0]

        def bank(choice):
            rot[0] += 1
            return banks[choice[rot[0] % len(choice)]]

        def mm(out_ap, lhs, rhs, start, stop):
            return lambda e: e.matmul(out_ap, lhs, rhs, start=start, stop=stop)

        def product(dst, lefts, rights, *tokens):
            PE.wait(*tokens)
            n = len(lefts)
            for k in range(n):
                (lh, ll), (rh, rl) = lefts[k], rights[k]
                PE.quiet(mm(dst, lh, rh, k == 0, False))
                PE.quiet(mm(dst, lh, rl, False, False))
                last = mm(dst, ll, rh, False, k == n - 1)
                if k < n - 1:
                    PE.quiet(last)
            token = PE.do(last)
            wtick(3 * n * dst.shape[1] / 512)
            return token

        def gemm_nat(b, i, dst, act_h, act_l, kt, c0, c1, *tokens):
            sl = slice(128 * i, 128 * i + 128)
            return product(dst, [(act_h[:, k, sl], act_l[:, k, sl]) for k in range(kt)],
                           [(b.hi[:, k, c0:c1], b.lo[:, k, c0:c1]) for k in range(kt)], b.tok, *tokens)

        def gemm_tr(b, c0, c1, half, dst, act_h, act_l, kt, *tokens):
            sl = slice(512 * half, 512 * half + 512)
            return product(dst, [(b.hi[:, k, c0:c1], b.lo[:, k, c0:c1]) for k in range(kt)],
                           [(act_h[:, k, sl], act_l[:, k, sl]) for k in range(kt)], b.tok, *tokens)

        def everyone():
            return [PE.last(), ACTQ.last(), DVE.last(), POOL.last()]

        def enter_phase():
            toks = everyone()
            for q in (ACTQ, DVE, POOL, SP):
                q.wait(toks)

        def act(o, i, f, *tokens, **kw):
            return ACTQ.do(lambda e: e.activation(o, i, f, **kw), *tokens)

        def tt(q, o, x, y, op, *tokens):
            return q.do(lambda e: e.tensor_tensor(o, x, y, op), *tokens)

        def ts(q, o, x, s1, s2, op0, op1, *tokens):
            return q.do(lambda e: e.tensor_scalar(o, x, s1, s2, op0, op1) if s2 is not None
                        else e.tensor_scalar(o, x, s1, None, op0), *tokens)

        def stt(o, x, s, y, op0, op1, *tokens):
            return DVE.do(lambda e: e.scalar_tensor_tensor(out=o, in0=x, scalar=s, in1=y, op0=op0, op1=op1), *tokens)

        def cp(q, o, i, *tokens):
            return q.do(lambda e: e.tensor_copy(o, i), *tokens)

        def rpow(o, i, n, *tokens):
            return POOL.do(lambda e: e.tensor_tensor(o, i, HALF[:, 0:n], ALU.pow), t_half, *tokens)

        def split_group(ps, k, g, gain, t_ps):
            sl = slice(512 * g, 512 * g + 512)
            if gain is None:
                t_h = act(AH[:, k, sl], ps.ap, ACT.Copy, t_ps)
                t_l = tt(DVE, AL[:, k, sl], ps.ap, AH[:, k, sl].bitcast(F), ALU.subtract, t_h)
            else:
                t_h = act(AH[:, k, sl], ps.ap, ACT.Identity, t_ps, t_vec, scale=gain)
                t_l = stt(AL[:, k, sl], ps.ap, gain, AH[:, k, sl].bitcast(F), ALU.mult, ALU.subtract, t_h)
            ps.free = [t_h, t_l]
            return t_l

        def norm_transpose(src, t_src, dst, junk, gain_name):
            t_n = []
            for i in range(NT):
                t_s = act(junk, src(i), ACT.Square, t_src[i], ACTQ.last(), accum_out=STAT[:, i:i + 1])
                t_m = ts(DVE, STAT[:, 8 + i:9 + i], STAT[:, i:i + 1], 1.0 / D, 1e-6, ALU.mult, ALU.add, t_s)
                t_r = rpow(STAT[:, 16 + i:17 + i], STAT[:, 8 + i:9 + i], 1, t_m)
                t_n.append(ts(DVE, dst(i), src(i), STAT[:, 16 + i:17 + i], None, ALU.mult, None, t_r))
            t_l = None
            for g in range(2):
                for k in range(8):
                    ps = bank(range(8))
                    PE.wait(ps.free, t_n[4 * g:4 * g + 4], t_cst)
                    for i in range(4):
                        last = (lambda o, s: lambda e: e.transpose(o, s, ident))(
                            ps.ap[:, 128 * i:128 * i + 128], dst(4 * g + i)[:, 128 * k:128 * k + 128])
                        if i < 3:
                            PE.quiet(last)
                    t_ps = PE.do(last)
                    t_l = split_group(ps, k, g, vec(gain_name, k), t_ps)
            return t_l

        XS = sb([128, 8, D], F, W0)
        JUNK = sb([128, D], F, W0 + 32 * KB)
        xv = a["x"].rearrange("a (i p) c -> i p (a c)", p=128)
        t_x = [SP.dma(XS[:, i, :], xv[i], land(f"x{i}")) for i in range(NT)]
        wfetch()
        t_act = norm_transpose(lambda i: XS[:, i, :], t_x, lambda i: XS[:, i, :], JUNK[:, :], "norm_gain")

        MIXA = sb([128, 8, 512], F, W0)
        QKV = sb([128, 8, 768], F, W0 + 16 * KB)
        QT = sb([128, 4, T], R, W0 + 40 * KB)
        KT = sb([128, 2, T], R, W0 + 56 * KB)
        PB = [sb([128, T], F, W0 + (64 + 4 * i) * KB) for i in range(2)]
        PT = [sb([128, T], F, W0 + (72 + 4 * i) * KB) for i in range(2)]
        COS = sb([128, 8, 64], F, W0 + 64 * KB)
        SIN = sb([128, 8, 64], F, W0 + 66 * KB)
        GT = sb([128, 640], F, W0 + 68 * KB)
        TMP = sb([128, 640], F, W0 + 71 * KB)
        TMP2 = sb([128, 640], F, W0 + 74 * KB)
        QS = sb([128, 4, 2, 64], F, W0 + 80 * KB)
        KS = sb([128, 4, 64], F, W0 + 82 * KB)
        enter_phase()
        t_cos = SP.dma(COS[:, :, :], a["consts"][:, C_COS:C_COS + 512].rearrange("p (i c) -> p i c", c=64), land("cos"))
        t_sin = SP.dma(SIN[:, :, :], a["consts"][:, C_SIN:C_SIN + 512].rearrange("p (i c) -> p i c", c=64), land("sin"))
        t_g1 = SP.dma(GT[:, 0:64], a["q_norm_a"][0].partition_broadcast(128), land("gq"))
        t_g2 = SP.dma(GT[:, 512:576], a["k_norm_a"][0].partition_broadcast(128), land("gk"))
        t_g = ts(DVE, GT[:, 0:64], GT[:, 0:64], 0.125, None, ALU.mult, None, t_g1)
        t_ga = cp(DVE, GT[:, 64:512].rearrange("p (h c) -> p h c", c=64), bc(GT[:, 0:64], 1, 7), t_g)
        t_gb = cp(DVE, GT[:, 576:640], GT[:, 512:576], t_g2)

        t_qkv = [[] for _ in range(NT)]
        for n in range(3):
            with Block() as b:
                for i in range(NT):
                    ps = bank(range(8))
                    t = gemm_nat(b, i, ps.ap[:, 0:256], AH, AL, 8, 0, 256, ps.free, t_act)
                    t = act(QKV[:, i, 256 * n:256 * n + 256], ps.ap[:, 0:256], ACT.Copy, t)
                    ps.free = [t]
                    t_qkv[i].append(t)
        t_rope = []
        for i in range(NT):
            qk = QKV[:, i, 0:640]
            q3 = qk.rearrange("p (h c) -> p h c", c=64)
            tm = TMP[:, :]
            t = tt(DVE, tm, qk, qk, ALU.mult, t_qkv[i], t_rope[-1:])
            t = DVE.do(lambda e, i=i: e.tensor_reduce(STAT[:, 32 + 10 * i:42 + 10 * i],
                                                      TMP[:, :].rearrange("p (h c) -> p h c", c=64), X, ALU.add), t)
            t = ts(DVE, STAT[:, 112 + 10 * i:122 + 10 * i], STAT[:, 32 + 10 * i:42 + 10 * i], 1.0 / 64, 1e-6,
                   ALU.mult, ALU.add, t)
            t = rpow(STAT[:, 192 + 10 * i:202 + 10 * i], STAT[:, 112 + 10 * i:122 + 10 * i], 10, t)
            t = tt(DVE, q3, q3, bc(STAT[:, 192 + 10 * i:202 + 10 * i], 2, 64), ALU.mult, t)
            t = tt(DVE, qk, qk, GT[:, :], ALU.mult, t, t_ga, t_gb)
            t1 = tt(POOL, tm.rearrange("p (h c) -> p h c", c=64), q3, bc(COS[:, i, :], 1, 10), ALU.mult, t, t_cos)
            q5 = qk.rearrange("p (h x f c) -> p h x f c", x=2, f=2, c=16)
            s5 = bc(SIN[:, i, :], 1, 10).rearrange("p h (x f c) -> p h x f c", x=2, f=2)
            o5 = TMP2[:, :].rearrange("p (h x f c) -> p h x f c", x=2, f=2, c=16)
            ta = tt(DVE, o5[:, :, :, 0, :], q5[:, :, :, 1, :], s5[:, :, :, 0, :], ALU.mult, t, t_sin)
            tb = tt(DVE, o5[:, :, :, 1, :], q5[:, :, :, 0, :], s5[:, :, :, 1, :], ALU.mult, t, t_sin)
            t_rope.append(tt(DVE, qk, tm, TMP2[:, :], ALU.add, t1, ta, tb))

        t_gA = [[] for _ in range(NT)]
        for n in range(2):
            with Block() as b:
                for i in range(NT):
                    ps = bank(range(8))
                    t = gemm_nat(b, i, ps.ap[:, 0:256], AH, AL, 8, 0, 256, ps.free, t_act)
                    t = act(MIXA[:, i, 256 * n:256 * n + 256], ps.ap[:, 0:256], ACT.Silu, t)
                    ps.free = [t]
                    t_gA[i].append(t)

        pslot = [Place(None), Place(None)]
        seq = [0]

        def attention(items, pbuf, tbuf):
            spair = [(banks[0], banks[1]), (banks[2], banks[3])]
            tpair = (banks[4], banks[5])
            opair = [banks[6], banks[7]]
            st = []
            single = tbuf[0] is tbuf[1]
            tslot = [Place(None)] * 2 if single else [Place(None), Place(None)]

            def scores(n):
                it = items[n]
                z = seq[0] + n
                s0, s1 = spair[z % 2]
                ps = ps_all[:, 1024 * (z % 2):1024 * (z % 2) + 1024]
                t_s = it["scores"](ps, s0.free + s1.free)
                c = slice(z % 16, z % 16 + 1)
                pl = pslot[z % 2]
                src, t_m, t_free = it["stat"](ps, pbuf[z % 2], NMX[:, c], t_s, pl.free)
                w = sum(it["nk"])
                p = pbuf[z % 2][:, 0:w]
                t_e = act(p, src, ACT.Exp, t_m, pl.free, bias=NMX[:, c], scale=1.0, accum_out=RSM[:, c])
                s0.free = s1.free = [t_free if t_free is not None else t_e]
                t_r = DVE.do(lambda e: e.reciprocal(RIN[:, c], RSM[:, c]), t_e)
                st.append(dict(z=z, c=c, p=p, t_e=t_e, t_r=t_r))

            def turn(n):
                it, s = items[n], st[n]
                z = s["z"]
                PE.wait(s["t_e"], tpair[0].free, tpair[1].free)
                pt = tbuf[z % 2]
                off = 0
                toks = []
                for half in range(2):
                    ks = list(range(4 * half, min(4 * half + 4, len(it["nk"]))))
                    if not ks:
                        continue
                    b = tpair[half]
                    for k in ks:
                        w = it["nk"][k]
                        last = (lambda o, i: lambda e: e.transpose(o, i, ident))(
                            b.ap[0:w, 128 * (k % 4):128 * (k % 4) + 128], s["p"][:, 128 * k:128 * k + w])
                        if k != ks[-1]:
                            PE.quiet(last)
                    toks.append((half, ks, PE.do(last)))
                pslot[z % 2].free = [PE.last()]
                outs = []
                for half, ks, t in toks:
                    b = tpair[half]
                    full = [k for k in ks if it["nk"][k] == 128]
                    parts = []
                    if full:
                        o0 = 128 * (full[0] % 4)
                        parts.append((slice(0, 128), 128 * full[0], 128 * len(full), o0))
                    if len(full) < len(ks):
                        parts.append((slice(0, it["nk"][ks[-1]]), 128 * ks[-1], 128, 128 * (ks[-1] % 4)))
                    for pr, d0, n_, o0 in parts:
                        if half == 0:
                            t2 = cp(DVE, pt[pr, d0:d0 + n_], b.ap[pr, o0:o0 + n_], t, tslot[z % 2].free)
                        else:
                            t2 = act(pt[pr, d0:d0 + n_], b.ap[pr, o0:o0 + n_], ACT.Copy, t, tslot[z % 2].free)
                        outs.append(t2)
                    b.free = [outs[-1]] if len(parts) == 1 else outs[-2:]
                s["t_pt"] = outs

            def values(n):
                it, s = items[n], st[n]
                z = s["z"]
                ob = opair[z % 2]
                PE.wait(ob.free, s["t_pt"], it["t_v"])
                pt = tbuf[z % 2]
                nk = it["nk"]
                for k, w in enumerate(nk):
                    last = mm(ob.ap[:, 0:64], pt[0:w, 128 * k:128 * k + 128], it["v"](k)[0:w], k == 0, k == len(nk) - 1)
                    if k < len(nk) - 1:
                        PE.quiet(last)
                t_o = PE.do(last)
                tslot[z % 2].free = [t_o]
                t_f = stt(it["out"], ob.ap[:, 0:64], RIN[:, s["c"]], it["out"], ALU.mult, ALU.mult, t_o, s["t_r"], it["t_g"])
                ob.free = [t_f]
                it["done"] = t_f

            N = len(items)
            for n in range(N + 2):
                if n < N:
                    scores(n)
                if single and n >= 2:
                    values(n - 2)
                if 1 <= n <= N:
                    turn(n - 1)
                if not single and n >= 2:
                    values(n - 2)
            seq[0] += N
            for p in banks:
                p.free = p.free + [PE.last(), ACTQ.last(), DVE.last()]

        def max_stat(ps, p, nmx, t_s, free, w):
            t_m = DVE.do(lambda e: e.tensor_reduce(nmx, ps[:, 0:w], X, ALU.max, negate=True), t_s)
            return ps[:, 0:w], t_m, None

        for kv in range(2):
            t_qt, t_kt = [], []
            t_lastq = t_lastk = None
            enter_phase()
            for i in range(NT):
                q3 = QKV[:, i, 256 * kv:256 * kv + 256].rearrange("p (h c) -> p h c", c=64)
                k1 = QKV[:, i, 512 + 64 * kv:576 + 64 * kv]
                t1 = act(QS[:, :, 0, :].bitcast(R), q3, ACT.Copy, t_rope[i], t_lastq)
                t2 = tt(DVE, QS[:, :, 1, :], q3, QS[:, :, 0, :], ALU.subtract, t1)
                t3 = act(KS[:, 0:2, :].bitcast(R), bc(k1, 1, 2), ACT.Copy, t_rope[i], t_lastk)
                t4 = tt(DVE, KS[:, 2:4, :], bc(k1, 1, 2), KS[:, 0:2, :], ALU.subtract, t3)
                ps = bank(range(8))
                PE.wait(ps.free, t2)
                for h in range(4):
                    f = (lambda o, s: lambda e: e.transpose(o, s, ident))(ps.ap[:, 128 * h:128 * h + 128], QS[:, h, :, :])
                    if h < 3:
                        PE.quiet(f)
                t_p = t_lastq = PE.do(f)
                t = act(QT[:, :, 128 * i:128 * i + 128], ps.ap.rearrange("p (h c) -> p h c", c=128), ACT.Copy, t_p)
                ps.free = [t]
                t_qt.append(t)
                ps = bank(range(8))
                PE.wait(ps.free, t4)
                for h in range(2):
                    f = (lambda o, s: lambda e: e.transpose(o, s, ident))(ps.ap[:, 128 * h:128 * h + 128], KS[:, 2 * h:2 * h + 2, :])
                    if h < 1:
                        PE.quiet(f)
                t_p = t_lastk = PE.do(f)
                t = cp(DVE, KT[:, :, 128 * i:128 * i + 128], ps.ap[:, 0:256].rearrange("p (h c) -> p h c", c=128), t_p)
                ps.free = [t]
                t_kt.append(t)
            items = []
            for h in range(4):
                for i in range(NT):
                    def scores(ps, free, h=h, i=i, t_kt=t_kt, t_qt=t_qt):
                        PE.wait(free, t_qt[i], t_kt)
                        for half in range(2):
                            for n in range(2):
                                f = mm(ps[:, 512 * half:512 * half + 512], QT[:, h, 128 * i:128 * i + 128],
                                       KT[:, n, 512 * half:512 * half + 512], n == 0, n == 1)
                                if half + n < 2:
                                    PE.quiet(f)
                        return PE.do(f)

                    items.append(dict(
                        nk=[128] * 8, scores=scores,
                        stat=lambda ps, p, nmx, t_s, free: max_stat(ps, p, nmx, t_s, free, 1024),
                        v=lambda k, kv=kv: QKV[:, k, 640 + 64 * kv:704 + 64 * kv], t_v=[t_qkv[k][2] for k in range(8)],
                        out=MIXA[:, i, 64 * (4 * kv + h):64 * (4 * kv + h) + 64], t_g=t_gA[i]))
            attention(items, PB, PT)

        MIXB = sb([128, 8, 512], F, W0 + 16 * KB)
        QH = sb([128, 2, T], R, W0 + 32 * KB)
        QL = sb([128, 2, T], R, W0 + 40 * KB)
        KH = sb([128, 2, T], R, W0 + 48 * KB)
        KL = sb([128, 2, T], R, W0 + 56 * KB)
        VB = sb([128, 8, 256], F, W0 + 64 * KB)
        BI = sb([128, 4, 14, 64], F, W0 + 72 * KB)
        SBN = [sb([128, 576], F, W0 + 86 * KB + 2304 * i) for i in range(2)]
        PTN = [sb([128, 640], F, W0 + 86 * KB + 4608)] * 2
        ZERO = sb([120, 128], F, W0 + 72 * KB)

        enter_phase()
        t = POOL.do(lambda e: e.memset(ZERO[:, :], 0.0))
        t = SP.dma(rpb_d, ZERO[:, :], land("rpb"), t)
        t_pad = SP.dma(rpb_d[:, 48:79], a["na_rpb"].rearrange("a h r c -> (a h r) c"), land("rpb"), t)
        t_pad = SP.dma(bias_d, bass.AP(rpb_d.tensor, 63, [[128, 120], [-1, 64], [1, 64]]), land("rpb"), t_pad)
        for hh in range(2):
            enter_phase()
            t_b = []
            for half in range(2):
                for h in range(4):
                    first = (4 * hh + h) * 15 + (1 if half == 0 else 0)
                    src = bias_d[first:first + 14].rearrange("r c k -> c r k")
                    t_b.append(SP.dma(BI[64 * half:64 * half + 64, h, :, :], src, land(f"bi{half}{h}"), t_pad))
            t_bi = []
            for h in range(4):
                t_bi.append(tt(POOL, BI[:, h, :, :], BI[:, h, :, :], bc(cst(C_COL, 64), 1, 14), ALU.add, t_b[h], t_b[4 + h], t_cst))
            t_q, t_k = [], []
            for (hi, lo, toks, sc) in ((QH, QL, t_q, 0.125), (KH, KL, t_k, 1.0)):
                with Block() as b:
                    for c in range(2):
                        for half in range(2):
                            ps = bank(range(8))
                            t = gemm_tr(b, 128 * c, 128 * c + 128, half, ps.ap, AH, AL, 8, ps.free, t_act)
                            sl = slice(512 * half, 512 * half + 512)
                            t_h = act(hi[:, c, sl], ps.ap, ACT.Copy, t, scale=sc)
                            t_l = stt(lo[:, c, sl], ps.ap, sc, hi[:, c, sl].bitcast(F), ALU.mult, ALU.subtract, t_h)
                            ps.free = [t_h, t_l]
                            toks += [t_h, t_l]
            t_v, t_g = [], []
            with Block() as b:
                for i in range(NT):
                    ps = bank(range(8))
                    t = gemm_nat(b, i, ps.ap[:, 0:256], AH, AL, 8, 0, 256, ps.free, t_act)
                    t = act(VB[:, i, :], ps.ap[:, 0:256], ACT.Copy, t)
                    ps.free = [t]
                    t_v.append(t)
            with Block() as b:
                for i in range(NT):
                    ps = bank(range(8))
                    t = gemm_nat(b, i, ps.ap[:, 0:256], AH, AL, 8, 0, 256, ps.free, t_act)
                    t = act(MIXB[:, i, 256 * hh:256 * hh + 256], ps.ap[:, 0:256], ACT.Silu, t)
                    ps.free = [t]
                    t_g.append(t)
            for inner in range(2):
                items = []
                t_mask = []
                if inner:
                    t_all = DVE.last()
                    t_mask = [POOL.do(lambda e: e.memset(BI[64:128, :, 2, :], NEG), t_all),
                              POOL.do(lambda e: e.memset(BI[0:64, :, 10, :], NEG), t_all)]
                for h in range(4):
                    for i in ((2, 3, 4, 5) if inner else (0, 1, 6, 7)):
                        w = 576 if inner else 512
                        row0 = 2 * i - 4 if inner else (0 if i < 2 else 8)
                        k0 = 64 * row0
                        j0 = row0 - 2 * i + 6

                        def scores(ps, free, h=h, i=i, w=w, k0=k0, t_q=t_q, t_k=t_k):
                            PE.wait(free, t_q, t_k)
                            pr = slice(64 * (h % 2), 64 * (h % 2) + 64)
                            qs = slice(128 * i, 128 * i + 128)
                            c = h // 2
                            for s in range(0, w, 512):
                                n = min(512, w - s)
                                ks = slice(k0 + s, k0 + s + n)
                                o = ps[:, s:s + n]
                                PE.quiet(mm(o, QH[pr, c, qs], KH[pr, c, ks], True, False))
                                PE.quiet(mm(o, QL[pr, c, qs], KH[pr, c, ks], False, False))
                                f = mm(o, QH[pr, c, qs], KL[pr, c, ks], False, True)
                                if s + 512 < w:
                                    PE.quiet(f)
                            return PE.do(f)

                        def stat(ps, p, nmx, t_s, free, h=h, w=w, j0=j0, t_bi=t_bi, t_mask=t_mask):
                            bias = BI[:, h, j0:j0 + w // 64, :].rearrange("p r c -> p (r c)")
                            t_a = tt(DVE, p[:, 0:w], ps[:, 0:w], bias, ALU.add, t_s, free, t_bi[h], t_mask)
                            t_m = DVE.do(lambda e: e.tensor_reduce(nmx, p[:, 0:w], X, ALU.max, negate=True), t_a)
                            return p[:, 0:w], t_m, t_a

                        nk = [128] * 4 + ([64] if inner else [])
                        items.append(dict(
                            nk=nk, scores=scores, stat=stat,
                            v=lambda k, h=h, k0=k0: VB[:, k0 // 128 + k, 64 * h:64 * h + 64], t_v=t_v,
                            out=MIXB[:, i, 64 * (4 * hh + h):64 * (4 * hh + h) + 64], t_g=t_g[i]))
                attention(items, SBN, PTN)

        XR = sb([128, 8, D], F, W0 + 32 * KB)
        FG = sb([128, D], F, W0 + 64 * KB)
        JK2 = sb([128, D], F, W0 + 68 * KB)
        XN = sb([128, 8, D], F, W0)
        enter_phase()
        t_xr = [SP.dma(XR[:, i, :], xv[i], land(f"x{i}")) for i in range(NT)]
        t_fg = SP.dma(FG[:, :], a["final_norm_gain"].partition_broadcast(128), land("fg"))
        t_act = None
        for i in range(NT):
            for g in range(2):
                ps = bank(range(8))
                PE.wait(ps.free)
                src = MIXA if g == 0 else MIXB
                for k in range(4):
                    f = (lambda o, s: lambda e: e.transpose(o, s, ident))(
                        ps.ap[:, 128 * k:128 * k + 128], src[:, i, 128 * k:128 * k + 128])
                    if k < 3:
                        PE.quiet(f, DVE.last())
                t_p = PE.do(f)
                sl = slice(128 * i, 128 * i + 128)
                pv = ps.ap.rearrange("p (k c) -> p k c", c=128)
                t_h = act(AH[:, 4 * g:4 * g + 4, sl], pv, ACT.Copy, t_p)
                t_l = tt(DVE, AL[:, 4 * g:4 * g + 4, sl], pv, AH[:, 4 * g:4 * g + 4, sl].bitcast(F), ALU.subtract, t_h)
                ps.free = [t_h, t_l]
                t_act = t_l
        t_x1 = [[] for _ in range(NT)]
        for n in range(4):
            with Block() as b:
                for i in range(NT):
                    ps = bank(range(8))
                    t = gemm_nat(b, i, ps.ap[:, 0:256], AH, AL, 8, 0, 256, ps.free, t_act)
                    xs = XR[:, i, 256 * n:256 * n + 256]
                    t = tt(DVE, xs, xs, ps.ap[:, 0:256], ALU.add, t, t_xr[i])
                    ps.free = [t]
                    t_x1[i].append(t)
        t_x2, t_sp = [], []
        for i in range(NT):
            t = act(JK2[:, :], XR[:, i, :], ACT.Square, t_x1[i], ACTQ.last(), accum_out=STAT[:, 24 + i:25 + i])
            t = ts(DVE, STAT[:, 32 + i:33 + i], STAT[:, 24 + i:25 + i], 1.0 / D, 1e-6, ALU.mult, ALU.add, t)
            t = rpow(STAT[:, 40 + i:41 + i], STAT[:, 32 + i:33 + i], 1, t)
            t = stt(XR[:, i, :], XR[:, i, :], STAT[:, 40 + i:41 + i], FG[:, :], ALU.mult, ALU.mult, t, t_fg)
            t_x2.append(t)
            t_sp.append(SP.dma(x2_d[128 * i:128 * i + 128, :], XR[:, i, :], land(f"x{i}"), t))

        t_act = norm_transpose(lambda i: XR[:, i, :], t_x2, lambda i: XN[:, i, :], JK2[:, :], "g_pre")
        STG = [sb([128, T], F, W0 + 4 * i * KB) for i in range(3)]
        WA = sb([128, T], F, W0 + 12 * KB)
        LW = sb([128, 512], F, W0 + 16 * KB)
        RST = sb([128, 512], F, W0 + 18 * KB)
        KA1 = sb([128, 4], F, W0 + 20 * KB)
        CD = DECAY

        TU, CU_, MP = 256, 4, 2

        class Slot:

            def __init__(self, n, regions):
                self.n, self.regions = n, [list(r) for r in regions]
                self.FR, self.FK, self.FV = (self.buf([128, TU + 1]) for _ in range(3))
                self.AR, self.BK = self.buf([128, 2, CU_, 64]), self.buf([128, CU_, 2, 64])
                self.BON, self.YT, self.ZAT = (self.buf([128, TU]) for _ in range(3))
                self.BHN, self.KHN, self.VNN = (self.buf([128, CU_ // 2, 128]) for _ in range(3))
                self.MTS, self.GS, self.QSS, self.YL, self.DG, self.HX = (self.buf([128, CU_, 64]) for _ in range(6))
                self.GM = [self.buf([128, CU_, 64]) for _ in range(3)]
                self.ZZ = [self.buf([128, CU_, 128]) for _ in range(2)]
                self.PCT = self.buf([128, CU_])
                self.SH, self.CH = [], []
                for _ in range(7):
                    o = self.place(4 * TU)
                    self.SH.append(sb([128, TU], F, o))
                    self.CH.append(sb([128, CU_, 64], F, o))
                self.SH.append(self.buf([128, TU]))
                self.banks = banks[3 * n:3 * n + 3]
                self.turn = 0
                self.done, self.f_free, self.loads = [], [], None

            def place(self, size):
                for r in self.regions:
                    if r[1] - r[0] >= size:
                        r[0] += size
                        return r[0] - size
                raise MemoryError

            def buf(self, shape):
                size = 4 * int(np.prod(shape[1:]))
                return sb(shape, F, self.place(size + (-size) % 32))

            def bank(self):
                self.turn += 1
                return self.banks[self.turn % 3]

        slots = [Slot(n, [(W0 + (21 + 36 * n) * KB, W0 + (57 + 36 * n) * KB)]) for n in range(2)]

        enter_phase()
        for q in (ACTQ, DVE, POOL, SP):
            q.wait(t_sp)
        t_rst = SP.dma(RST[:, :], a["consts"][:, C_RST:C_RST + 512], land("rst"))
        t_lw = [SP.dma(LW[0:64, :], a["w_decay_up_2"], land("lw0")), SP.dma(LW[64:128, :], a["w_iclr_up_2"], land("lw1"))]
        t_ka = ts(DVE, KA1[:, :], VT[:, VOFF["k_a"]:VOFF["k_a"] + 4], -1.0, 1.0, ALU.mult, ALU.add, t_vec)

        def load_shifted(buf, tile, h, name, *tokens):
            if h:
                return SP.dma(buf[:, :], feat_d[tile][:, TU * h - 1:TU * h + TU], land(name), t_feat[tile], *tokens)
            return [POOL.do(lambda e: e.memset(buf[:, 0:1], 0.0), *tokens),
                    SP.dma(buf[:, 1:TU + 1], feat_d[tile][:, 0:TU], land(name), t_feat[tile], *tokens)]

        def shifted(buf, tmp, mu, *tokens):
            x = buf[:, 1:TU + 1]
            t = tt(DVE, tmp[:, :], buf[:, 0:TU], x, ALU.subtract, *tokens)
            return stt(x, tmp[:, :], mu, x, ALU.mult, ALU.add, t)

        stage = [Place(STG[i]) for i in range(3)]
        n_st = [0]
        t_feat, t_zg, t_cnd, t_zbd = [None] * 13, [None] * 20, [], []

        def product_parts(dst, lefts, rights, *tokens):
            PE.wait(*tokens)
            n = len(lefts)
            for k in range(n):
                (lh, ll), (rh, rl) = lefts[k], rights[k]
                PE.quiet(mm(dst, lh, rh, k == 0, False))
                PE.quiet(mm(dst, lh, rl, False, False))
                last = mm(dst, ll, rh, False, k == n - 1)
                wtick(3 * dst.shape[1] / 512)
                if k < n - 1:
                    PE.quiet(last)
                else:
                    dense_token[0] = PE.do(last)
                yield

        dense_token = [None]

        def next_stage():
            n_st[0] += 1
            return stage[n_st[0] % 3], land(f"stg{n_st[0] % 3}")

        def dense():
            for pair in PAIRS:
                with Block() as b:
                    for c, (kind, n) in enumerate(pair):
                        st_, ld = next_stage()
                        t_o = []
                        for half in range(2):
                            sl = slice(512 * half, 512 * half + 512)
                            cs = slice(128 * c, 128 * c + 128)
                            ps = bank((6, 7))
                            yield from product_parts(ps.ap, [(b.hi[:, k, cs], b.lo[:, k, cs]) for k in range(8)],
                                                     [(AH[:, k, sl], AL[:, k, sl]) for k in range(8)], b.tok, ps.free, t_act)
                            t, o = dense_token[0], st_.ap[:, sl]
                            t = act(o, ps.ap, ACT.Copy, t, st_.free)
                            ps.free = [t]
                            t_o.append(t)
                            yield
                        dst = feat_d[n] if kind == "f" else zg_d[n if kind == "z" else 4 + n]
                        t = SP.dma(dst, st_.ap[:, :], ld, t_o)
                        st_.free = [t]
                        if kind == "f":
                            t_feat[n] = t
                        else:
                            t_zg[n if kind == "z" else 4 + n] = t
            for dst, c0, w, toks in ((cn_d, 0, 256, t_cnd), (cn_d, 256, 160, t_cnd), (zb_d, 0, 256, t_zbd), (zb_d, 256, 256, t_zbd)):
                with Block() as b:
                    for g in range(2):
                        st_, ld = next_stage()
                        sv = st_.ap[:, 0:4 * w].rearrange("p (i c) -> p i c", i=4)
                        t_o = []
                        for i in range(4):
                            sl = slice(128 * (4 * g + i), 128 * (4 * g + i) + 128)
                            ps = bank((6, 7))
                            yield from product_parts(ps.ap[:, 0:w], [(AH[:, k, sl], AL[:, k, sl]) for k in range(8)],
                                                     [(b.hi[:, k, 0:w], b.lo[:, k, 0:w]) for k in range(8)], b.tok, ps.free, t_act)
                            t = act(sv[:, i, :], ps.ap[:, 0:w], ACT.Copy, dense_token[0], st_.free)
                            ps.free = [t]
                            t_o.append(t)
                        t = SP.dma(dst[512 * g:512 * g + 512, c0:c0 + w].rearrange("(i p) c -> p i c", p=128), sv, ld, t_o)
                        st_.free = [t]
                        toks.append(t)

        filler = dense()
        credit = [0.0]

        def fill(us):
            credit[0] += us
            while credit[0] > 0.6:
                credit[0] -= 0.64
                next(filler, None)

        def need(table, n):
            while table[n] is None:
                next(filler)

        for n in (12, 0, 4, 8):
            need(t_feat, n)

        t_wa = []
        for h in range(T // TU):
            S = slots[h % 2]
            t = load_shifted(S.FR, 12, h, f"fr{S.n}", S.f_free)
            t = shifted(S.FR, S.SH[7], vec("mu", 12), t, t_vec, DVE.last())
            sl = slice(TU * h, TU * h + TU)
            t_wa.append([act(WA[0:64, sl], S.FR[0:64, 1:TU + 1], ACT.Tanh, t),
                         cp(DVE, WA[64:128, sl], S.FR[64:128, 1:TU + 1], t)])
            S.f_free = t_wa[h]
            fill(1.3)

        ch3 = lambda t_: t_.rearrange("p (c t) -> p c t", t=64)

        def mask(col, n):
            return bc(cst(col, 64), 1, n)

        def load_unit(S, j, h):
            for s in range(3):
                need(t_feat, 4 * s + j)
            S.loads = [load_shifted(b_, 4 * s + j, h, f"{n_}{S.n}", S.f_free)
                       for s, (b_, n_) in enumerate(((S.FR, "fr"), (S.FK, "fk"), (S.FV, "fv")))]

        STAGE, NAT, INV, CHAIN, NORM, OFFSET = 0.7, 0.7, 0.7, 0.7, 0.7, 18

        def head_scale(S, sq, t_sq, c0, mul, add, floor):
            ps = S.bank()
            PE.wait(ps.free, t_sq)
            for m in range(MP):
                f = mm(ps.ap[:, 2 * m:2 * m + 2], sq[:, 128 * m:128 * m + 128], cst(C_ONE2, 2), True, True)
                if m < MP - 1:
                    PE.quiet(f)
            t = PE.do(f)
            s0, s1 = STAT[:, c0:c0 + CU_], STAT[:, c0 + 8:c0 + 8 + CU_]
            if floor is None:
                t = ts(DVE, s0, ps.ap[:, 0:CU_], mul, add, ALU.mult, ALU.add, t)
            else:
                t = ts(DVE, s0, ps.ap[:, 0:CU_], floor, None, ALU.max, None, t)
            ps.free = [t]
            t = rpow(s1, s0, CU_, t)
            t = cp(POOL, S.HX[:, :, :], bc(s1, 2, 64), t, S.hx_free)
            yield STAGE
            ps = S.bank()
            PE.wait(t, ps.free)
            for m in range(MP):
                l = S.HX[:, 2 * m:2 * m + 2, :].rearrange("p h c -> p (h c)")
                f = mm(ps.ap[:, 128 * m:128 * m + 128], l, ident, True, True)
                if m < MP - 1:
                    PE.quiet(f)
            S.scale = ps, PE.do(f)
            S.hx_free = [S.scale[1]]

        class Chain:
            units, state, read = 0, None, [None, None]

        chain = Chain()
        S2 = sb([128, 2, 64], F, W0 + 20 * KB + 512)

        def unit(S, j, h, following):
            sl = slice(TU * h, TU * h + TU)
            SG, AI, CU, E1, E2, E3, KK, TM = S.SH
            AR, BK, BON, YT, ZAT = S.AR, S.BK, S.BON, S.YT, S.ZAT
            BHN, KHN, VNN, MTS, GS, QSS, YL, DG, PCT = S.BHN, S.KHN, S.VNN, S.MTS, S.GS, S.QSS, S.YL, S.DG, S.PCT
            ARB, AKT, RKT = S.GM
            ND, NDT, NOT, B3, B4, B5, B6 = S.CH
            ZA_, ZB_ = S.ZZ
            if S.loads is None:
                load_unit(S, j, h)
            t_in, S.loads = S.loads, None
            done = S.done
            for q in (ACTQ, DVE, POOL):
                q.wait(done)
            r_, k_, v_ = (b_[:, 1:TU + 1] for b_ in (S.FR, S.FK, S.FV))
            tk = []
            for p0, dst, bias in ((0, SG, "w0"), (64, AI, "a0")):
                ps = S.bank()
                pv = ps.ap[:, 0:TU]
                t = PE.do(mm(pv, LW[p0:p0 + 64, 128 * j:128 * j + 128], WA[p0:p0 + 64, sl], True, True), ps.free, t_lw, t_wa[h])
                t = act(dst[:, :], pv, ACT.Sigmoid, t, t_vec, bias=vec(bias, j))
                ps.free = [t]
                tk.append(t)
            t_s, t_ai = tk
            t_k1 = shifted(S.FK, TM, vec("mu", 4 + j), t_in[1])
            t_kk = ts(DVE, KK[:, :], k_, vec("k_k", j), None, ALU.mult, None, t_k1)
            t_sq = act(E2[:, :], KK[:, :], ACT.Square, t_kk)
            yield STAGE
            t_cu = DVE.do(lambda e: e.tensor_tensor_scan(CU[:, :], RST[:, 0:TU], SG[:, :], 0.0, ALU.mult, ALU.add), t_s, t_rst)
            t_e1 = act(E1[:, :], CU[:, :], ACT.Exp, t_cu, scale=-CD)
            t_e3 = act(E3[:, :], CU[:, :], ACT.Exp, t_cu, scale=CD)
            t_r1 = shifted(S.FR, TM, vec("mu", j), t_in[0], t_k1)
            yield STAGE
            yield from head_scale(S, E2, t_sq, 256 + 64 * S.n, None, None, 1e-24)
            ps, t_hs = S.scale
            t_v1 = shifted(S.FV, TM, vec("mu", 8 + j), t_in[2], t_r1)
            t_pc = cp(DVE, PCT[:, :], ch3(E1[:, :])[:, :, 63], t_e1)
            t_a1 = tt(POOL, AR[:, 1], ch3(r_), ch3(E1[:, :]), ALU.mult, t_e1, t_r1)
            yield STAGE
            t_tm = tt(DVE, TM[:, :], CU[:, :], SG[:, :], ALU.subtract, t_cu, t_v1)
            t_kn = tt(DVE, KK[:, :], KK[:, :], ps.ap[:, 0:TU], ALU.mult, t_hs, t_sq)
            ps.free = [t_kn]
            t_e2 = act(E2[:, :], TM[:, :], ACT.Exp, t_tm, t_hs, scale=-CD)
            yield STAGE
            t_a0 = stt(AR[:, 0], ch3(KK[:, :]), -1.0, ch3(E2[:, :]), ALU.mult, ALU.mult, t_e2, t_kn)
            t = ts(DVE, TM[:, :], AI[:, :], vec("k_a", j), KA1[:, j:j + 1], ALU.mult, ALU.add, t_ai, t_ka, t_e2)
            t_kf = tt(DVE, k_, k_, TM[:, :], ALU.mult, t, t_kk)
            yield STAGE
            t_b = tt(DVE, TM[:, :], KK[:, :], AI[:, :], ALU.mult, t_kf, t_kn)
            t_b1 = tt(DVE, BK[:, :, 1, :], ch3(k_), ch3(E3[:, :]), ALU.mult, t_kf, t_e3)
            t_b0 = tt(DVE, BK[:, :, 0, :], ch3(TM[:, :]), ch3(E3[:, :]), ALU.mult, t_b, t_e3)
            t_dg = tt(POOL, DG[:, :, :], mask(C_I64, CU_), bc(PCT[:, :], 2, 64), ALU.mult, t_pc)
            yield STAGE
            t_bo = stt(TM[:, :], r_, vec("r_k", j), k_, ALU.mult, ALU.mult, t_b0, t_r1, t_kf)
            t_bh = tt(DVE, ch3(CU[:, :]), BK[:, :, 0, :], bc(PCT[:, :], 2, 64), ALU.mult, t_b0, t_pc, t_e1, t_e3, t_tm)
            t_kh = tt(DVE, ch3(SG[:, :]), BK[:, :, 1, :], bc(PCT[:, :], 2, 64), ALU.mult, t_b1, t_tm)
            t_nat = dict(a=[], b=[], k=[], v=[])

            def turned(name, src, t_src):
                ps = S.bank()
                PE.wait(ps.free, t_src)
                for m in range(MP):
                    s = AR[:, 0, 2 * m:2 * m + 2, :].rearrange("p c t -> p (c t)") if name == "a" else src[:, 128 * m:128 * m + 128]
                    f = (lambda o, s_: lambda e: e.transpose(o, s_, ident))(ps.ap[:, 128 * m:128 * m + 128], s)
                    if m < MP - 1:
                        PE.quiet(f)
                t = PE.do(f)
                pv = ps.ap[:, 0:TU].rearrange("p (m c) -> p m c", c=128)
                if name == "a":
                    for e in range(2):
                        t_nat["a"].append(act(ZA_[:, MP * e:MP * e + MP, 0:64], pv[:, :, 64 * e:64 * e + 64], ACT.Copy, t))
                else:
                    t_nat[name].append(act({"b": BHN, "k": KHN, "v": VNN}[name][:, :, :], pv, ACT.Copy, t))
                ps.free = t_nat[name][-1:]

            turned("a", None, t_a0)
            turned("v", v_, t_v1)
            yield NAT
            turned("b", CU, t_bh)
            turned("k", SG, t_kh)
            yield NAT
            ps = S.bank()
            t = PE.do(mm(ps.ap[:, 0:TU], cst(C_BLK, 128), TM[:, :], True, True), t_bo, ps.free)
            t_p = tt(DVE, BON[:, :], v_, ps.ap[:, 0:TU], ALU.mult, t, t_v1)
            ps.free = [t_p]
            t_ar, t_bk = [t_a0, t_a1], [t_b0, t_b1]
            stage1 = [t_p, t_dg, t_pc, t_nat["a"], t_nat["b"], t_nat["k"], t_nat["v"]]
            S.f_free = stage1 + [t_kf]
            if following:
                load_unit(S, *following)
            yield NAT

            def grams(n, left, right):
                ps = [S.bank(), S.bank()]
                PE.wait(ps[0].free, ps[1].free, t_ar, t_bk)
                for m in range(MP):
                    for e, q in ((0, 0), (1, 1), (0, 1), (1, 0)):
                        pr = slice(64 * e, 64 * e + 64)
                        f = mm(ps[e].ap[64 * q:64 * q + 64, n * m:n * m + n], left(pr, 2 * m + q), right(pr, 2 * m + q), True, True)
                        if m < MP - 1 or (e, q) != (1, 0):
                            PE.quiet(f)
                return ps, PE.do(f)

            tg = {x: [] for x in ("nd", "arb", "akt", "rkt", "ndt", "not")}
            for s, d0, d1, n0, n1, k0 in ((0, ND, ARB, "nd", "arb", C_MD), (1, AKT, RKT, "akt", "rkt", C_MS)):
                pss, t = grams(128, lambda pr, c, s=s: BK[pr, c, s, :], lambda pr, c: AR[pr, :, c, :])
                for e in range(2):
                    gs = slice(MP * e, MP * e + MP)
                    pv = pss[e].ap[:, 0:TU].rearrange("p (m s c) -> p m s c", s=2, c=64)
                    tg[n0].append(tt(DVE, d0[:, gs, :], pv[:, :, 0, :], mask(k0, MP), ALU.mult, t, stage1))
                    tg[n1].append(tt(DVE, d1[:, gs, :], pv[:, :, 1, :], mask(C_MI, MP), ALU.mult, t, stage1))
                    pss[e].free = [tg[n1][-1]]
                if s == 0:
                    pss, t = grams(64, lambda pr, c: AR[pr, 0, c, :], lambda pr, c: BK[pr, c, 0, :])
                    for e in range(2):
                        gs = slice(MP * e, MP * e + MP)
                        pv = pss[e].ap[:, 0:64 * MP].rearrange("p (m c) -> p m c", c=64)
                        tg["ndt"].append(tt(DVE, NDT[:, gs, :], pv, mask(C_MDT, MP), ALU.mult, t))
                        tg["not"].append(tt(DVE, NOT[:, gs, :], pv, mask(C_MOT, MP), ALU.mult, t))
                        pss[e].free = [tg["not"][-1]]
                yield INV
            t_d1 = tt(POOL, B5[:, :, :], ND[:, :, :], mask(C_I64, CU_), ALU.add, tg["nd"], stage1)

            def blocks(lhs, rhs, *tokens, n=64):
                ps = S.bank()
                PE.wait(ps.free, *tokens)
                for x in range(CU_):
                    for q in range(2):
                        pq = slice(64 * q, 64 * q + 64)
                        f = mm(ps.ap[pq, n * x:n * x + n], lhs(pq, x), rhs(pq, x), True, True)
                        if not (q and x == CU_ - 1):
                            PE.quiet(f)
                return ps, ps.ap[:, 0:n * CU_].rearrange("p (x c) -> p x c", x=CU_), PE.do(f)

            def whole(buf):
                return lambda pq, x: buf[pq, x, :]

            def take(q, dst, r, add=None, *tokens):
                ps, pv, t = r
                if add is not None:
                    t = tt(DVE, dst, pv, add, ALU.add, t, *tokens)
                elif q is ACTQ:
                    t = act(dst, pv, ACT.Copy, t, *tokens)
                else:
                    t = cp(DVE, dst, pv, t, *tokens)
                ps.free = [t]
                return t

            ACTQ.wait(stage1)
            t_n2 = take(ACTQ, B3[:, :, :], blocks(whole(NDT), whole(ND), tg["nd"], tg["ndt"]))
            t_n2t = take(DVE, B4[:, :, :], blocks(whole(ND), whole(NDT)))
            yield INV
            t_x = take(ACTQ, ZA_[:, :, 64:128], blocks(whole(AKT), lambda pq, x: VNN[pq, x % MP, 64 * (x // MP):64 * (x // MP) + 64],
                                                       tg["akt"], t_nat["v"]))
            yield INV
            r4 = blocks(whole(B4), whole(B3), t_n2, t_n2t)
            r4t = blocks(whole(B3), whole(B4))
            t_n4 = take(ACTQ, ND[:, :, :], r4, None, t_d1, r4t[2])
            t_n4t = take(DVE, NDT[:, :, :], r4t)
            yield INV
            t_d2 = take(DVE, B6[:, :, :], blocks(whole(B4), whole(B5), t_d1), B5[:, :, :])
            yield INV
            t_n8t = take(ACTQ, B3[:, :, :], blocks(whole(ND), whole(NDT), t_n4, t_n4t))
            yield INV
            t_d3 = take(DVE, B5[:, :, :], blocks(whole(NDT), whole(B6), t_d2), B6[:, :, :])
            yield INV
            t_d4 = take(DVE, B6[:, :, :], blocks(whole(B3), whole(B5), t_n8t, t_d3), B5[:, :, :])
            yield INV
            t_f = take(ACTQ, B4[:, :, :], blocks(whole(NOT), whole(B6), t_d4, tg["not"]))
            t_z = take(DVE, ZB_[:, :, :], blocks(whole(B6), whole(ZA_), t_x, t_nat["a"], n=128))
            yield INV
            for it in range(3):
                t_z = take(DVE, ZA_[:, :, :], blocks(whole(B4), whole(ZB_ if it == 0 else ZA_), t_f, t_z, n=128), ZB_[:, :, :])
                yield INV

            W_ = lambda e, pq, m: ZA_[pq, MP * e + m, 0:64]
            U_ = lambda e, pq, m: ZA_[pq, MP * e + m, 64:128]
            H_ = lambda buf: (lambda e, pq, m: buf[pq, m, 64 * e:64 * e + 64])
            G_ = lambda buf: (lambda e, pq, m: buf[pq, MP * e + m, :])
            plans = [("mt", [(W_, H_(BHN))]), ("g", [(H_(BHN), U_), (H_(KHN), H_(VNN))]), ("q", [(W_, G_(ARB))]),
                     ("y", [(U_, G_(ARB)), (H_(VNN), G_(RKT))])]
            t_out = {}
            for name, terms in plans:
                t_out[name] = []
                ps = [S.bank(), S.bank()]
                PE.wait(ps[0].free, ps[1].free, t_z, t_nat["b"], t_nat["k"], tg["arb"], tg["rkt"])
                for m in range(MP):
                    for pairs in (((0, 0), (1, 1)), ((0, 1), (1, 0))):
                        for x, (l, r) in enumerate(terms):
                            for e, q in pairs:
                                pq = slice(64 * q, 64 * q + 64)
                                f = mm(ps[q].ap[64 * e:64 * e + 64, 64 * m:64 * m + 64], l(e, pq, m), r(e, pq, m),
                                       x == 0, x == len(terms) - 1)
                                if not (m == MP - 1 and (e, q) == (1, 0) and x == len(terms) - 1):
                                    PE.quiet(f)
                t = PE.do(f)
                for q in range(2):
                    pv = ps[q].ap[:, 0:64 * MP].rearrange("p (m c) -> p m c", c=64)
                    view = lambda b_: b_[:, :, :].rearrange("p (m q) c -> p m q c", q=2)[:, :, q, :]
                    if name == "mt":
                        t2 = tt(DVE, view(MTS), pv, view(DG), ALU.add, t, t_dg)
                    elif name == "q":
                        t2 = tt(DVE, view(QSS), pv, AR[:, 1].rearrange("p (m q) c -> p m q c", q=2)[:, :, q, :], ALU.add, t, t_a1)
                    else:
                        t2 = act(view(GS if name == "g" else YL), pv, ACT.Copy, t)
                    ps[q].free = [t2]
                    t_out[name].append(t2)
                yield INV

            need(t_zg, j)
            t_za = SP.dma(ZAT[:, :], zg_d[j][:, sl], land(f"za{S.n}"), t_zg[j], done)
            t_za = act(ZAT[:, :], ZAT[:, :], ACT.Silu, t_za)
            index = j * (T // TU) + h
            while chain.units < index:
                yield 0
            if h == 0:
                chain.state = POOL.do(lambda e: e.memset(S2[:, 0, :], 0.0), chain.state, chain.read)
            yb = S.banks[2]
            PE.wait(yb.free)
            for c in range(CU_):
                cur, nxt = c % 2, (c + 1) % 2
                final = h == T // TU - 1 and c == CU_ - 1
                PE.wait(chain.state, t_out["q"], t_out["mt"])
                if not final:
                    sp = S.banks[c % 2]
                    PE.wait(sp.free)
                    PE.quiet(mm(sp.ap[0:64, 0:64], MTS[0:64, c, :], S2[0:64, cur, :], True, True))
                    t_sp_ = PE.do(mm(sp.ap[64:128, 0:64], MTS[64:128, c, :], S2[64:128, cur, :], True, True))
                    chain.state = tt(DVE, S2[:, nxt, :], sp.ap[:, 0:64], GS[:, c, :], ALU.add, t_sp_, t_out["g"], chain.read[nxt])
                    sp.free = [chain.state]
                PE.quiet(mm(yb.ap[0:64, 64 * c:64 * c + 64], S2[0:64, cur, :], QSS[0:64, c, :], True, True))
                chain.read[cur] = t_y = PE.do(mm(yb.ap[64:128, 64 * c:64 * c + 64], S2[64:128, cur, :], QSS[64:128, c, :], True, True))
                if c == CU_ - 1:
                    chain.units += 1
                yield CHAIN
            t = tt(DVE, YT[:, :], yb.ap[:, 0:TU], YL[:, :, :].rearrange("p c t -> p (c t)"), ALU.add, t_y, t_out["y"], S.y_free)
            yb.free = [t]
            ps = S.bank()
            t = PE.do(mm(ps.ap[:, 0:TU], cst(C_BLKM, 128), YT[:, :], True, True), t, ps.free)
            t_yc = tt(DVE, YT[:, :], YT[:, :], ps.ap[:, 0:TU], ALU.subtract, t)
            ps.free = [t_yc]
            yield NORM
            t_sq = act(E1[:, :], YT[:, :], ACT.Square, t_yc, t_z)
            yield from head_scale(S, E1, t_sq, 288 + 64 * S.n, 1.0 / 64, 64e-5, None)
            ps, t_hs = S.scale
            t = tt(DVE, YT[:, :], YT[:, :], ps.ap[:, 0:TU], ALU.mult, t_hs, t_sq)
            ps.free = [t]
            t = ts(DVE, YT[:, :], YT[:, :], vec("gn_gain", j), vec("gn_bias", j), ALU.mult, ALU.add, t)
            t = tt(DVE, YT[:, :], YT[:, :], BON[:, :], ALU.add, t, t_p)
            yield NORM
            t = tt(DVE, YT[:, :], YT[:, :], ZAT[:, :], ALU.mult, t, t_za)
            t_o = SP.dma(y_d[j][:, sl], YT[:, :], land(f"y{S.n}"), t)
            t_yd.append(t_o)
            S.done = [t, t_out["q"], t_out["mt"], t_out["g"], t_out["y"], t_y]
            S.y_free = [t_o]
            yield NORM

        t_yd = []
        order = [(j, h) for j in range(4) for h in range(T // TU)]

        def flow(n):
            mine = order[n::2]
            S = slots[n]
            S.hx_free, S.y_free = [], []
            for x, (j, h) in enumerate(mine):
                yield from unit(S, j, h, mine[x + 1] if x + 1 < len(mine) else None)

        flows = [flow(0), flow(1)]
        for _ in range(OFFSET):
            fill(next(flows[0]))
        while flows:
            for f in list(flows):
                us = next(f, None)
                if us is None:
                    flows.remove(f)
                else:
                    fill(us)
        for _ in filler:
            pass

        ZB = sb([128, 8, 512], F, W0)
        CN = sb([128, 8, 416], F, W0 + 16 * KB)
        RT = sb([128, 2, 8, 2, 16], F, W0 + 29 * KB)
        CTH = sb([128, 3, T], R, W0 + 31 * KB)
        CTL = sb([128, 3, T], R, W0 + 43 * KB)
        VN = sb([128, 8, 512], F, W0 + 55 * KB)
        QN = [sb([128, 768], F, W0 + (71 + 3 * i) * KB) for i in range(2)]
        PM = [sb([128, T], F, W0 + (77 + 4 * i) * KB) for i in range(2)]
        PTM = [sb([128, T], F, W0 + (85 + 4 * i) * KB) for i in range(2)]
        TAB = [sb([128, 8, 16], F, W0 + 77 * KB + 512 * i) for i in range(5)]
        JK3 = sb([128, 256], F, W0 + 85 * KB)
        QTM = sb([96, 8, T], F, RA)
        KTM = sb([96, 8, T], F, RA + 32 * KB)
        YAH = sb([128, 4, T], R, W0 + 16 * KB)
        YAL = sb([128, 4, T], R, W0 + 32 * KB)
        YS = sb([128, T], F, W0 + 48 * KB)
        enter_phase()
        SP.wait(t_yd)
        t_cl = SP.dma(CN[:, :, :], cn_d.rearrange("(i p) c -> p i c", p=128), land("cn"), t_cnd)
        t_zl = SP.dma(ZB[:, :, :], zb_d.rearrange("(i p) c -> p i c", p=128), land("zb"), t_zbd)
        t_c = [[t_cl, t_cl] for _ in range(NT)]
        t_zb = [act(ZB[:, i, :], ZB[:, i, :], ACT.Silu, t_zl) for i in range(NT)]

        t_st = []
        for i in range(NT):
            t_st.append(act(JK3[:, :], CN[:, i, 0:256], ACT.Square, t_c[i], ACTQ.last(), accum_out=STAT[:, 64 + 2 * i:65 + 2 * i]))
            t_st.append(act(JK3[:, 0:128], CN[:, i, 256:384], ACT.Square, ACTQ.last(), accum_out=STAT[:, 65 + 2 * i:66 + 2 * i]))
        s_in = STAT[:, 64:80].rearrange("p (i s) -> p s i", s=2)
        s_ms = STAT[:, 80:96].rearrange("p (i s) -> p s i", s=2)
        t_m = [ts(DVE, s_ms[:, s, :], s_in[:, s, :], 1.0 / n, 1e-6, ALU.mult, ALU.add, t_st) for s, n in ((0, 256), (1, 128))]
        t_r = rpow(STAT[:, 96:112], STAT[:, 80:96], 16, t_m)
        t_cn = []
        for i in range(NT):
            t1 = ts(DVE, CN[:, i, 0:256], CN[:, i, 0:256], STAT[:, 96 + 2 * i:97 + 2 * i], None, ALU.mult, None, t_r)
            t2 = ts(DVE, CN[:, i, 256:384], CN[:, i, 256:384], STAT[:, 97 + 2 * i:98 + 2 * i], None, ALU.mult, None, t_r)
            t_cn.append([t1, t2])

        ang, sinT, cosT, yy, nn = (TAB[i][:, :, :] for i in range(5))
        MAGIC = 12582912.0
        two_pi = 2.0 * np.pi
        c1 = 6.28125
        c2 = float((np.float32(two_pi - c1).view(np.uint32) & np.uint32(0xFFFFF000)).view(np.float32))
        c3 = float(two_pi - c1 - c2)
        t_a = tt(DVE, ang, bc(VT[:, 0:8], 2, 16), bc(cst(C_INV, 16), 1, 8), ALU.mult, t_vec)
        t_tab = []
        for dst, turn_, add in ((sinT, 0.0, 0.0), (cosT, 0.25, float(np.pi / 2))):
            t = ts(DVE, yy, ang, 1.0 / two_pi, turn_, ALU.mult, ALU.add, t_a, t_tab)
            t = ts(DVE, nn, yy, MAGIC, None, ALU.add, None, t)
            t = ts(DVE, yy, nn, -MAGIC, None, ALU.add, None, t)
            f2 = lambda ap: ap.rearrange("p i c -> p (i c)")
            t = stt(f2(dst), f2(yy), -c1, f2(ang), ALU.mult, ALU.add, t)
            t = stt(f2(dst), f2(yy), -c2, f2(dst), ALU.mult, ALU.add, t)
            t = stt(f2(dst), f2(yy), -c3, f2(dst), ALU.mult, ALU.add, t)
            t = ts(DVE, dst, dst, add, None, ALU.add, None, t)
            t = ts(DVE, dst, dst, 3.1415925, -3.1415925, ALU.min, ALU.max, t)
            t_tab = [act(dst, dst, ACT.Sin, t)] + t_tab
        kp = CN[:, :, 384:416].rearrange("p i (f c) -> p i f c", f=2)
        RA_, RB_ = RT[:, 0], RT[:, 1]

        def rotate(x4, cos, sin, *tokens):
            t1 = tt(DVE, RA_, x4, bc(cos, 2, 2), ALU.mult, DVE.last(), *tokens)
            t2 = tt(DVE, RB_[:, :, 0, :], x4[:, :, 1, :], sin, ALU.mult, DVE.last(), *tokens)
            t3 = tt(DVE, RB_[:, :, 1, :], x4[:, :, 0, :], sin, ALU.mult, DVE.last(), *tokens)
            t4 = tt(DVE, x4[:, :, 0, :], RA_[:, :, 0, :], RB_[:, :, 0, :], ALU.subtract, t1, t2, t3)
            return tt(DVE, x4[:, :, 1, :], RA_[:, :, 1, :], RB_[:, :, 1, :], ALU.add, t4)

        t_kp = rotate(kp, cosT, sinT, t_tab, *[t_c[i][1] for i in range(NT)])

        t_ct = [[], []]
        for k in range(3):
            gain = vec("g_q", k) if k < 2 else vec("g_kv")
            for g in range(2):
                ps = bank(range(8))
                PE.wait(ps.free, t_cn[4 * g:4 * g + 4])
                for i in range(4):
                    f = (lambda o, s: lambda e: e.transpose(o, s, ident))(
                        ps.ap[:, 128 * i:128 * i + 128], CN[:, 4 * g + i, 128 * k:128 * k + 128])
                    if i < 3:
                        PE.quiet(f)
                t = PE.do(f)
                sl = slice(512 * g, 512 * g + 512)
                t_h = act(CTH[:, k, sl], ps.ap, ACT.Identity, t, t_vec, scale=gain)
                t_l = stt(CTL[:, k, sl], ps.ap, gain, CTH[:, k, sl].bitcast(F), ALU.mult, ALU.subtract, t_h)
                ps.free = [t_h, t_l]
                t_ct[g] += [t_h, t_l]
        enter_phase()
        t_q = [[] for _ in range(NT)]
        qfree = [[], []]
        with Block() as b:
            for i in range(NT):
                z = i % 2
                sl = slice(128 * i, 128 * i + 128)
                t_e = []
                for g in range(2):
                    ps = bank(range(8))
                    t = product(ps.ap[:, 0:384], [(CTH[:, k, sl], CTL[:, k, sl]) for k in range(2)],
                                [(b.hi[:, k, 384 * g:384 * g + 384], b.lo[:, k, 384 * g:384 * g + 384]) for k in range(2)],
                                b.tok, ps.free, t_ct[i // 4])
                    t = act(QN[z][:, 384 * g:384 * g + 384], ps.ap[:, 0:384], ACT.Copy, t, qfree[z], scale=96.0 ** -0.5)
                    ps.free = [t]
                    t_e.append(t)
                pe4 = QN[z][:, :].rearrange("p (h c) -> p h c", c=96)[:, :, 64:96].rearrange("p h (f c) -> p h f c", f=2)
                t_rot = rotate(pe4, bc(cosT[:, i, :], 1, 8), bc(sinT[:, i, :], 1, 8), t_tab, t_e)
                for g in range(2):
                    ps = bank(range(8))
                    PE.wait(ps.free, t_rot)
                    for h in range(4):
                        f = (lambda o, s: lambda e: e.transpose(o, s, ident))(
                            ps.ap[0:96, 128 * h:128 * h + 128], QN[z][:, 96 * (4 * g + h):96 * (4 * g + h) + 96])
                        if h < 3:
                            PE.quiet(f)
                    t = PE.do(f)
                    o = QTM[:, 4 * g:4 * g + 4, sl]
                    pv = ps.ap[0:96, :].rearrange("p (h c) -> p h c", c=128)
                    t = act(o, pv, ACT.Copy, t) if g else cp(DVE, o, pv, t)
                    ps.free = [t]
                    t_q[i].append(t)
                qfree[z] = [PE.last()]
        t_k, t_v = [], []
        with Block() as b:
            kh_, kl_, vh_, vl_ = (x[:, 0, o:o + 512] for o in (0, 512) for x in (b.hi, b.lo))
            for i in range(NT):
                sl = slice(128 * i, 128 * i + 128)
                ps = bank(range(8))
                t = product(ps.ap, [(CTH[:, 2, sl], CTL[:, 2, sl])], [(vh_, vl_)],
                            b.tok, ps.free, t_ct[i // 4])
                t = act(VN[:, i, :], ps.ap, ACT.Copy, t)
                ps.free = [t]
                t_v.append(t)
            for j in range(4):
                for half in range(2):
                    sl = slice(512 * half, 512 * half + 512)
                    ps = bank(range(8))
                    t = product(ps.ap, [(kh_[:, 128 * j:128 * j + 128], kl_[:, 128 * j:128 * j + 128])],
                                [(CTH[:, 2, sl], CTL[:, 2, sl])], b.tok, ps.free, t_ct[half])
                    t1 = cp(DVE, KTM[0:64, 2 * j, sl], ps.ap[0:64, :], t)
                    t2 = act(KTM[0:64, 2 * j + 1, sl], ps.ap[64:128, :], ACT.Copy, t, t1)
                    ps.free = [t1, t2]
                    t_k += [t1, t2]
        for half in range(2):
            sl = slice(512 * half, 512 * half + 512)
            ps = bank(range(8))
            PE.wait(ps.free, t_kp)
            for i in range(4):
                f = (lambda o, s: lambda e: e.transpose(o, s, ident))(
                    ps.ap[0:32, 128 * i:128 * i + 128], CN[:, 4 * half + i, 384:416])
                if i < 3:
                    PE.quiet(f)
            t = PE.do(f)
            for h in range(0, 8, 2):
                t_k.append(cp(DVE, KTM[64:96, h, sl], ps.ap[0:32, :], t))
            t = [t, DVE.last()]
            for h in range(1, 8, 2):
                t_k.append(act(KTM[64:96, h, sl], ps.ap[0:32, :], ACT.Copy, t))
            ps.free = [DVE.last(), ACTQ.last()]

        enter_phase()
        ys_free, t_ya = [], []
        for j in range(4):
            t = SP.dma(YS[:, :], y_d[j], land("ys"), ys_free)
            t_h = act(YAH[:, j, :], YS[:, :], ACT.Copy, t)
            t_l = tt(POOL, YAL[:, j, :], YS[:, :], YAH[:, j, :].bitcast(F), ALU.subtract, t_h)
            ys_free = [t_h, t_l]
            t_ya += [t_h, t_l]
        items = []
        for h in range(8):
            for i in range(NT):
                w = 128 * (i + 1)

                def scores(ps, free, h=h, i=i, w=w):
                    PE.wait(free, t_q[i], t_k)
                    for s in range(0, w, 512):
                        n = min(512, w - s)
                        f = mm(ps[:, s:s + n], QTM[:, h, 128 * i:128 * i + 128], KTM[:, h, s:s + n], True, True)
                        if s + 512 < w:
                            PE.quiet(f)
                    return PE.do(f)

                def stat(ps, p, nmx, t_s, free, w=w):
                    d = ps[:, w - 128:w]
                    t_a = tt(DVE, d, d, cst(C_CAUS, 128), ALU.add, t_s)
                    return max_stat(ps, p, nmx, t_a, free, w)

                items.append(dict(nk=[128] * (i + 1), scores=scores, stat=stat,
                                  v=lambda k, h=h: VN[:, k, 64 * h:64 * h + 64], t_v=t_v,
                                  out=ZB[:, i, 64 * h:64 * h + 64], t_g=t_zb[i]))
        attention(items, PM, PTM)

        YBH = sb([128, 4, T], R, W0 + 48 * KB)
        YBL = sb([128, 4, T], R, W0 + 64 * KB)
        GA = [sb([128, T], F, W0 + (80 + 4 * i) * KB) for i in range(2)]
        MG = sb([128, 2, T], F, W0)
        M2 = [sb([128, 512], F, W0 + (8 + 2 * i) * KB) for i in range(2)]
        OT = sb([128, 8, D], F, W0 + 16 * KB)
        X2 = sb([128, 8, D], F, W0 + 48 * KB)
        GP = sb([128, D], F, W0 + 88 * KB)
        JK4 = sb([128, D], F, W0 + 8 * KB)
        enter_phase()
        for q in (SP,):
            q.wait(everyone())
        t_gp = SP.dma(GP[:, :], a["g_post_2"].partition_broadcast(128), land("gp"))
        t_yb = []
        for i in range(NT):
            ps = bank(range(8))
            PE.wait(ps.free)
            for k in range(4):
                f = (lambda o, s: lambda e: e.transpose(o, s, ident))(
                    ps.ap[:, 128 * k:128 * k + 128], ZB[:, i, 128 * k:128 * k + 128])
                if k < 3:
                    PE.quiet(f)
            t = PE.do(f)
            sl = slice(128 * i, 128 * i + 128)
            pv = ps.ap.rearrange("p (k c) -> p k c", c=128)
            t_h = act(YBH[:, :, sl], pv, ACT.Copy, t)
            t_l = tt(DVE, YBL[:, :, sl], pv, YBH[:, :, sl].bitcast(F), ALU.subtract, t_h)
            ps.free = [t_h, t_l]
            t_yb += [t_h, t_l]
        gfree = [[], []]
        n_g = 0
        mfree = [[], []]
        t_mer = []
        DVE.wait(PE.last())
        for n in range(4):
            t_m1 = {}
            for br, (H, L, t_in) in enumerate(((YAH, YAL, t_ya), (YBH, YBL, t_yb))):
                with Block() as b:
                    for c in range(2):
                        z = n_g % 2
                        n_g += 1
                        ct = 2 * n + c
                        t_gl = SP.dma(GA[z][:, :], zg_d[4 + 8 * br + ct], land(f"ga{z}"), gfree[z], t_zg[4 + 8 * br + ct])
                        t_gl = act(GA[z][:, :], GA[z][:, :], ACT.Sigmoid, t_gl, t_vec, bias=vec("b_gate", 8 * br + ct))
                        for half in range(2):
                            sl = slice(512 * half, 512 * half + 512)
                            ps = bank(range(8))
                            t = gemm_tr(b, 128 * c, 128 * c + 128, half, ps.ap, H, L, 4, ps.free, t_in)
                            if br == 0:
                                t = tt(DVE, MG[:, c, sl], ps.ap, GA[z][:, sl], ALU.mult, t, t_gl, t_mer[-4:])
                                ps.free = [t]
                                t_m1[c, half] = t
                            else:
                                t1 = tt(DVE, M2[half][:, :], ps.ap, GA[z][:, sl], ALU.mult, t, t_gl, mfree[half])
                                ps.free = [t1]
                                t = tt(DVE, M2[half][:, :], M2[half][:, :], MG[:, c, sl], ALU.add, t1, t_m1[c, half])
                                t_h = act(AH[:, ct, sl], M2[half][:, :], ACT.Copy, t)
                                t_l = tt(DVE, AL[:, ct, sl], M2[half][:, :], AH[:, ct, sl].bitcast(F), ALU.subtract, t_h)
                                mfree[half] = [t_h, t_l]
                                t_mer += [t_h, t_l]
                        gfree[z] = [DVE.last()]
        for q in (SP, ACTQ, DVE):
            q.wait(everyone())
        t_x2 = [SP.dma(X2[:, i, :], x2_d[128 * i:128 * i + 128, :], land(f"x{i}"), t_sp[i]) for i in range(NT)]
        t_ot = [[] for _ in range(NT)]
        for n in range(4):
            with Block() as b:
                for i in range(NT):
                    ps = bank(range(8))
                    t = gemm_nat(b, i, ps.ap[:, 0:256], AH, AL, 8, 0, 256, ps.free, t_mer)
                    t = act(OT[:, i, 256 * n:256 * n + 256], ps.ap[:, 0:256], ACT.Copy, t)
                    ps.free = [t]
                    t_ot[i].append(t)
        t_out = []
        for i in range(NT):
            t = act(JK4[:, :], OT[:, i, :], ACT.Square, t_ot[i], ACTQ.last(), accum_out=STAT[:, 24 + i:25 + i])
            t = ts(DVE, STAT[:, 32 + i:33 + i], STAT[:, 24 + i:25 + i], 1.0 / D, 1e-6, ALU.mult, ALU.add, t)
            t = rpow(STAT[:, 40 + i:41 + i], STAT[:, 32 + i:33 + i], 1, t)
            t = stt(OT[:, i, :], OT[:, i, :], STAT[:, 40 + i:41 + i], GP[:, :], ALU.mult, ALU.mult, t, t_gp)
            t = tt(DVE, OT[:, i, :], OT[:, i, :], X2[:, i, :], ALU.add, t, t_x2[i])
            t_out.append(SP.dma(out[0, 128 * i:128 * i + 128, :], OT[:, i, :], land(f"o{i}"), t))
        SP.wait(t_out)

        block = ctx.enter_context(nc.Block())

        @block.sync
        def _(e):
            SP.emit(e)

        @block.gpsimd
        def _(e):
            POOL.emit(e)

        @block.vector
        def _(e):
            DVE.emit(e)

        @block.scalar
        def _(e):
            ACTQ.emit(e)

        @block.tensor
        def _(e):
            PE.emit(e)


_INS = ["x", "norm_gain", "w_in", "q_norm_a", "k_norm_a", "na_rpb", "w_out", "final_norm_gain", "positions_2", "g_pre_2",
        "w_in_2", "b_gate_2", "mu_shift_2", "w0_2", "w_decay_up_2", "a0_2", "w_iclr_up_2", "k_k_2", "k_a_2", "r_k_2",
        "gn_gain_2", "gn_bias_2", "w_out_a_2", "g_q_2", "w_uq_2", "g_kv_2", "w_ukv_2", "w_out_b_2", "w_o_2", "g_post_2"]


def kernel(**inputs):
    import numpy as _np
    import concourse.bacc as _bacc
    from concourse import mybir as _mybir
    from concourse.bass_utils import run_bass_kernel_spmd as _run

    nc = _bacc.Bacc("TRN2", target_bir_lowering=False, num_devices=1)
    arrays, args = {}, {}
    for name in _INS:
        arrays[f"in_{name}"] = _np.ascontiguousarray(inputs[name])
    arrays["in_consts"] = constants()
    for name, v in arrays.items():
        args[name[3:]] = nc.dram_tensor(name, v.shape, _mybir.dt.from_np(v.dtype), kind="ExternalInput").ap()
    out = nc.dram_tensor("out_0", (1, T, D), F, kind="ExternalOutput").ap()
    build(nc, args, out)
    r = _run(nc, [arrays], core_ids=[0])
    return r.results[0]["out_0"]
```

```python
from contextlib import ExitStack

import numpy as np

import concourse.bass as bass
from concourse import mybir

F = mybir.dt.float32
R = mybir.dt.float32r
I32 = mybir.dt.int32
ALU = mybir.AluOpType
ACT = mybir.ActivationFunctionType
X = mybir.AxisListType.X

KB = 1024
T = 1024
D = 1024
NT = 8
NEG = -1.0e30
DECAY = 0.6065306597

C_ID, C_CAUS, C_BLK, C_BLKM, C_COL = 0, 128, 256, 384, 512
C_MD, C_MS, C_MI, C_MDT, C_MOT, C_I64, C_INV, C_ONE2 = 576, 640, 704, 768, 832, 896, 960, 976
C_END = 978
C_COS, C_SIN, C_RST = 978, 978 + 512, 978 + 1024
C_ALL = 978 + 2048

VROWS = [("pos", 8), ("mu", 13), ("w0", 4), ("a0", 4), ("k_k", 4), ("k_a", 4),
         ("r_k", 4), ("gn_gain", 4), ("gn_bias", 4), ("g_q", 2), ("g_kv", 1), ("b_gate", 16)]
VOFF = {}
_o = 0
for _n, _c in VROWS:
    VOFF[_n] = _o
    _o += _c
VTOT = _o


def constants():
    c = np.zeros((128, C_ALL), np.float64)
    p = np.arange(128)
    c[:, C_ID:C_ID + 128] = np.eye(128)
    c[:, C_CAUS:C_CAUS + 128] = np.where(p[None, :] <= p[:, None], 0.0, NEG)
    same = (p[:, None] // 64) == (p[None, :] // 64)
    c[:, C_BLK:C_BLK + 128] = same
    c[:, C_BLKM:C_BLKM + 128] = same / 64.0
    j = np.arange(64)
    col = p % 64
    start = np.clip(col - 8, 0, 48)
    c[:, C_COL:C_COL + 64] = np.where((j[None] >= start[:, None]) & (j[None] < start[:, None] + 16), 0.0, NEG)
    s = (p % 64)[:, None]
    t = j[None]
    blk = (s // 16) == (t // 16)
    c[:, C_MD:C_MD + 64] = (s < t) & blk
    c[:, C_MS:C_MS + 64] = s < t
    c[:, C_MI:C_MI + 64] = s <= t
    c[:, C_MDT:C_MDT + 64] = (t < s) & blk
    c[:, C_MOT:C_MOT + 64] = (t < s) & ~blk
    c[:, C_I64:C_I64 + 64] = s == t
    c[:, C_INV:C_INV + 16] = (np.float32(10000.0) ** (-np.arange(0, 32, 2, dtype=np.float32) / np.float32(32)))[None]
    c[:64, C_ONE2] = 1.0
    c[64:, C_ONE2 + 1] = 1.0
    inv = np.float32(10000.0) ** (-np.arange(16, dtype=np.float32) * np.float32(2.0 / 32))
    tok = np.arange(T)
    ar = (tok // 64).astype(np.float32)[:, None] * inv[None]
    ac = (tok % 64).astype(np.float32)[:, None] * inv[None]
    ang = np.concatenate([ar, ar, ac, ac], 1).astype(np.float64)
    sign = np.where((np.arange(64) // 16) % 2 == 0, -1.0, 1.0)
    c[:, C_COS:C_COS + 512] = np.cos(ang).reshape(8, 128, 64).transpose(1, 0, 2).reshape(128, 512)
    c[:, C_SIN:C_SIN + 512] = (np.sin(ang) * sign).reshape(8, 128, 64).transpose(1, 0, 2).reshape(128, 512)
    c[:, C_RST:C_RST + 1024] = (np.arange(T) % 64 != 0)[None]
    return c.astype(np.float32)


class Queue:

    def __init__(self, sem, serial=False):
        self.sem, self.n, self.seen, self.items = sem, 0, {}, []
        self.serial = serial

    def wait(self, *tokens):
        for tok in tokens:
            if tok is None:
                continue
            if isinstance(tok, list):
                self.wait(*tok)
                continue
            sem, value = tok
            if value and self.seen.get(id(sem), 0) < value:
                self.seen[id(sem)] = value
                self.items.append(lambda e, s=sem, v=value: e.wait_ge(s, v))

    def do(self, make, *tokens):
        self.wait(*tokens)
        if self.serial:
            self.wait((self.sem, self.n))
        self.n += 1
        self.items.append(lambda e: make(e).then_inc(self.sem, 1))
        return (self.sem, self.n)

    def quiet(self, make, *tokens):
        self.wait(*tokens)
        self.items.append(make)

    def dma(self, out, in_, land, *tokens):
        self.wait(*tokens)
        land.n += 16
        self.items.append(lambda e: e.dma_start(out, in_).then_inc(land.sem, 16))
        return (land.sem, land.n)

    def last(self):
        return (self.sem, self.n)

    def emit(self, engine):
        for item in self.items:
            item(engine)


class Land:

    def __init__(self, sem):
        self.sem, self.n = sem, 0


class Place:

    def __init__(self, ap):
        self.ap, self.free = ap, []


def bc(ap, dim, n):
    shape = list(ap.shape)
    shape.insert(dim, n)
    return ap.unsqueeze(dim).to_broadcast(shape)


def build(nc, a, out):
    ctx = ExitStack()
    with ctx:
        def sem(name):
            return ctx.enter_context(nc.semaphore(name))

        BASE = nc.sbuf_base + (-nc.sbuf_base) % 32
        count = [0]

        def sb(shape, dt, offset):
            count[0] += 1
            return nc.alloc_sbuf_tensor_at(f"t{count[0]}", shape, dt, offset=BASE + offset)

        PE, ACTQ, DVE, SP = (Queue(sem(n)) for n in ("s_pe", "s_act", "s_dve", "s_sp"))
        POOL = Queue(sem("s_pool"), serial=True)
        lands = {}

        def land(name):
            if name not in lands:
                lands[name] = Land(sem("d_" + name))
            return lands[name]

        ps_all = ctx.enter_context(nc.psum_tensor("ps", [128, 4096], F))
        banks = [Place(ps_all[:, 512 * i:512 * (i + 1)]) for i in range(8)]

        RA = 0
        RW = 64 * KB
        RC = 104 * KB
        RS = 108 * KB
        W0 = 114 * KB
        AH = sb([128, 8, T], R, RA)
        AL = sb([128, 8, T], R, RA + 32 * KB)
        WST = sb([128, 2048], F, RW)
        WHI = [sb([128, 2048], R, RW + (8 + 8 * i) * KB) for i in range(2)]
        WLO = [sb([128, 2048], R, RW + (24 + 8 * i) * KB) for i in range(2)]
        CST = sb([128, C_END], F, RC)
        VT = sb([128, 128], F, RS)
        VTR = sb([128, 128], F, RS + 512)
        STAT = sb([128, 512], F, RS + 1024)
        POSI = sb([8, 128], I32, RS + 3072)
        HALF = sb([128, 128], F, RS + 3584)
        NMX = sb([128, 16], F, RS + 4096)
        RSM = sb([128, 16], F, RS + 4160)
        RIN = sb([128, 16], F, RS + 4224)
        S2 = sb([128, 2, 64], F, RS + 4288)
        PCT = sb([128, 16], F, RS + 4800)

        def cst(col, n):
            return CST[:, col:col + n]

        ident = cst(C_ID, 128)

        def vec(name, k=0, p0=0, p1=128):
            return VT[p0:p1, VOFF[name] + k:VOFF[name] + k + 1]

        def dram(name, shape):
            return nc.dram_tensor(name, shape, F, kind="Internal").ap()

        rpb_d = dram("rpb_pad", [120, 128])
        bias_d = dram("rpb_rows", [120, 64, 64])
        g0_d = dram("gate_spill", [T, 256])
        x2_d = dram("x2_spill", [T, D])
        feat_d = dram("feat_spill", [13, 128, T])
        zg_d = dram("zgate_spill", [20, 128, T])
        cn_d = dram("compressed_spill", [T, 416])
        zb_d = dram("zb_spill", [4, 128, T])
        y_d = dram("recurrence_spill", [4, 128, T])

        t_cst = POOL.dma(CST[:, :], a["consts"][:, 0:C_END], land("cst"))
        t_half = POOL.do(lambda e: e.memset(HALF[:, :], -0.5))
        t_vec = []

        wplan = []

        def want(src, kt, cols):
            wplan.append((src, kt, cols))

        w1 = a["w_in"].rearrange("a k n -> (a k) n")
        w2 = a["w_in_2"]
        wo1 = a["w_out"].rearrange("a k n -> (a k) n")
        O1 = dict(qkv=0, ga=768, qb=1280, kb=1792, vb=2304, gb=2816)
        for c in (512, 0, 256):
            want(w1[:, c:c + 256], 8, 256)
        for c in range(768, 1280, 256):
            want(w1[:, c:c + 256], 8, 256)
        for h in range(2):
            for s in ("qb", "kb", "vb", "gb"):
                c = O1[s] + 256 * (1 - h if s == "gb" else h)
                want(w1[:, c:c + 256], 8, 256)
        for c in range(0, 1024, 256):
            want(wo1[:, c:c + 256], 8, 256)
        TILES = [("f", 12), ("f", 0), ("f", 4), ("f", 8), ("z", 0), ("f", 1), ("f", 5), ("f", 9), ("f", 2), ("f", 6),
                 ("f", 10), ("z", 1), ("f", 3), ("f", 7), ("f", 11), ("z", 2), ("z", 3)] + [("b", n) for n in range(4)] + [("g", n) for n in range(16)]
        first_col = dict(f=0, z=1664, b=2592, g=3104)
        PAIRS = [TILES[n:n + 2] for n in range(0, len(TILES), 2)]
        want(w2[:, 2176:2432], 8, 256)
        want(w2[:, 2432:2592], 8, 160)
        for pair in PAIRS:
            cols = [first_col[kind] + 128 * n for kind, n in pair]
            want([w2[:, c:c + 128] for c in cols], 8, 128 * len(pair))
        want(a["w_ukv_2"], 1, 1024)
        want(a["w_uq_2"], 2, 768)
        MERGES = [(br, n + m) for n in (0, 2) for br in (1, 0) for m in range(2)]
        for br, n in MERGES:
            want(a[("w_out_a_2", "w_out_b_2")[br]][:, 256 * n:256 * n + 256], 4, 256)
        for c in range(0, 1024, 256):
            want(a["w_o_2"][:, c:c + 256], 8, 256)

        wst = Place(WST)
        wsl = [Place(None), Place(None)]
        wready = []
        wcoming = []
        wnext = [0]

        def wfetch():
            n = len(wready) + len(wcoming)
            if n >= len(wplan) or wcoming:
                return
            src, kt, cols = wplan[n]
            st = WST[:, 0:kt * cols].rearrange("p (k c) -> p k c", k=kt)
            if src is a["w_ukv_2"]:
                by_head = src.rearrange("p (h s c) -> p s h c", s=2, c=64)
                parts = [(WST[:, 512 * s:512 * s + 512].rearrange("p (h c) -> p h c", c=64), by_head[:, s]) for s in range(2)]
            elif isinstance(src, list):
                parts = [(st[:, :, 128 * m:128 * m + 128], x.rearrange("(k p) c -> p k c", p=128)) for m, x in enumerate(src)]
            else:
                parts = [(st, src.rearrange("(k p) c -> p k c", p=128))]
            for o, x in parts:
                t = SP.dma(o, x, land("w"), wst.free)
            wcoming.append([t, 0, []])

        def wsplit(last):
            if not wcoming:
                return
            t_d, done, toks = wcoming[0]
            n = len(wready)
            src, kt, cols = wplan[n]
            sl = wsl[n % 2]
            size = kt * cols
            upto = size if last else min(size, done + 512)
            if n == 0:
                for m in range(0, size, 512):
                    part = slice(m, m + 512)
                    t_h = ACTQ.do((lambda o, i: lambda e: e.activation(o, i, ACT.Copy))(WHI[0][:, part], WST[:, part]), t_d)
                    toks.append(tt(POOL if m == 512 else DVE, WLO[0][:, part], WST[:, part], WHI[0][:, part].bitcast(F),
                                   ALU.subtract, t_h))
            elif done < upto:
                part = slice(done, upto)
                t_h = ACTQ.do(lambda e: e.activation(WHI[n % 2][:, part], WST[:, part], ACT.Copy), t_d, sl.free)
                t_l = POOL.do(lambda e: e.tensor_tensor(WLO[n % 2][:, part], WST[:, part], WHI[n % 2][:, part].bitcast(F),
                                                        ALU.subtract), t_h, sl.free)
                toks += [t_h, t_l]
                wcoming[0][1] = upto
            if upto == size:
                wcoming.pop()
                wst.free = toks if n == 0 else toks[-2:]
                view = lambda x: x[n % 2][:, 0:size].rearrange("p (k c) -> p k c", k=kt)
                wready.append((view(WHI), view(WLO), wst.free, sl))

        ticks = [0, 0]

        def wtick(products):
            ticks[0] += products
            while wcoming and ticks[0] >= 20 + 9 * ticks[1]:
                ticks[1] += 1
                wsplit(False)

        class Block:

            def __enter__(self):
                n = wnext[0]
                wnext[0] += 1
                if len(wready) <= n:
                    wfetch()
                    wsplit(True)
                wfetch()
                ticks[:] = [0, 0]
                self.hi, self.lo, self.tok, self.slot = wready[n]
                return self

            def __exit__(self, *exc):
                if len(wready) == wnext[0]:
                    wsplit(True)
                self.slot.free = [PE.last()]

        t_pad = []

        def load_vectors():
            t_vrow = []
            srcs = {}
            for name, key in [("mu", "mu_shift_2"), ("w0", "w0_2"), ("a0", "a0_2"), ("k_k", "k_k_2"),
                              ("k_a", "k_a_2"), ("gn_gain", "gn_gain_2"), ("gn_bias", "gn_bias_2"), ("g_q", "g_q_2"),
                              ("g_kv", "g_kv_2"), ("b_gate", "b_gate_2")]:
                srcs[name] = a[key].rearrange("(r c) -> r c", c=128)
            srcs["r_k"] = a["r_k_2"].rearrange("(r h) d -> r (h d)", h=2)
            t_zero = POOL.do(lambda e: e.memset(VTR[:, :], 0.0))
            for n, (name, rows) in enumerate(VROWS[1:]):
                o = VOFF[name]
                t_vrow.append(SP.dma(VTR[o:o + rows, :], srcs[name], land(f"v{n}"), t_zero))
            t_posi = SP.dma(POSI[:, :], a["positions_2"].rearrange("a (r c) -> (a r) c", c=128), land("posi"))
            t_rows.extend([t_zero, t_posi, t_vrow])

        t_rows = []

        def turn_vectors():
            t_zero, t_posi, t_vrow = t_rows
            t_pos = DVE.do(lambda e: e.tensor_copy(VTR[0:8, :], POSI[:, :]), t_posi, t_zero)
            bk = banks[7]
            t_vt = PE.do(lambda e: e.transpose(bk.ap[:, 0:128], VTR[:, :], ident), t_cst, t_vrow, t_pos, bk.free)
            t_vec.append(DVE.do(lambda e: e.tensor_copy(VT[:, :], bk.ap[:, 0:128]), t_vt))
            bk.free = [t_vec[0]]
            t = POOL.do(lambda e: e.memset(VTR[:, :], 0.0), t_vt)
            t = SP.dma(rpb_d, VTR[0:120, :], land("rpb"), t)
            t = SP.dma(rpb_d[:, 48:79], a["na_rpb"].rearrange("a h r c -> (a h r) c"), land("rpb"), t)
            t_pad.append(SP.dma(bias_d, bass.AP(rpb_d.tensor, 63, [[128, 120], [-1, 64], [1, 64]]), land("rpb"), t))

        rot = [0]

        def bank(choice):
            rot[0] += 1
            return banks[choice[rot[0] % len(choice)]]

        def mm(out_ap, lhs, rhs, start, stop):
            return lambda e: e.matmul(out_ap, lhs, rhs, start=start, stop=stop)

        def product(dst, lefts, rights, *tokens):
            PE.wait(*tokens)
            n = len(lefts)
            for k in range(n):
                (lh, ll), (rh, rl) = lefts[k], rights[k]
                PE.quiet(mm(dst, lh, rh, k == 0, False))
                PE.quiet(mm(dst, lh, rl, False, False))
                last = mm(dst, ll, rh, False, k == n - 1)
                if k < n - 1:
                    PE.quiet(last)
            token = PE.do(last)
            wtick(3 * n * dst.shape[1] / 512)
            return token

        dense_token = [None]

        def product_parts(dst, lefts, rights, *tokens):
            PE.wait(*tokens)
            n = len(lefts)
            for k in range(n):
                (lh, ll), (rh, rl) = lefts[k], rights[k]
                PE.quiet(mm(dst, lh, rh, k == 0, False))
                PE.quiet(mm(dst, lh, rl, False, False))
                last = mm(dst, ll, rh, False, k == n - 1)
                wtick(3 * dst.shape[1] / 512)
                if k < n - 1:
                    PE.quiet(last)
                else:
                    dense_token[0] = PE.do(last)
                yield

        def gemm_nat(b, i, dst, act_h, act_l, kt, c0, c1, *tokens):
            sl = slice(128 * i, 128 * i + 128)
            return product(dst, [(act_h[:, k, sl], act_l[:, k, sl]) for k in range(kt)],
                           [(b.hi[:, k, c0:c1], b.lo[:, k, c0:c1]) for k in range(kt)], b.tok, *tokens)

        def gemm_tr(b, c0, c1, half, dst, act_h, act_l, kt, *tokens):
            sl = slice(512 * half, 512 * half + 512)
            return product(dst, [(b.hi[:, k, c0:c1], b.lo[:, k, c0:c1]) for k in range(kt)],
                           [(act_h[:, k, sl], act_l[:, k, sl]) for k in range(kt)], b.tok, *tokens)

        def everyone():
            return [PE.last(), ACTQ.last(), DVE.last(), POOL.last()]

        def enter_phase():
            toks = everyone()
            for q in (ACTQ, DVE, POOL, SP):
                q.wait(toks)

        def act(o, i, f, *tokens, **kw):
            return ACTQ.do(lambda e: e.activation(o, i, f, **kw), *tokens)

        def tt(q, o, x, y, op, *tokens):
            return q.do(lambda e: e.tensor_tensor(o, x, y, op), *tokens)

        def ts(q, o, x, s1, s2, op0, op1, *tokens):
            return q.do(lambda e: e.tensor_scalar(o, x, s1, s2, op0, op1) if s2 is not None
                        else e.tensor_scalar(o, x, s1, None, op0), *tokens)

        def stt(o, x, s, y, op0, op1, *tokens):
            return DVE.do(lambda e: e.scalar_tensor_tensor(out=o, in0=x, scalar=s, in1=y, op0=op0, op1=op1), *tokens)

        def cp(q, o, i, *tokens):
            return q.do(lambda e: e.tensor_copy(o, i), *tokens)

        def rpow(o, i, n, *tokens):
            return POOL.do(lambda e: e.tensor_tensor(o, i, HALF[:, 0:n], ALU.pow), t_half, *tokens)

        def norm_stat(i, src, junk, c0, *tokens):
            s0, s1, s2 = (STAT[:, c0 + 8 * n + i:c0 + 8 * n + i + 1] for n in range(3))
            t = act(junk, src, ACT.Square, *tokens, ACTQ.last(), accum_out=s0)
            t = ts(DVE, s1, s0, 1.0 / D, 1e-6, ALU.mult, ALU.add, t)
            return s2, rpow(s2, s1, 1, t)

        def norm_tile(i, src, dst, junk, gain, c0, *tokens):
            s2, t = norm_stat(i, src, junk, c0, tokens[0])
            return stt(dst, src, s2, gain, ALU.mult, ALU.mult, t, *tokens[1:])

        def transpose_tile(i, src, t_src):
            toks = []
            sl = slice(128 * i, 128 * i + 128)
            for g in range(2):
                ps = bank(range(8))
                PE.wait(ps.free, t_src, t_cst)
                for k in range(4):
                    f = (lambda o, x: lambda e: e.transpose(o, x, ident))(
                        ps.ap[:, 128 * k:128 * k + 128], src[:, 512 * g + 128 * k:512 * g + 128 * k + 128])
                    if k < 3:
                        PE.quiet(f)
                t = PE.do(f)
                pv = ps.ap.rearrange("p (k c) -> p k c", c=128)
                hi, lo = AH[:, 4 * g:4 * g + 4, sl], AL[:, 4 * g:4 * g + 4, sl]
                t_h = act(hi, pv, ACT.Copy, t)
                t_l = tt(DVE, lo, pv, hi.bitcast(F), ALU.subtract, t_h)
                ps.free = [t_h, t_l]
                toks += [t_h, t_l]
            return toks

        XS = [sb([128, D], F, W0 + (4 * i if i < 4 else 24 + 4 * i) * KB) for i in range(NT)]
        JUNK = sb([128, D], F, W0 + 56 * KB)
        xv = a["x"].rearrange("a (i p) c -> i p (a c)", p=128)
        GAIN1 = sb([128, D], F, W0 + 60 * KB)
        t_x = [SP.dma(XS[0][:, :], xv[0], land("x0"))]
        t_gn = SP.dma(GAIN1[:, :], a["norm_gain"][0].partition_broadcast(128), land("gain"))
        wfetch()
        t_x += [SP.dma(XS[1][:, :], xv[1], land("x1"))]
        t_x += [SP.dma(XS[i][:, :], xv[i], land(f"x{i}")) for i in range(2, NT)]
        MIXA = sb([128, 8, 512], F, W0)
        QKV = sb([128, 8, 768], F, W0 + 16 * KB)
        QT = sb([128, 4, T], R, W0 + 40 * KB)
        KT = sb([128, 2, T], R, W0 + 56 * KB)
        PB = [sb([128, T], F, W0 + (64 + 4 * i) * KB) for i in range(2)]
        PT = [sb([128, T], F, W0 + (72 + 4 * i) * KB) for i in range(2)]
        COS = sb([128, 8, 64], F, W0 + 64 * KB)
        SIN = sb([128, 8, 64], F, W0 + 66 * KB)
        GT = sb([128, 640], F, W0 + 68 * KB)
        TMP = sb([128, 512], F, W0 + 71 * KB)
        ROT = [sb([128, 2, 256], F, W0 + (73 + 2 * z) * KB) for z in range(2)]
        QS = sb([128, 4, 2, 64], F, W0 + 80 * KB)
        KS = sb([128, 4, 64], F, W0 + 82 * KB)
        KT2 = sb([128, 2, T], R, W0 + 83 * KB)
        t_cos = SP.dma(COS[:, :, :], a["consts"][:, C_COS:C_COS + 512].rearrange("p (i c) -> p i c", c=64), land("cos"))
        t_sin = SP.dma(SIN[:, :, :], a["consts"][:, C_SIN:C_SIN + 512].rearrange("p (i c) -> p i c", c=64), land("sin"))
        t_g1 = SP.dma(GT[:, 0:64], a["q_norm_a"][0].partition_broadcast(128), land("gq"))
        t_g2 = SP.dma(GT[:, 512:576], a["k_norm_a"][0].partition_broadcast(128), land("gk"))
        t_qkv = [[None] * 3 for _ in range(NT)]
        t_rope = [[None] * 3 for _ in range(NT)]
        HEADS = ((512, 2), (0, 4), (256, 4))
        t_sq, t_rs, rope_free = [[], [], []], [None] * 3, [None, None]

        def rope_stat(n, j0, heads):
            return STAT[:, j0 + 64 + 32 * n:j0 + 64 + 32 * n + 8 * heads]

        def squares(i, n):
            c0, heads = HEADS[n]
            w = 64 * heads
            qk, tm = QKV[:, i, c0:c0 + w], TMP[:, 256:256 + w]
            t = act(tm, qk, ACT.Square, t_qkv[i][n], t_sq[n][-1:], t_sq[n - 1][-1:] if n else None)
            o = rope_stat(n, 0, heads)[:, heads * i:heads * i + heads]
            t_sq[n].append(DVE.do(lambda e: e.tensor_reduce(o, tm.rearrange("p (h c) -> p h c", c=64), X, ALU.add), t))

        def rope_scale(n):
            heads = HEADS[n][1]
            s1, s2 = rope_stat(n, 0, heads), rope_stat(n, 96, heads)
            t = ts(DVE, s2, s1, 1.0 / 64, 1e-6, ALU.mult, ALU.add, t_sq[n])
            t_rs[n] = rpow(rope_stat(n, 192, heads), s2, 8 * heads, t)

        def rope(i, n):
            c0, heads = HEADS[n]
            w = 64 * heads
            z = i % 2
            s3 = rope_stat(n, 192, heads)[:, heads * i:heads * i + heads]
            qk = QKV[:, i, c0:c0 + w]
            q3 = qk.rearrange("p (h c) -> p h c", c=64)
            tm, tm2 = ROT[z][:, 0, 0:w], ROT[z][:, 1, 0:w]
            t = tt(DVE, q3, q3, bc(s3, 2, 64), ALU.mult, t_rs[n])
            t = tt(DVE, qk, qk, GT[:, c0:c0 + w], ALU.mult, t, t_ga, t_gb)
            t1 = tt(POOL, tm.rearrange("p (h c) -> p h c", c=64), q3, bc(COS[:, i, :], 1, heads), ALU.mult, t, t_cos, rope_free[z])
            q5 = qk.rearrange("p (h x f c) -> p h x f c", x=2, f=2, c=16)
            s5 = bc(SIN[:, i, :], 1, heads).rearrange("p h (x f c) -> p h x f c", x=2, f=2)
            o5 = tm2.rearrange("p (h x f c) -> p h x f c", x=2, f=2, c=16)
            ta = tt(DVE, o5[:, :, :, 0, :], q5[:, :, :, 1, :], s5[:, :, :, 0, :], ALU.mult, t, t_sin, rope_free[z])
            tb = tt(DVE, o5[:, :, :, 1, :], q5[:, :, :, 0, :], s5[:, :, :, 1, :], ALU.mult, t, t_sin)
            return lambda: rope_end(i, n, qk, tm, tm2, t1, ta, tb)

        def rope_end(i, n, qk, tm, tm2, *tokens):
            t_rope[i][n] = rope_free[i % 2] = tt(DVE, qk, tm, tm2, ALU.add, *tokens)

        rope_open = []

        def rope_step(i, n):
            rope_open.append(rope(i, n))
            if len(rope_open) > 1 or i == NT - 1:
                rope_open.pop(0)()
            if i == NT - 1:
                while rope_open:
                    rope_open.pop(0)()

        def norm_next(i):
            t_n.append(norm_tile(i, XS[i][:, :], XS[i][:, :], JUNK[:, :], GAIN1[:, :], 0, t_x[i], t_gn))

        t_act, t_n = [], []
        norm_next(0)
        t_act.append(transpose_tile(0, XS[0][:, :], t_n[0]))
        for n, c0 in enumerate((512, 0, 256)):
            with Block() as b:
                for i in range(NT):
                    if n == 0:
                        for m in (1, 2) if i == 0 else (i + 2,):
                            if m < NT:
                                norm_next(m)
                        if i + 1 < NT:
                            t_act.append(transpose_tile(i + 1, XS[i + 1][:, :], t_n[i + 1]))
                    ps = bank(range(8))
                    t = gemm_nat(b, i, ps.ap[:, 0:256], AH, AL, 8, 0, 256, ps.free, t_act[i])
                    t = act(QKV[:, i, c0:c0 + 256], ps.ap[:, 0:256], ACT.Copy, t)
                    ps.free = [t]
                    t_qkv[i][n] = t
                    if i:
                        squares(i - 1, n)
                    if n:
                        rope_step(i, n - 1)
                squares(NT - 1, n)
                rope_scale(n)
            if n == 0:
                t_g = ts(DVE, GT[:, 0:64], GT[:, 0:64], 0.125, None, ALU.mult, None, t_g1)
                t_ga = cp(DVE, GT[:, 64:512].rearrange("p (h c) -> p h c", c=64), bc(GT[:, 0:64], 1, 7), t_g)
                t_gb = cp(DVE, GT[:, 576:640], GT[:, 512:576], t_g2)
                load_vectors()

        KTS = [KT, KT2]
        t_last = dict(q=None, k=None)
        t_qt = [[None] * NT for _ in range(2)]
        t_kt = [[None] * NT for _ in range(2)]

        t_split = {}

        def split_group(kv, i):
            q3 = QKV[:, i, 256 * kv:256 * kv + 256].rearrange("p (h c) -> p h c", c=64)
            k1 = QKV[:, i, 512 + 64 * kv:576 + 64 * kv]
            t1 = act(QS[:, :, 0, :].bitcast(R), q3, ACT.Copy, t_rope[i][1 + kv], t_last["q"])
            t2 = tt(DVE, QS[:, :, 1, :], q3, QS[:, :, 0, :], ALU.subtract, t1)
            t3 = act(KS[:, 0:2, :].bitcast(R), bc(k1, 1, 2), ACT.Copy, t_rope[i][0], t_last["k"])
            t4 = tt(DVE, KS[:, 2:4, :], bc(k1, 1, 2), KS[:, 0:2, :], ALU.subtract, t3)
            t_split[kv, i] = t2, t4

        def turn_group(kv, i, choice, *tokens):
            t2, t4 = t_split[kv, i]
            ps = bank(choice)
            PE.wait(ps.free, t2)
            for h in range(4):
                f = (lambda o, s: lambda e: e.transpose(o, s, ident))(ps.ap[:, 128 * h:128 * h + 128], QS[:, h, :, :])
                if h < 3:
                    PE.quiet(f)
            t_p = t_last["q"] = PE.do(f)
            t = act(QT[:, :, 128 * i:128 * i + 128], ps.ap.rearrange("p (h c) -> p h c", c=128), ACT.Copy, t_p, *tokens)
            ps.free = [t]
            t_qt[kv][i] = t
            ps = bank(choice)
            PE.wait(ps.free, t4)
            for h in range(2):
                f = (lambda o, s: lambda e: e.transpose(o, s, ident))(ps.ap[:, 128 * h:128 * h + 128], KS[:, 2 * h:2 * h + 2, :])
                if h < 1:
                    PE.quiet(f)
            t_p = t_last["k"] = PE.do(f)
            t = cp(DVE, KTS[kv][:, :, 128 * i:128 * i + 128], ps.ap[:, 0:256].rearrange("p (h c) -> p h c", c=128), t_p, *tokens)
            ps.free = [t]
            t_kt[kv][i] = t

        for q in (ACTQ, DVE):
            q.wait(t_act, t_n)
        t_gA = [[] for _ in range(NT)]
        for n in range(2):
            with Block() as b:
                for i in range(NT):
                    ps = bank(range(8))
                    t = gemm_nat(b, i, ps.ap[:, 0:256], AH, AL, 8, 0, 256, ps.free, t_act[i])
                    t = act(MIXA[:, i, 256 * n:256 * n + 256], ps.ap[:, 0:256], ACT.Silu, t)
                    ps.free = [t]
                    t_gA[i].append(t)
                    if n == 0:
                        rope_step(i, 2)
                    else:
                        if i:
                            turn_group(0, i - 1, range(8))
                        split_group(0, i)
        turn_group(0, NT - 1, range(8))

        seq = [0]

        def attention(items, pbuf, tbuf, between=None, outs=(6, 7)):
            spair = [(banks[0], banks[1]), (banks[2], banks[3])]
            tpair = (banks[4], banks[5])
            opair = [banks[n] for n in outs]
            st = []
            depth = len(pbuf)
            pslot = [Place(None) for _ in pbuf]
            for p in pslot:
                p.free = [PE.last()]
            tslot = pslot if tbuf is None else [Place(None), Place(None)]
            tbuf = tbuf or pbuf

            def scores(n):
                it = items[n]
                z = seq[0] + n
                s0, s1 = spair[z % 2]
                ps = ps_all[:, 1024 * (z % 2):1024 * (z % 2) + 1024]
                t_s = it["scores"](ps, s0.free + s1.free)
                c = slice(z % 16, z % 16 + 1)
                pl = pslot[z % depth]
                src, t_m, t_free = it["stat"](ps, pbuf[z % depth], NMX[:, c], t_s, pl.free)
                w = sum(it["nk"])
                p = pbuf[z % depth][:, 0:w]
                t_e = act(p, src, ACT.Exp, t_m, pl.free, bias=NMX[:, c], scale=1.0, accum_out=RSM[:, c])
                s0.free = s1.free = [t_free if t_free is not None else t_e]
                st.append(dict(z=z, c=c, p=p, t_e=t_e))

            def turn(n):
                it, s = items[n], st[n]
                z = s["z"]
                PE.wait(s["t_e"], tpair[0].free, tpair[1].free)
                pt = tbuf[z % len(tbuf)]
                off = 0
                toks = []
                for half in range(2):
                    ks = list(range(4 * half, min(4 * half + 4, len(it["nk"]))))
                    if not ks:
                        continue
                    b = tpair[half]
                    for k in ks:
                        w = it["nk"][k]
                        last = (lambda o, i: lambda e: e.transpose(o, i, ident))(
                            b.ap[0:w, 128 * (k % 4):128 * (k % 4) + 128], s["p"][:, 128 * k:128 * k + w])
                        if k != ks[-1]:
                            PE.quiet(last)
                    toks.append((half, ks, PE.do(last)))
                if tslot is not pslot:
                    pslot[z % depth].free = [PE.last()]
                outs = []
                for half, ks, t in toks:
                    b = tpair[half]
                    full = [k for k in ks if it["nk"][k] == 128]
                    parts = []
                    if full:
                        o0 = 128 * (full[0] % 4)
                        parts.append((slice(0, 128), 128 * full[0], 128 * len(full), o0))
                    if len(full) < len(ks):
                        parts.append((slice(0, it["nk"][ks[-1]]), 128 * ks[-1], 128, 128 * (ks[-1] % 4)))
                    for pr, d0, n_, o0 in parts:
                        if half == 0:
                            t2 = cp(DVE, pt[pr, d0:d0 + n_], b.ap[pr, o0:o0 + n_], t, tslot[z % len(tslot)].free)
                        else:
                            t2 = act(pt[pr, d0:d0 + n_], b.ap[pr, o0:o0 + n_], ACT.Copy, t, tslot[z % len(tslot)].free)
                        outs.append(t2)
                    b.free = [outs[-1]] if len(parts) == 1 else outs[-2:]
                s["t_pt"] = outs

            def values(n):
                it, s = items[n], st[n]
                z = s["z"]
                ob = opair[z % 2]
                PE.wait(ob.free, s["t_pt"], it["t_v"])
                pt = tbuf[z % len(tbuf)]
                nk = it["nk"]
                for k, w in enumerate(nk):
                    last = mm(ob.ap[:, 0:64], pt[0:w, 128 * k:128 * k + 128], it["v"](k)[0:w], k == 0, k == len(nk) - 1)
                    if k < len(nk) - 1:
                        PE.quiet(last)
                t_o = PE.do(last)
                tslot[z % len(tslot)].free = [t_o]
                t_r = DVE.do(lambda e: e.reciprocal(RIN[:, s["c"]], RSM[:, s["c"]]), s["t_e"])
                if it["t_g"] is None:
                    t_f = ts(DVE, it["out"], ob.ap[:, 0:64], RIN[:, s["c"]], None, ALU.mult, None, t_o, t_r)
                else:
                    t_f = stt(it["out"], ob.ap[:, 0:64], RIN[:, s["c"]], it["out"], ALU.mult, ALU.mult, t_o, t_r, it["t_g"])
                ob.free = [t_f]
                it["done"] = t_f

            N = len(items)
            for n in range(N + 2):
                if n < N:
                    scores(n)
                if 1 <= n <= N:
                    turn(n - 1)
                if n >= 2:
                    values(n - 2)
                if between:
                    between(n)
            seq[0] += N
            for p in banks:
                p.free = p.free + [PE.last(), ACTQ.last(), DVE.last()]

        def max_stat(ps, p, nmx, t_s, free, w):
            t_m = DVE.do(lambda e: e.tensor_reduce(nmx, ps[:, 0:w], X, ALU.max, negate=True), t_s)
            return ps[:, 0:w], t_m, None

        for q in (ACTQ, DVE):
            q.wait(t_rope[NT - 1])
        for kv in range(2):
            items = []
            t_scored = [None] * NT
            for i in range(NT):
                for h in range(4):
                    def scores(ps, free, h=h, i=i, kv=kv, t_scored=t_scored):
                        PE.wait(free, t_qt[kv][i], t_kt[kv])
                        for half in range(2):
                            for n in range(2):
                                f = mm(ps[:, 512 * half:512 * half + 512], QT[:, h, 128 * i:128 * i + 128],
                                       KTS[kv][:, n, 512 * half:512 * half + 512], n == 0, n == 1)
                                if half + n < 2:
                                    PE.quiet(f)
                        t_scored[i] = PE.do(f)
                        return t_scored[i]

                    items.append(dict(
                        nk=[128] * 8, scores=scores,
                        stat=lambda ps, p, nmx, t_s, free: max_stat(ps, p, nmx, t_s, free, 1024),
                        v=lambda k, kv=kv: QKV[:, k, 640 + 64 * kv:704 + 64 * kv], t_v=[t_qkv[k][0] for k in range(8)],
                        out=MIXA[:, i, 64 * (4 * kv + h):64 * (4 * kv + h) + 64], t_g=t_gA[i]))

            def following(n, t_scored=t_scored):
                i = (n - 4) // 4
                if 0 <= i < NT:
                    if n % 4 == 0:
                        split_group(1, i)
                    elif n % 4 == 1:
                        turn_group(1, i, (6, 7), t_scored[i])

            attention(items, PB, PT, following if kv == 0 else None)
            if kv == 0:
                turn_vectors()

        MIXB = sb([128, 8, 512], F, W0 + 16 * KB)
        QH = sb([128, 2, T], R, W0 + 32 * KB)
        QL = sb([128, 2, T], R, W0 + 40 * KB)
        KH = sb([128, 2, T], R, W0 + 48 * KB)
        KL = sb([128, 2, T], R, W0 + 56 * KB)
        VB = sb([128, 8, 256], F, W0 + 64 * KB)
        BI = sb([128, 4, 14, 64], F, W0 + 72 * KB)
        SBN = [sb([128, 640], F, W0 + 86 * KB + 2560 * i) for i in range(3)]

        t_g0, t_g1 = [], []
        GST = sb([128, 256], F, RS + 4928)
        for hh in range(2):
            enter_phase()
            t_q, t_k = [], []
            for (hi, lo, toks, sc) in ((QH, QL, t_q, 0.125), (KH, KL, t_k, 1.0)):
                with Block() as b:
                    for c in range(2):
                        for half in range(2):
                            ps = bank(range(8))
                            t = gemm_tr(b, 128 * c, 128 * c + 128, half, ps.ap, AH, AL, 8, ps.free, t_act[4 * half:4 * half + 4])
                            sl = slice(512 * half, 512 * half + 512)
                            t_h = act(hi[:, c, sl], ps.ap, ACT.Copy, t, scale=sc)
                            t_l = stt(lo[:, c, sl], ps.ap, sc, hi[:, c, sl].bitcast(F), ALU.mult, ALU.subtract, t_h)
                            ps.free = [t_h, t_l]
                            toks += [t_h, t_l]
            t_b = []
            for half in range(2):
                for h in range(4):
                    first = (4 * hh + h) * 15 + (1 if half == 0 else 0)
                    src = bias_d[first:first + 14].rearrange("r c k -> c r k")
                    t_b.append(SP.dma(BI[64 * half:64 * half + 64, h, :, :], src, land(f"bi{half}{h}"), t_pad))
            t_bi = []
            for h in range(4):
                t_bi.append(tt(POOL, BI[:, h, :, :], BI[:, h, :, :], bc(cst(C_COL, 64), 1, 14), ALU.add, t_b[h], t_b[4 + h], t_cst))
            t_v, t_g = [], []
            with Block() as b:
                for i in range(NT):
                    ps = bank(range(8))
                    t = gemm_nat(b, i, ps.ap[:, 0:256], AH, AL, 8, 0, 256, ps.free, t_act[i])
                    t = act(VB[:, i, :], ps.ap[:, 0:256], ACT.Copy, t)
                    ps.free = [t]
                    t_v.append(t)
            gate_block = Block()
            gate_block.__enter__()

            def gate_work(b=gate_block, hh=hh):
                for i in range(NT):
                    sl = slice(128 * i, 128 * i + 128)
                    ps = banks[7]
                    yield from product_parts(ps.ap[:, 0:256], [(AH[:, k, sl], AL[:, k, sl]) for k in range(8)],
                                             [(b.hi[:, k, 0:256], b.lo[:, k, 0:256]) for k in range(8)], b.tok, ps.free, t_act[i])
                    if hh == 0:
                        t = act(MIXB[:, i, 256:512], ps.ap[:, 0:256], ACT.Copy, dense_token[0])
                        t_g1.append(t)
                    else:
                        t = act(GST[:, :], ps.ap[:, 0:256], ACT.Copy, dense_token[0], t_g0[-1:])
                        t_g0.append(SP.dma(g0_d[sl, :], GST[:, :], land("g0"), t))
                    ps.free = [t]

            gate_parts = gate_work()

            def between(n):
                for _ in range(0 if n % 2 else 4):
                    next(gate_parts, None)

            if hh == 1:
                t_g = [act(MIXB[:, i, 256:512], MIXB[:, i, 256:512], ACT.Silu, t_g1[i]) for i in range(NT)]
            for inner in range(2):
                items = []
                t_mask = []
                if inner:
                    t_all = DVE.last()
                    t_mask = [POOL.do(lambda e: e.memset(BI[64:128, :, 2, :], NEG), t_all),
                              POOL.do(lambda e: e.memset(BI[0:64, :, 10, :], NEG), t_all)]
                for h in range(4):
                    for i in ((2, 3, 4, 5) if inner else (0, 1, 6, 7)):
                        w = 576 if inner else 512
                        row0 = 2 * i - 4 if inner else (0 if i < 2 else 8)
                        k0 = 64 * row0
                        j0 = row0 - 2 * i + 6

                        def scores(ps, free, h=h, i=i, w=w, k0=k0, t_q=t_q, t_k=t_k):
                            PE.wait(free, t_q, t_k)
                            pr = slice(64 * (h % 2), 64 * (h % 2) + 64)
                            qs = slice(128 * i, 128 * i + 128)
                            c = h // 2
                            for s in range(0, w, 512):
                                n = min(512, w - s)
                                ks = slice(k0 + s, k0 + s + n)
                                o = ps[:, s:s + n]
                                PE.quiet(mm(o, QH[pr, c, qs], KH[pr, c, ks], True, False))
                                PE.quiet(mm(o, QL[pr, c, qs], KH[pr, c, ks], False, False))
                                f = mm(o, QH[pr, c, qs], KL[pr, c, ks], False, True)
                                if s + 512 < w:
                                    PE.quiet(f)
                            return PE.do(f)

                        def stat(ps, p, nmx, t_s, free, h=h, w=w, j0=j0, t_bi=t_bi, t_mask=t_mask):
                            bias = BI[:, h, j0:j0 + w // 64, :].rearrange("p r c -> p (r c)")
                            t_a = tt(DVE, p[:, 0:w], ps[:, 0:w], bias, ALU.add, t_s, free, t_bi[h], t_mask)
                            t_m = DVE.do(lambda e: e.tensor_reduce(nmx, p[:, 0:w], X, ALU.max, negate=True), t_a)
                            return p[:, 0:w], t_m, t_a

                        nk = [128] * 4 + ([64] if inner else [])
                        items.append(dict(
                            nk=nk, scores=scores, stat=stat,
                            v=lambda k, h=h, k0=k0: VB[:, k0 // 128 + k, 64 * h:64 * h + 64], t_v=t_v,
                            out=MIXB[:, i, 64 * (4 * hh + h):64 * (4 * hh + h) + 64], t_g=t_g[i] if hh else None))
                attention(items, SBN, None, between, outs=(6, 6))
            for _ in gate_parts:
                pass
            gate_block.__exit__()

        XR = sb([128, 8, D], F, W0 + 32 * KB)
        FG = sb([128, D], F, W0 + 64 * KB)
        JK2 = sb([128, D], F, W0 + 68 * KB)
        XN = sb([128, 8, D], F, W0)
        enter_phase()
        G0 = sb([128, 8, 256], F, W0 + 76 * KB)
        t_gl0 = SP.dma(G0[:, :, :], g0_d.rearrange("(i p) c -> p i c", p=128), land("g0"), t_g0)
        t_xr = [SP.dma(XR[:, i, :], xv[i], land(f"x{i}")) for i in range(NT)]
        t_fg = SP.dma(FG[:, :], a["final_norm_gain"].partition_broadcast(128), land("fg"))
        GAIN2 = sb([128, D], F, W0 + 72 * KB)
        t_g2 = SP.dma(GAIN2[:, :], a["g_pre_2"].partition_broadcast(128), land("gain"))
        t_mixed = DVE.last()
        t_gated = []
        for i in range(NT):
            t_s = act(G0[:, i, :], G0[:, i, :], ACT.Silu, t_gl0)
            t_gated.append(tt(DVE, MIXB[:, i, 0:256], MIXB[:, i, 0:256], G0[:, i, :], ALU.mult, t_s))
        t_act = []
        for i in range(NT):
            toks = []
            for g, src in enumerate((MIXA, MIXB)):
                ps = bank(range(8))
                PE.wait(ps.free, t_mixed, t_gated[i] if g else None)
                for k in range(4):
                    f = (lambda o, x: lambda e: e.transpose(o, x, ident))(
                        ps.ap[:, 128 * k:128 * k + 128], src[:, i, 128 * k:128 * k + 128])
                    if k < 3:
                        PE.quiet(f)
                t_p = PE.do(f)
                sl = slice(128 * i, 128 * i + 128)
                pv = ps.ap.rearrange("p (k c) -> p k c", c=128)
                t_h = act(AH[:, 4 * g:4 * g + 4, sl], pv, ACT.Copy, t_p)
                t_l = tt(DVE, AL[:, 4 * g:4 * g + 4, sl], pv, AH[:, 4 * g:4 * g + 4, sl].bitcast(F), ALU.subtract, t_h)
                ps.free = [t_h, t_l]
                toks += [t_h, t_l]
            t_act.append(toks)
        t_mt = PE.last()
        t_x1 = [[] for _ in range(NT)]
        t_sp, t_f, t_n, t_act2 = [], [], [], []

        def turn_next(i):
            t_act2.append(transpose_tile(i, XN[:, i, :], [t_n[i], PE.last()]))

        def norms(i):
            if i < NT:
                r1, t_r1 = norm_stat(i, XR[:, i, :], JK2[:, :], 24, t_x1[i])
            if i > 0:
                r2, t_r2 = norm_stat(i - 1, XR[:, i - 1, :], JK2[:, :], 48, t_f[i - 1])
            if i < NT:
                t_f.append(stt(XR[:, i, :], XR[:, i, :], r1, FG[:, :], ALU.mult, ALU.mult, t_r1, t_fg))
                t_sp.append(SP.dma(x2_d[128 * i:128 * i + 128, :], XR[:, i, :], land(f"x{i}"), t_f[i]))
            if i > 0:
                t_n.append(stt(XN[:, i - 1, :], XR[:, i - 1, :], r2, GAIN2[:, :], ALU.mult, ALU.mult, t_r2, t_g2, t_mt))
            if i > 1 and i < NT:
                turn_next(i - 2)

        for n in range(4):
            with Block() as b:
                for i in range(NT):
                    ps = bank(range(8))
                    t = gemm_nat(b, i, ps.ap[:, 0:256], AH, AL, 8, 0, 256, ps.free, t_act[i])
                    xs = XR[:, i, 256 * n:256 * n + 256]
                    t = tt(DVE, xs, xs, ps.ap[:, 0:256], ALU.add, t, t_xr[i])
                    ps.free = [t]
                    t_x1[i].append(t)
                    if n == 3:
                        norms(i)
        norms(NT)
        turn_next(6)
        turn_next(7)
        t_act = t_act2

        STG = [sb([128, T], F, W0 + 4 * i * KB) for i in range(3)]
        WA = sb([128, T], F, W0 + 12 * KB)
        LW = sb([128, 512], F, W0 + 16 * KB)
        RST = sb([128, 512], F, W0 + 18 * KB)
        KA1 = sb([128, 4], F, W0 + 20 * KB)
        CD = DECAY

        TU, CU_, MP = 256, 4, 2

        class Slot:

            def __init__(self, n, regions):
                self.n, self.regions = n, [list(r) for r in regions]
                self.FR, self.FK, self.FV = (self.buf([128, TU + 1]) for _ in range(3))
                self.AR, self.BK = self.buf([128, 2, CU_, 64]), self.buf([128, CU_, 2, 64])
                self.BON, self.YT, self.ZAT = (self.buf([128, TU]) for _ in range(3))
                self.BHN, self.KHN, self.VNN = (self.buf([128, CU_ // 2, 128]) for _ in range(3))
                self.DG, self.HX = (self.buf([128, CU_, 64]) for _ in range(2))
                self.BD, self.BF = (self.buf([128, CU_, 128]) for _ in range(2))
                self.t_zero = [POOL.do(lambda e, b=b: e.memset(b[:, :, :], 0.0)) for b in (self.BD, self.BF)]
                self.GM = [self.buf([128, CU_, 64]) for _ in range(3)]
                self.ZZ = [self.buf([128, CU_, 128]) for _ in range(2)]
                self.PCT = self.buf([128, CU_])
                o = self.place(28 * TU)
                self.SH = [sb([128, TU], F, o + 4 * TU * n) for n in range(7)] + [self.buf([128, TU])]
                self.CH = [sb([128, CU_, 64], F, o + 4 * TU * n) for n in (0, 1, 2, 5, 6)]
                self.NB = sb([128, CU_, 2, 64], F, o + 12 * TU)
                self.MTS, self.GS, self.QSS, self.YL = (sb([128, CU_, 64], F, o + 4 * TU * n) for n in (0, 1, 2, 4))
                self.banks = banks[3 * n:3 * n + 3]
                self.turn = 0
                self.done, self.f_free, self.loads = [], [], None

            def place(self, size):
                for r in self.regions:
                    if r[1] - r[0] >= size:
                        r[0] += size
                        return r[0] - size
                raise MemoryError

            def buf(self, shape):
                size = 4 * int(np.prod(shape[1:]))
                return sb(shape, F, self.place(size + (-size) % 32))

            def bank(self):
                self.turn += 1
                return self.banks[self.turn % 3]


        enter_phase()
        for q in (ACTQ, DVE, POOL, SP):
            q.wait(t_sp)
        slots = [Slot(n, [(W0 + (21 + 36 * n) * KB, W0 + (57 + 36 * n) * KB)]) for n in range(2)]
        t_rst = SP.dma(RST[:, :], a["consts"][:, C_RST:C_RST + 512], land("rst"))
        t_lw = [SP.dma(LW[0:64, :], a["w_decay_up_2"], land("lw0")), SP.dma(LW[64:128, :], a["w_iclr_up_2"], land("lw1"))]
        t_ka = ts(DVE, KA1[:, :], VT[:, VOFF["k_a"]:VOFF["k_a"] + 4], -1.0, 1.0, ALU.mult, ALU.add, t_vec)

        def load_shifted(buf, tile, h, name, *tokens):
            if h:
                return SP.dma(buf[:, :], feat_d[tile][:, TU * h - 1:TU * h + TU], land(name), t_feat[tile], *tokens)
            return [POOL.do(lambda e: e.memset(buf[:, 0:1], 0.0), *tokens),
                    SP.dma(buf[:, 1:TU + 1], feat_d[tile][:, 0:TU], land(name), t_feat[tile], *tokens)]

        def shifted(buf, tmp, mu, *tokens):
            x = buf[:, 1:TU + 1]
            t = tt(DVE, tmp[:, :], buf[:, 0:TU], x, ALU.subtract, *tokens)
            return stt(x, tmp[:, :], mu, x, ALU.mult, ALU.add, t)

        stage = [Place(STG[i]) for i in range(3)]
        n_st = [0]
        t_feat, t_zg, t_cnd, t_zbd = [None] * 13, [None] * 20, [], [None] * 4


        def next_stage():
            n_st[0] += 1
            return stage[n_st[0] % 3], land(f"stg{n_st[0] % 3}")

        def natural():
            for dst, c0, w, toks in ((cn_d, 0, 256, t_cnd), (cn_d, 256, 160, t_cnd)):
                with Block() as b:
                    for g in range(2):
                        st_, ld = next_stage()
                        sv = st_.ap[:, 0:4 * w].rearrange("p (i c) -> p i c", i=4)
                        t_o = []
                        for i in range(4):
                            sl = slice(128 * (4 * g + i), 128 * (4 * g + i) + 128)
                            ps = bank((6, 7))
                            yield from product_parts(ps.ap[:, 0:w], [(AH[:, k, sl], AL[:, k, sl]) for k in range(8)],
                                                     [(b.hi[:, k, 0:w], b.lo[:, k, 0:w]) for k in range(8)], b.tok, ps.free, t_act[4 * g + i])
                            t = act(sv[:, i, :], ps.ap[:, 0:w], ACT.Copy, dense_token[0], st_.free)
                            ps.free = [t]
                            t_o.append(t)
                        t = SP.dma(dst[512 * g:512 * g + 512, c0:c0 + w].rearrange("(i p) c -> p i c", p=128), sv, ld, t_o)
                        st_.free = [t]
                        toks.append(t)

        def dense():
            yield from natural()
            for pair in PAIRS:
                with Block() as b:
                    for c, (kind, n) in enumerate(pair):
                        st_, ld = next_stage()
                        t_o = []
                        for half in range(2):
                            sl = slice(512 * half, 512 * half + 512)
                            cs = slice(128 * c, 128 * c + 128)
                            ps = bank((6, 7))
                            yield from product_parts(ps.ap, [(b.hi[:, k, cs], b.lo[:, k, cs]) for k in range(8)],
                                                     [(AH[:, k, sl], AL[:, k, sl]) for k in range(8)], b.tok, ps.free,
                                                     t_act[4 * half:4 * half + 4])
                            t, o = dense_token[0], st_.ap[:, sl]
                            t = act(o, ps.ap, ACT.Copy, t, st_.free)
                            ps.free = [t]
                            t_o.append(t)
                            yield
                        dst = {"f": feat_d, "z": zg_d[0:4], "g": zg_d[4:20], "b": zb_d}[kind][n]
                        t = SP.dma(dst, st_.ap[:, :], ld, t_o)
                        st_.free = [t]
                        if kind == "f":
                            t_feat[n] = t
                        elif kind == "b":
                            t_zbd[n] = t
                        else:
                            t_zg[n if kind == "z" else 4 + n] = t

        filler = dense()
        credit = [0.0]

        def fill(us):
            credit[0] += us
            while credit[0] > 0.6:
                credit[0] -= 0.64
                next(filler, None)

        def need(table, n):
            while table[n] is None:
                next(filler)

        need(t_feat, 12)

        t_wa = []
        for h in range(T // TU):
            S = slots[h % 2]
            t = load_shifted(S.FR, 12, h, f"fr{S.n}", S.f_free)
            t = shifted(S.FR, S.SH[7], vec("mu", 12), t, t_vec, DVE.last())
            sl = slice(TU * h, TU * h + TU)
            t_wa.append([act(WA[0:64, sl], S.FR[0:64, 1:TU + 1], ACT.Tanh, t),
                         cp(DVE, WA[64:128, sl], S.FR[64:128, 1:TU + 1], t)])
            S.f_free = t_wa[h]
            fill(3)

        ch3 = lambda t_: t_.rearrange("p (c t) -> p c t", t=64)

        def mask(col, n):
            return bc(cst(col, 64), 1, n)

        def load_unit(S, j, h):
            for s in range(3):
                need(t_feat, 4 * s + j)
            S.loads = [load_shifted(b_, 4 * s + j, h, f"{n_}{S.n}", S.f_free)
                       for s, (b_, n_) in enumerate(((S.FR, "fr"), (S.FK, "fk"), (S.FV, "fv")))]

        STAGE, NAT, INV, CHAIN, NORM, OFFSET = 0.94, 0.61, 0.57, 0.67, 0.54, 18

        def head_scale(S, sq, t_sq, c0, mul, add, floor):
            ps = S.bank()
            PE.wait(ps.free, t_sq)
            for m in range(MP):
                f = mm(ps.ap[:, 2 * m:2 * m + 2], sq[:, 128 * m:128 * m + 128], cst(C_ONE2, 2), True, True)
                if m < MP - 1:
                    PE.quiet(f)
            t = PE.do(f)
            s0, s1 = STAT[:, c0:c0 + CU_], STAT[:, c0 + 8:c0 + 8 + CU_]
            if floor is None:
                t = ts(DVE, s0, ps.ap[:, 0:CU_], mul, add, ALU.mult, ALU.add, t)
            else:
                t = ts(DVE, s0, ps.ap[:, 0:CU_], floor, None, ALU.max, None, t)
            ps.free = [t]
            t = rpow(s1, s0, CU_, t)
            t = cp(POOL, S.HX[:, :, :], bc(s1, 2, 64), t, S.hx_free)
            yield STAGE
            ps = S.bank()
            PE.wait(t, ps.free)
            for m in range(MP):
                l = S.HX[:, 2 * m:2 * m + 2, :].rearrange("p h c -> p (h c)")
                f = mm(ps.ap[:, 128 * m:128 * m + 128], l, ident, True, True)
                if m < MP - 1:
                    PE.quiet(f)
            S.scale = ps, PE.do(f)
            S.hx_free = [S.scale[1]]

        class Chain:
            units, state, read = 0, None, [None, None]

        chain = Chain()
        S2 = sb([128, 2, 64], F, W0 + 20 * KB + 512)

        def unit(S, j, h, following):
            sl = slice(TU * h, TU * h + TU)
            SG, AI, CU, E1, E2, E3, KK, TM = S.SH
            AR, BK, BON, YT, ZAT = S.AR, S.BK, S.BON, S.YT, S.ZAT
            BHN, KHN, VNN, MTS, GS, QSS, YL, DG, PCT = S.BHN, S.KHN, S.VNN, S.MTS, S.GS, S.QSS, S.YL, S.DG, S.PCT
            ARB, AKT, RKT = S.GM
            ND, NDT, NOT, B4, B6 = S.CH
            B3, B5 = S.NB[:, :, 0, :], S.NB[:, :, 1, :]
            BD, BF = S.BD, S.BF
            ZA_, ZB_ = S.ZZ
            if S.loads is None:
                load_unit(S, j, h)
            t_in, S.loads = S.loads, None
            done = S.done
            for q in (ACTQ, DVE, POOL):
                q.wait(done)
            r_, k_, v_ = (b_[:, 1:TU + 1] for b_ in (S.FR, S.FK, S.FV))
            tk = []
            for p0, dst, bias in ((0, SG, "w0"), (64, AI, "a0")):
                ps = S.bank()
                pv = ps.ap[:, 0:TU]
                t = PE.do(mm(pv, LW[p0:p0 + 64, 128 * j:128 * j + 128], WA[p0:p0 + 64, sl], True, True), ps.free, t_lw, t_wa[h])
                t = act(dst[:, :], pv, ACT.Sigmoid, t, t_vec, bias=vec(bias, j))
                ps.free = [t]
                tk.append(t)
            t_s, t_ai = tk
            t_k1 = shifted(S.FK, TM, vec("mu", 4 + j), t_in[1])
            t_kk = ts(DVE, KK[:, :], k_, vec("k_k", j), None, ALU.mult, None, t_k1)
            t_sq = act(E2[:, :], KK[:, :], ACT.Square, t_kk)
            yield STAGE
            t_cu = DVE.do(lambda e: e.tensor_tensor_scan(CU[:, :], RST[:, 0:TU], SG[:, :], 0.0, ALU.mult, ALU.add), t_s, t_rst)
            t_e1 = act(E1[:, :], CU[:, :], ACT.Exp, t_cu, scale=-CD)
            t_e3 = act(E3[:, :], CU[:, :], ACT.Exp, t_cu, scale=CD)
            t_r1 = shifted(S.FR, TM, vec("mu", j), t_in[0], t_k1)
            yield STAGE
            yield from head_scale(S, E2, t_sq, 256 + 64 * S.n, None, None, 1e-24)
            ps, t_hs = S.scale
            t_v1 = shifted(S.FV, TM, vec("mu", 8 + j), t_in[2], t_r1)
            t_pc = cp(DVE, PCT[:, :], ch3(E1[:, :])[:, :, 63], t_e1)
            t_a1 = tt(POOL, AR[:, 1], ch3(r_), ch3(E1[:, :]), ALU.mult, t_e1, t_r1)
            yield STAGE
            t_tm = tt(DVE, TM[:, :], CU[:, :], SG[:, :], ALU.subtract, t_cu, t_v1)
            t_kn = tt(DVE, KK[:, :], KK[:, :], ps.ap[:, 0:TU], ALU.mult, t_hs, t_sq)
            ps.free = [t_kn]
            t_e2 = act(E2[:, :], TM[:, :], ACT.Exp, t_tm, t_hs, scale=-CD)
            yield STAGE
            t_a0 = stt(AR[:, 0], ch3(KK[:, :]), -1.0, ch3(E2[:, :]), ALU.mult, ALU.mult, t_e2, t_kn)
            t = ts(DVE, TM[:, :], AI[:, :], vec("k_a", j), KA1[:, j:j + 1], ALU.mult, ALU.add, t_ai, t_ka, t_e2)
            t_kf = tt(DVE, k_, k_, TM[:, :], ALU.mult, t, t_kk)
            yield STAGE
            t_b = tt(DVE, TM[:, :], KK[:, :], AI[:, :], ALU.mult, t_kf, t_kn)
            t_b1 = tt(DVE, BK[:, :, 1, :], ch3(k_), ch3(E3[:, :]), ALU.mult, t_kf, t_e3)
            t_b0 = tt(DVE, BK[:, :, 0, :], ch3(TM[:, :]), ch3(E3[:, :]), ALU.mult, t_b, t_e3)
            t_dg = tt(POOL, DG[:, :, :], mask(C_I64, CU_), bc(PCT[:, :], 2, 64), ALU.mult, t_pc)
            yield STAGE
            t_bo = stt(TM[:, :], r_, vec("r_k", j), k_, ALU.mult, ALU.mult, t_b0, t_r1, t_kf)
            t_bh = tt(DVE, ch3(CU[:, :]), BK[:, :, 0, :], bc(PCT[:, :], 2, 64), ALU.mult, t_b0, t_pc, t_e1, t_e3, t_tm)
            t_kh = tt(DVE, ch3(SG[:, :]), BK[:, :, 1, :], bc(PCT[:, :], 2, 64), ALU.mult, t_b1, t_tm)
            t_nat = dict(a=[], b=[], k=[], v=[])

            def turned(name, src, t_src):
                ps = S.bank()
                PE.wait(ps.free, t_src)
                for m in range(MP):
                    s = AR[:, 0, 2 * m:2 * m + 2, :].rearrange("p c t -> p (c t)") if name == "a" else src[:, 128 * m:128 * m + 128]
                    f = (lambda o, s_: lambda e: e.transpose(o, s_, ident))(ps.ap[:, 128 * m:128 * m + 128], s)
                    if m < MP - 1:
                        PE.quiet(f)
                t = PE.do(f)
                pv = ps.ap[:, 0:TU].rearrange("p (m c) -> p m c", c=128)
                if name == "a":
                    for e in range(2):
                        t_nat["a"].append(act(ZA_[:, MP * e:MP * e + MP, 0:64], pv[:, :, 64 * e:64 * e + 64], ACT.Copy, t))
                else:
                    t_nat[name].append(act({"b": BHN, "k": KHN, "v": VNN}[name][:, :, :], pv, ACT.Copy, t))
                ps.free = t_nat[name][-1:]

            turned("a", None, t_a0)
            turned("v", v_, t_v1)
            yield NAT
            turned("b", CU, t_bh)
            turned("k", SG, t_kh)
            yield NAT
            ps = S.bank()
            t = PE.do(mm(ps.ap[:, 0:TU], cst(C_BLK, 128), TM[:, :], True, True), t_bo, ps.free)
            t_p = tt(DVE, BON[:, :], v_, ps.ap[:, 0:TU], ALU.mult, t, t_v1)
            ps.free = [t_p]
            t_ar, t_bk = [t_a0, t_a1], [t_b0, t_b1]
            stage1 = [t_p, t_dg, t_pc, t_nat["a"], t_nat["b"], t_nat["k"], t_nat["v"]]
            S.f_free = stage1 + [t_kf]
            if following:
                load_unit(S, *following)
            yield NAT

            def grams(n, left, right):
                ps = [S.bank(), S.bank()]
                PE.wait(ps[0].free, ps[1].free, t_ar, t_bk)
                for m in range(MP):
                    for e, q in ((0, 0), (1, 1), (0, 1), (1, 0)):
                        pr = slice(64 * e, 64 * e + 64)
                        f = mm(ps[e].ap[64 * q:64 * q + 64, n * m:n * m + n], left(pr, 2 * m + q), right(pr, 2 * m + q), True, True)
                        if m < MP - 1 or (e, q) != (1, 0):
                            PE.quiet(f)
                return ps, PE.do(f)

            tg = {x: [] for x in ("nd", "arb", "akt", "rkt", "ndt", "not")}
            for s, d0, d1, n0, n1, k0 in ((0, ND, ARB, "nd", "arb", C_MD), (1, AKT, RKT, "akt", "rkt", C_MS)):
                pss, t = grams(128, lambda pr, c, s=s: BK[pr, c, s, :], lambda pr, c: AR[pr, :, c, :])
                for e in range(2):
                    gs = slice(MP * e, MP * e + MP)
                    pv = pss[e].ap[:, 0:TU].rearrange("p (m s c) -> p m s c", s=2, c=64)
                    tg[n0].append(tt(DVE, d0[:, gs, :], pv[:, :, 0, :], mask(k0, MP), ALU.mult, t, stage1))
                    tg[n1].append(tt(DVE, d1[:, gs, :], pv[:, :, 1, :], mask(C_MI, MP), ALU.mult, t, stage1))
                    pss[e].free = [tg[n1][-1]]
                if s == 0:
                    pss, t = grams(64, lambda pr, c: AR[pr, 0, c, :], lambda pr, c: BK[pr, c, 0, :])
                    for e in range(2):
                        gs = slice(MP * e, MP * e + MP)
                        pv = pss[e].ap[:, 0:64 * MP].rearrange("p (m c) -> p m c", c=64)
                        tg["ndt"].append(tt(DVE, NDT[:, gs, :], pv, mask(C_MDT, MP), ALU.mult, t))
                        tg["not"].append(tt(DVE, NOT[:, gs, :], pv, mask(C_MOT, MP), ALU.mult, t))
                        pss[e].free = [tg["not"][-1]]
                yield INV
            t_d1 = tt(POOL, B5, ND[:, :, :], mask(C_I64, CU_), ALU.add, tg["nd"], stage1)

            def blocks(lhs, rhs, *tokens, n=64):
                ps = S.bank()
                PE.wait(ps.free, *tokens)
                for x in range(CU_):
                    for q in range(2):
                        pq = slice(64 * q, 64 * q + 64)
                        f = mm(ps.ap[pq, n * x:n * x + n], lhs(pq, x), rhs(pq, x), True, True)
                        if not (q and x == CU_ - 1):
                            PE.quiet(f)
                return ps, ps.ap[:, 0:n * CU_].rearrange("p (x c) -> p x c", x=CU_), PE.do(f)

            def whole(buf):
                return lambda pq, x: buf[pq, x]

            def take(q, dst, r, add=None, *tokens):
                ps, pv, t = r
                if add is not None:
                    t = tt(DVE, dst, pv, add, ALU.add, t, *tokens)
                elif q is ACTQ:
                    t = act(dst, pv, ACT.Copy, t, *tokens)
                else:
                    t = cp(DVE, dst, pv, t, *tokens)
                ps.free = [t]
                return t

            ACTQ.wait(stage1)
            t_n2 = take(ACTQ, B3, blocks(whole(NDT), whole(ND), tg["nd"], tg["ndt"]))
            t_n2t = take(DVE, B4[:, :, :], blocks(whole(ND), whole(NDT)))
            yield INV
            t_x = take(ACTQ, ZA_[:, :, 64:128], blocks(whole(AKT), lambda pq, x: VNN[pq, x % MP, 64 * (x // MP):64 * (x // MP) + 64],
                                                       tg["akt"], t_nat["v"]))
            yield INV
            r4 = blocks(whole(B4), whole(B3), t_n2, t_n2t)
            r4t = blocks(whole(B3), whole(B4))
            t_n4 = take(ACTQ, ND[:, :, :], r4, None, t_d1, r4t[2])
            t_n4t = take(DVE, NDT[:, :, :], r4t)
            yield INV
            t_d2 = take(DVE, B6[:, :, :], blocks(whole(B4), whole(B5), t_d1), B5)
            yield INV
            t_n8t = take(ACTQ, B3, blocks(whole(ND), whole(NDT), t_n4, t_n4t))
            yield INV
            t_d3 = take(DVE, B5, blocks(whole(NDT), whole(B6), t_d2), B6[:, :, :])
            yield INV
            ps, pv, t = blocks(whole(B3), whole(B5), t_n8t, t_d3)
            t_d4, t_f, t_z = [], [], []
            for q in range(2):
                pq = slice(64 * q, 64 * q + 64)
                t_d4.append(tt(DVE, BD[pq, :, 64 * q:64 * q + 64], pv[pq], B5[pq], ALU.add, t, S.t_zero))
            ps.free = t_d4
            yield INV

            def full(lhs, rhs, *tokens):
                ps = S.bank()
                PE.wait(ps.free, *tokens)
                for x in range(CU_):
                    f = mm(ps.ap[:, 128 * x:128 * x + 128], lhs[:, x, :], rhs[:, x, :], True, True)
                    if x < CU_ - 1:
                        PE.quiet(f)
                return ps, ps.ap[:, 0:128 * CU_].rearrange("p (x c) -> p x c", x=CU_), PE.do(f)

            ps, pv, t = blocks(whole(NOT), lambda pq, x: BD[pq, x, pq], t_d4, tg["not"])
            for q in range(2):
                pq = slice(64 * q, 64 * q + 64)
                t_f.append(act(BF[pq, :, 64 * q:64 * q + 64], pv[pq], ACT.Copy, t, S.t_zero))
            ps.free = t_f
            t_z = take(DVE, ZB_[:, :, :], full(BD, ZA_, t_x, t_nat["a"]))
            yield INV
            for it in range(3):
                t_z = take(DVE, ZA_[:, :, :], full(BF, ZB_ if it == 0 else ZA_, t_f, t_z), ZB_[:, :, :])
                yield INV

            W_ = lambda e, pq, m: ZA_[pq, MP * e + m, 0:64]
            U_ = lambda e, pq, m: ZA_[pq, MP * e + m, 64:128]
            H_ = lambda buf: (lambda e, pq, m: buf[pq, m, 64 * e:64 * e + 64])
            G_ = lambda buf: (lambda e, pq, m: buf[pq, MP * e + m, :])
            plans = [("mt", [(W_, H_(BHN))]), ("g", [(H_(BHN), U_), (H_(KHN), H_(VNN))]), ("q", [(W_, G_(ARB))]),
                     ("y", [(U_, G_(ARB)), (H_(VNN), G_(RKT))])]
            t_out = {}
            for name, terms in plans:
                t_out[name] = []
                ps = [S.bank(), S.bank()]
                PE.wait(ps[0].free, ps[1].free, t_z, t_nat["b"], t_nat["k"], tg["arb"], tg["rkt"])
                for m in range(MP):
                    for pairs in (((0, 0), (1, 1)), ((0, 1), (1, 0))):
                        for x, (l, r) in enumerate(terms):
                            for e, q in pairs:
                                pq = slice(64 * q, 64 * q + 64)
                                f = mm(ps[q].ap[64 * e:64 * e + 64, 64 * m:64 * m + 64], l(e, pq, m), r(e, pq, m),
                                       x == 0, x == len(terms) - 1)
                                if not (m == MP - 1 and (e, q) == (1, 0) and x == len(terms) - 1):
                                    PE.quiet(f)
                t = PE.do(f)
                for q in range(2):
                    pv = ps[q].ap[:, 0:64 * MP].rearrange("p (m c) -> p m c", c=64)
                    view = lambda b_: b_[:, :, :].rearrange("p (m q) c -> p m q c", q=2)[:, :, q, :]
                    if name == "mt":
                        t2 = tt(DVE, view(MTS), pv, view(DG), ALU.add, t, t_dg)
                    elif name == "q":
                        t2 = tt(DVE, view(QSS), pv, AR[:, 1].rearrange("p (m q) c -> p m q c", q=2)[:, :, q, :], ALU.add, t, t_a1)
                    else:
                        t2 = act(view(GS if name == "g" else YL), pv, ACT.Copy, t)
                    ps[q].free = [t2]
                    t_out[name].append(t2)
                yield INV

            need(t_zg, j)
            t_za = SP.dma(ZAT[:, :], zg_d[j][:, sl], land(f"za{S.n}"), t_zg[j], done)
            t_za = act(ZAT[:, :], ZAT[:, :], ACT.Silu, t_za)
            index = j * (T // TU) + h
            while chain.units < index:
                yield 0
            if h == 0:
                chain.state = POOL.do(lambda e: e.memset(S2[:, 0, :], 0.0), chain.state, chain.read)
            yb = S.banks[2]
            PE.wait(yb.free)
            for c in range(CU_):
                cur, nxt = c % 2, (c + 1) % 2
                final = h == T // TU - 1 and c == CU_ - 1
                PE.wait(chain.state, t_out["q"], t_out["mt"])
                if not final:
                    sp = S.banks[c % 2]
                    PE.wait(sp.free)
                    PE.quiet(mm(sp.ap[0:64, 0:64], MTS[0:64, c, :], S2[0:64, cur, :], True, True))
                    t_sp_ = PE.do(mm(sp.ap[64:128, 0:64], MTS[64:128, c, :], S2[64:128, cur, :], True, True))
                    chain.state = tt(DVE, S2[:, nxt, :], sp.ap[:, 0:64], GS[:, c, :], ALU.add, t_sp_, t_out["g"], chain.read[nxt])
                    sp.free = [chain.state]
                PE.quiet(mm(yb.ap[0:64, 64 * c:64 * c + 64], S2[0:64, cur, :], QSS[0:64, c, :], True, True))
                chain.read[cur] = t_y = PE.do(mm(yb.ap[64:128, 64 * c:64 * c + 64], S2[64:128, cur, :], QSS[64:128, c, :], True, True))
                if c == CU_ - 1:
                    chain.units += 1
                yield CHAIN
            t = tt(DVE, YT[:, :], yb.ap[:, 0:TU], YL[:, :, :].rearrange("p c t -> p (c t)"), ALU.add, t_y, t_out["y"], S.y_free)
            yb.free = [t]
            ps = S.bank()
            t = PE.do(mm(ps.ap[:, 0:TU], cst(C_BLKM, 128), YT[:, :], True, True), t, ps.free)
            t_yc = tt(DVE, YT[:, :], YT[:, :], ps.ap[:, 0:TU], ALU.subtract, t)
            ps.free = [t_yc]
            yield NORM
            t_sq = act(E1[:, :], YT[:, :], ACT.Square, t_yc, t_z)
            yield from head_scale(S, E1, t_sq, 288 + 64 * S.n, 1.0 / 64, 64e-5, None)
            ps, t_hs = S.scale
            t = tt(DVE, YT[:, :], YT[:, :], ps.ap[:, 0:TU], ALU.mult, t_hs, t_sq)
            ps.free = [t]
            t = ts(DVE, YT[:, :], YT[:, :], vec("gn_gain", j), vec("gn_bias", j), ALU.mult, ALU.add, t)
            t = tt(DVE, YT[:, :], YT[:, :], BON[:, :], ALU.add, t, t_p)
            yield NORM
            t = tt(DVE, YT[:, :], YT[:, :], ZAT[:, :], ALU.mult, t, t_za)
            t_o = SP.dma(y_d[j][:, sl], YT[:, :], land(f"y{S.n}"), t)
            t_yd.append(t_o)
            S.done = [t, t_out["q"], t_out["mt"], t_out["g"], t_out["y"], t_y]
            S.y_free = [t_o]
            yield NORM

        t_yd = []
        order = [(j, h) for j in range(4) for h in range(T // TU)]

        def flow(n):
            mine = order[n::2]
            S = slots[n]
            S.hx_free, S.y_free = [], []
            for x, (j, h) in enumerate(mine):
                yield from unit(S, j, h, mine[x + 1] if x + 1 < len(mine) else None)

        flows = [flow(0), flow(1)]
        for _ in range(OFFSET):
            fill(next(flows[0]))
        while flows:
            for f in list(flows):
                us = next(f, None)
                if us is None:
                    flows.remove(f)
                else:
                    fill(us)
        OB = sb([128, 8, 512], F, W0)
        CN = sb([128, 8, 416], F, W0 + 16 * KB)
        RT = sb([128, 2, 8, 2, 16], F, W0 + 29 * KB)
        CTH = sb([128, 3, T], R, W0 + 31 * KB)
        CTL = sb([128, 3, T], R, W0 + 43 * KB)
        VN = sb([128, 8, 512], F, W0 + 55 * KB)
        QN = [sb([128, 768], F, W0 + (71 + 3 * i) * KB) for i in range(2)]
        PM = [sb([128, T], F, W0 + (77 + 4 * i) * KB) for i in range(2)]
        PTM = [sb([128, T], F, W0 + (85 + 4 * i) * KB) for i in range(2)]
        TAB = [sb([128, 8, 16], F, W0 + 77 * KB + 512 * i) for i in range(5)]
        JK3 = sb([128, 256], F, W0 + 85 * KB)
        QTM = sb([96, 8, T], F, RA)
        KTM = sb([96, 8, T], F, RA + 32 * KB)
        YBH = sb([128, 4, T], R, W0 + 16 * KB)
        YBL = sb([128, 4, T], R, W0 + 32 * KB)
        ZT = sb([128, T], F, W0 + 48 * KB)
        enter_phase()
        SP.wait(t_yd)
        high = range(6)
        t_cl = SP.dma(CN[:, :, :], cn_d.rearrange("(i p) c -> p i c", p=128), land("cn"), t_cnd)
        t_c = [[t_cl, t_cl] for _ in range(NT)]

        ang, sinT, cosT, yy, nn = (TAB[i][:, :, :] for i in range(5))
        MAGIC = 12582912.0
        two_pi = 2.0 * np.pi
        c1 = 6.28125
        c2 = float((np.float32(two_pi - c1).view(np.uint32) & np.uint32(0xFFFFF000)).view(np.float32))
        c3 = float(two_pi - c1 - c2)
        t_a = tt(DVE, ang, bc(VT[:, 0:8], 2, 16), bc(cst(C_INV, 16), 1, 8), ALU.mult, t_vec)
        t_tab = []
        for dst, turn_, add in ((sinT, 0.0, 0.0), (cosT, 0.25, float(np.pi / 2))):
            fill(3)
            t = ts(DVE, yy, ang, 1.0 / two_pi, turn_, ALU.mult, ALU.add, t_a, t_tab)
            t = ts(DVE, nn, yy, MAGIC, None, ALU.add, None, t)
            t = ts(DVE, yy, nn, -MAGIC, None, ALU.add, None, t)
            f2 = lambda ap: ap.rearrange("p i c -> p (i c)")
            t = stt(f2(dst), f2(yy), -c1, f2(ang), ALU.mult, ALU.add, t)
            t = stt(f2(dst), f2(yy), -c2, f2(dst), ALU.mult, ALU.add, t)
            t = stt(f2(dst), f2(yy), -c3, f2(dst), ALU.mult, ALU.add, t)
            t = ts(DVE, dst, dst, add, None, ALU.add, None, t)
            t = ts(DVE, dst, dst, 3.1415925, -3.1415925, ALU.min, ALU.max, t)
            t_tab = [act(dst, dst, ACT.Sin, t)] + t_tab
        t_st = []
        for i in range(NT):
            fill(0.9)
            t_st.append(act(JK3[:, :], CN[:, i, 0:256], ACT.Square, t_c[i], ACTQ.last(), accum_out=STAT[:, 64 + 2 * i:65 + 2 * i]))
            t_st.append(act(JK3[:, 0:128], CN[:, i, 256:384], ACT.Square, ACTQ.last(), accum_out=STAT[:, 65 + 2 * i:66 + 2 * i]))
        s_in = STAT[:, 64:80].rearrange("p (i s) -> p s i", s=2)
        s_ms = STAT[:, 80:96].rearrange("p (i s) -> p s i", s=2)
        t_m = [ts(DVE, s_ms[:, s, :], s_in[:, s, :], 1.0 / n, 1e-6, ALU.mult, ALU.add, t_st) for s, n in ((0, 256), (1, 128))]
        t_r = rpow(STAT[:, 96:112], STAT[:, 80:96], 16, t_m)
        t_cn = []
        for i in range(NT):
            fill(0.9)
            t1 = ts(DVE, CN[:, i, 0:256], CN[:, i, 0:256], STAT[:, 96 + 2 * i:97 + 2 * i], None, ALU.mult, None, t_r)
            t2 = ts(DVE, CN[:, i, 256:384], CN[:, i, 256:384], STAT[:, 97 + 2 * i:98 + 2 * i], None, ALU.mult, None, t_r)
            t_cn.append([t1, t2])

        kp = CN[:, :, 384:416].rearrange("p i (f c) -> p i f c", f=2)
        RA_, RB_ = RT[:, 0], RT[:, 1]

        def rotate(x4, cos, sin, *tokens):
            t1 = tt(DVE, RA_, x4, bc(cos, 2, 2), ALU.mult, DVE.last(), *tokens)
            t2 = tt(DVE, RB_[:, :, 0, :], x4[:, :, 1, :], sin, ALU.mult, DVE.last(), *tokens)
            t3 = tt(DVE, RB_[:, :, 1, :], x4[:, :, 0, :], sin, ALU.mult, DVE.last(), *tokens)
            t4 = tt(DVE, x4[:, :, 0, :], RA_[:, :, 0, :], RB_[:, :, 0, :], ALU.subtract, t1, t2, t3)
            return tt(DVE, x4[:, :, 1, :], RA_[:, :, 1, :], RB_[:, :, 1, :], ALU.add, t4)

        t_kp = rotate(kp, cosT, sinT, t_tab, *[t_c[i][1] for i in range(NT)])

        t_ct = [[], []]
        for k in range(3):
            gain = vec("g_q", k) if k < 2 else vec("g_kv")
            for g in range(2):
                fill(1.3)
                ps = bank(high)
                PE.wait(ps.free, t_cn[4 * g:4 * g + 4])
                for i in range(4):
                    f = (lambda o, s: lambda e: e.transpose(o, s, ident))(
                        ps.ap[:, 128 * i:128 * i + 128], CN[:, 4 * g + i, 128 * k:128 * k + 128])
                    if i < 3:
                        PE.quiet(f)
                t = PE.do(f)
                sl = slice(512 * g, 512 * g + 512)
                t_h = act(CTH[:, k, sl], ps.ap, ACT.Identity, t, t_vec, scale=gain)
                t_l = stt(CTL[:, k, sl], ps.ap, gain, CTH[:, k, sl].bitcast(F), ALU.mult, ALU.subtract, t_h)
                ps.free = [t_h, t_l]
                t_ct[g] += [t_h, t_l]
        for _ in filler:
            pass
        enter_phase()
        t_k, t_v = [], []
        with Block() as b:
            kh_, kl_, vh_, vl_ = (x[:, 0, o:o + 512] for o in (0, 512) for x in (b.hi, b.lo))
            for i in range(NT):
                sl = slice(128 * i, 128 * i + 128)
                ps = bank(range(8))
                t = product(ps.ap, [(CTH[:, 2, sl], CTL[:, 2, sl])], [(vh_, vl_)],
                            b.tok, ps.free, t_ct[i // 4])
                t = act(VN[:, i, :], ps.ap, ACT.Copy, t)
                ps.free = [t]
                t_v.append(t)
            for j in range(4):
                for half in range(2):
                    sl = slice(512 * half, 512 * half + 512)
                    ps = bank(range(8))
                    t = product(ps.ap, [(kh_[:, 128 * j:128 * j + 128], kl_[:, 128 * j:128 * j + 128])],
                                [(CTH[:, 2, sl], CTL[:, 2, sl])], b.tok, ps.free, t_ct[half])
                    t1 = cp(DVE, KTM[0:64, 2 * j, sl], ps.ap[0:64, :], t)
                    t2 = act(KTM[0:64, 2 * j + 1, sl], ps.ap[64:128, :], ACT.Copy, t, t1)
                    ps.free = [t1, t2]
                    t_k += [t1, t2]
        t_kr = []
        for half in range(2):
            sl = slice(512 * half, 512 * half + 512)
            ps = bank(range(8))
            PE.wait(ps.free, t_kp)
            for i in range(4):
                f = (lambda o, s: lambda e: e.transpose(o, s, ident))(
                    ps.ap[0:32, 128 * i:128 * i + 128], CN[:, 4 * half + i, 384:416])
                if i < 3:
                    PE.quiet(f)
            t = PE.do(f)
            t_kr.append(cp(DVE, KTM[64:96, 0, sl], ps.ap[0:32, :], t))
            ps.free = [t_kr[half]]
        t_rk = [t_kr] + [[cp(POOL, KTM[64:96, h, :], KTM[64:96, 0, :], t_kr)] for h in range(1, 8)]

        t_q = [[] for _ in range(NT)]
        qfree = [[], []]
        def turn_queries(i, t_rot):
            z = i % 2
            sl = slice(128 * i, 128 * i + 128)
            for g in range(2):
                ps = bank(range(8))
                PE.wait(ps.free, t_rot)
                for h in range(4):
                    f = (lambda o, s: lambda e: e.transpose(o, s, ident))(
                        ps.ap[0:96, 128 * h:128 * h + 128], QN[z][:, 96 * (4 * g + h):96 * (4 * g + h) + 96])
                    if h < 3:
                        PE.quiet(f)
                t = PE.do(f)
                o = QTM[:, 4 * g:4 * g + 4, sl]
                pv = ps.ap[0:96, :].rearrange("p (h c) -> p h c", c=128)
                t = act(o, pv, ACT.Copy, t) if g else cp(DVE, o, pv, t)
                ps.free = [t]
                t_q[i].append(t)
            qfree[z] = [PE.last()]

        t_rot = [None] * NT
        with Block() as b:
            for i in range(NT):
                z = i % 2
                sl = slice(128 * i, 128 * i + 128)
                t_e = []
                for g in range(2):
                    ps = bank(range(8))
                    t = product(ps.ap[:, 0:384], [(CTH[:, k, sl], CTL[:, k, sl]) for k in range(2)],
                                [(b.hi[:, k, 384 * g:384 * g + 384], b.lo[:, k, 384 * g:384 * g + 384]) for k in range(2)],
                                b.tok, ps.free, t_ct[i // 4])
                    t = act(QN[z][:, 384 * g:384 * g + 384], ps.ap[:, 0:384], ACT.Copy, t, qfree[z], scale=96.0 ** -0.5)
                    ps.free = [t]
                    t_e.append(t)
                pe4 = QN[z][:, :].rearrange("p (h c) -> p h c", c=96)[:, :, 64:96].rearrange("p h (f c) -> p h f c", f=2)
                t_rot[i] = rotate(pe4, bc(cosT[:, i, :], 1, 8), bc(sinT[:, i, :], 1, 8), t_tab, t_e)
                if i:
                    turn_queries(i - 1, t_rot[i - 1])
            turn_queries(NT - 1, t_rot[NT - 1])
        for q in (ACTQ, DVE):
            q.wait([x.free for x in stage])
        enter_phase()
        t_yb, t_z = [], {}

        def load_gate(k):
            t_z[k] = SP.dma(ZT[:, :], zb_d[k], land("zt"), t_zbd[k], t_yb)

        def gate_gate(k):
            t_z[k] = act(ZT[:, :], ZT[:, :], ACT.Silu, t_z[k])

        def gate_heads(k):
            t_done = DVE.last()
            for half in range(2):
                sl = slice(512 * half, 512 * half + 512)
                ps = banks[6 + half]
                PE.wait(ps.free, t_done)
                for i in range(4):
                    f = (lambda o, x: lambda e: e.transpose(o, x, ident))(
                        ps.ap[:, 128 * i:128 * i + 128], OB[:, 4 * half + i, 128 * k:128 * k + 128])
                    if i < 3:
                        PE.quiet(f)
                t = PE.do(f)
                t = tt(DVE, ZT[:, sl], ZT[:, sl], ps.ap, ALU.mult, t, t_z[k])
                ps.free = [t]
                t_h = act(YBH[:, k, sl], ZT[:, sl], ACT.Copy, t)
                t_l = tt(POOL, YBL[:, k, sl], ZT[:, sl], YBH[:, k, sl].bitcast(F), ALU.subtract, t_h)
                t_yb.extend([t_h, t_l])

        def during(n):
            k, m = n // 16, n % 16
            if m == 4 and k < 4:
                load_gate(k)
            elif m == 12 and k < 4:
                gate_gate(k)
            elif m == 1 and k >= 1:
                gate_heads(k - 1)

        items = []
        for h in range(8):
            for i in (7, 0, 6, 1, 5, 2, 4, 3):
                w = 128 * (i + 1)

                def scores(ps, free, h=h, i=i, w=w):
                    PE.wait(free, t_q[i], t_k, t_rk[h])
                    for s in range(0, w, 512):
                        n = min(512, w - s)
                        f = mm(ps[:, s:s + n], QTM[:, h, 128 * i:128 * i + 128], KTM[:, h, s:s + n], True, True)
                        if s + 512 < w:
                            PE.quiet(f)
                    return PE.do(f)

                def stat(ps, p, nmx, t_s, free, w=w):
                    d = ps[:, w - 128:w]
                    t_a = tt(DVE, d, d, cst(C_CAUS, 128), ALU.add, t_s)
                    return max_stat(ps, p, nmx, t_a, free, w)

                items.append(dict(nk=[128] * (i + 1), scores=scores, stat=stat,
                                  v=lambda k, h=h: VN[:, k, 64 * h:64 * h + 64], t_v=t_v,
                                  out=OB[:, i, 64 * h:64 * h + 64], t_g=None))
        attention(items, PM, PTM, during)

        YAH = sb([128, 4, T], R, W0 + 48 * KB)
        YAL = sb([128, 4, T], R, W0 + 64 * KB)
        GA = [sb([128, T], F, W0 + (80 + 4 * i) * KB) for i in range(2)]
        MG = sb([128, 4, T], F, W0)
        M2 = [sb([128, 512], F, W0 + (88 + 2 * i) * KB) for i in range(2)]
        OT = sb([128, 8, D], F, W0 + 16 * KB)
        X2 = sb([128, 8, D], F, W0 + 48 * KB)
        GP = sb([128, D], F, W0)
        JK4 = sb([128, D], F, W0 + 8 * KB)
        SP.wait(t_yb[-4:])
        enter_phase()
        gfree, t_gl = [[], []], {}
        gate_tiles = [8 * br + 2 * n + c for br, n in MERGES for c in range(2)]

        def load_output_gate(u):
            if u < len(gate_tiles):
                t_gl[u] = SP.dma(GA[u % 2][:, :], zg_d[4 + gate_tiles[u]], land(f"ga{u % 2}"), gfree[u % 2], t_zg[4 + gate_tiles[u]])

        load_output_gate(0)
        load_output_gate(1)
        t_yl = [SP.dma(YAL[:, j, :].bitcast(F), y_d[j], land(f"ya{j}")) for j in range(4)]
        t_ya = []
        mfree = [[], []]
        t_mer, t_m1 = [], {}
        for x, (br, n) in enumerate(MERGES):
            H, L, t_in = ((YAH, YAL, t_ya), (YBH, YBL, t_yb))[br]
            with Block() as b:
                for c in range(2):
                    u = 2 * x + c
                    z = u % 2
                    ct = 2 * n + c
                    g = 2 * (n % 2) + c
                    t_g = act(GA[z][:, :], GA[z][:, :], ACT.Sigmoid, t_gl[u], t_vec, bias=vec("b_gate", 8 * br + ct))
                    if x < 2:
                        j = 2 * x + c
                        t_h = act(YAH[:, j, :], YAL[:, j, :].bitcast(F), ACT.Copy, t_yl[j])
                        t_l = tt(DVE, YAL[:, j, :], YAL[:, j, :].bitcast(F), YAH[:, j, :].bitcast(F), ALU.subtract, t_h)
                        t_ya += [t_h, t_l]
                    for half in range(2):
                        sl = slice(512 * half, 512 * half + 512)
                        ps = bank(range(8))
                        t = gemm_tr(b, 128 * c, 128 * c + 128, half, ps.ap, H, L, 4, ps.free, t_in)
                        if br == 1:
                            t = tt(DVE, MG[:, g, sl], ps.ap, GA[z][:, sl], ALU.mult, t, t_g, t_mer[-8:])
                            ps.free = [t]
                            t_m1[ct, half] = t
                        else:
                            t1 = tt(DVE, M2[half][:, :], ps.ap, GA[z][:, sl], ALU.mult, t, t_g, mfree[half])
                            ps.free = [t1]
                            t = tt(DVE, M2[half][:, :], M2[half][:, :], MG[:, g, sl], ALU.add, t1, t_m1[ct, half])
                            t_h = act(AH[:, ct, sl], M2[half][:, :], ACT.Copy, t)
                            t_l = tt(DVE, AL[:, ct, sl], M2[half][:, :], AH[:, ct, sl].bitcast(F), ALU.subtract, t_h)
                            mfree[half] = [t_h, t_l]
                            t_mer += [t_h, t_l]
                    gfree[z] = [DVE.last()]
                    load_output_gate(u + 2)
        for q in (SP, ACTQ, DVE):
            q.wait(everyone())
        t_gp = SP.dma(GP[:, :], a["g_post_2"].partition_broadcast(128), land("gp"))
        t_x2 = [SP.dma(X2[:, i, :], x2_d[128 * i:128 * i + 128, :], land(f"x{i}"), t_sp[i]) for i in range(NT)]
        t_ot = [[] for _ in range(NT)]
        t_out = []
        for n in range(4):
            with Block() as b:
                for i in range(NT):
                    ps = bank(range(8))
                    t = gemm_nat(b, i, ps.ap[:, 0:256], AH, AL, 8, 0, 256, ps.free, t_mer)
                    t = act(OT[:, i, 256 * n:256 * n + 256], ps.ap[:, 0:256], ACT.Copy, t)
                    ps.free = [t]
                    t_ot[i].append(t)
                    if n == 3:
                        t = norm_tile(i, OT[:, i, :], OT[:, i, :], JK4[:, :], GP[:, :], 24, t_ot[i], t_gp)
                        t = tt(DVE, OT[:, i, :], OT[:, i, :], X2[:, i, :], ALU.add, t, t_x2[i])
                        t_out.append(SP.dma(out[0, 128 * i:128 * i + 128, :], OT[:, i, :], land(f"o{i}"), t))
        SP.wait(t_out)

        block = ctx.enter_context(nc.Block())

        @block.sync
        def _(e):
            SP.emit(e)

        @block.gpsimd
        def _(e):
            POOL.emit(e)

        @block.vector
        def _(e):
            DVE.emit(e)

        @block.scalar
        def _(e):
            ACTQ.emit(e)

        @block.tensor
        def _(e):
            PE.emit(e)


_INS = ["x", "norm_gain", "w_in", "q_norm_a", "k_norm_a", "na_rpb", "w_out", "final_norm_gain", "positions_2", "g_pre_2",
        "w_in_2", "b_gate_2", "mu_shift_2", "w0_2", "w_decay_up_2", "a0_2", "w_iclr_up_2", "k_k_2", "k_a_2", "r_k_2",
        "gn_gain_2", "gn_bias_2", "w_out_a_2", "g_q_2", "w_uq_2", "g_kv_2", "w_ukv_2", "w_out_b_2", "w_o_2", "g_post_2"]


def kernel(**inputs):
    import numpy as _np
    import concourse.bacc as _bacc
    from concourse import mybir as _mybir
    from concourse.bass_utils import run_bass_kernel_spmd as _run

    nc = _bacc.Bacc("TRN2", target_bir_lowering=False, num_devices=1)
    arrays, args = {}, {}
    for name in _INS:
        arrays[f"in_{name}"] = _np.ascontiguousarray(inputs[name])
    arrays["in_consts"] = constants()
    for name, v in arrays.items():
        args[name[3:]] = nc.dram_tensor(name, v.shape, _mybir.dt.from_np(v.dtype), kind="ExternalInput").ap()
    out = nc.dram_tensor("out_0", (1, T, D), F, kind="ExternalOutput").ap()
    build(nc, args, out)
    r = _run(nc, [arrays], core_ids=[0])
    return r.results[0]["out_0"]
```
